# Optimizing a Trainium2 kernel written in Bass

```python
import jax
import jax.numpy as jnp
from jax import lax
import numpy as np
import math
import jax, jax.numpy as jnp

D_MODEL = 1024
BATCH = 1
SEQ = 512
DEPTH = 2

CTX_LEN = 256
GRID_W = 64
N_MIXERS = 4
MLP_HIDDEN = 4 * D_MODEL
N_MOD = 6
NORM_EPS = 1e-6
NEG_INF = -1e30

ATTN_HEADS = 16
ATTN_KV_HEADS = 4
ATTN_GROUP = ATTN_HEADS // ATTN_KV_HEADS
HEAD_DIM = D_MODEL // ATTN_HEADS
WINDOW = 128
ATTN_BLOCK = 128
ROPE_BASE = 10000.0
ROPE_AXIS_DIM = HEAD_DIM // 2
ROPE_FREQS = ROPE_AXIS_DIM // 2

GLA_HEADS = 4
GLA_KEY_DIM = D_MODEL // 2
GLA_VAL_DIM = D_MODEL
GLA_DK = GLA_KEY_DIM // GLA_HEADS
GLA_DV = GLA_VAL_DIM // GLA_HEADS
GLA_GATE_RANK = 16
GLA_TAU = 16.0
SCAN_CHUNK = 64

RWKV_HEAD_SIZE = 64
RWKV_HEADS = D_MODEL // RWKV_HEAD_SIZE
RWKV_DECAY_RANK = 64
RWKV_AAA_RANK = 64
RWKV_GATE_RANK = 128
RWKV_LN_EPS = 64e-5
L2_EPS = 1e-12

HGRN_EXPAND = 128
HGRN_HEADS = D_MODEL // HGRN_EXPAND
HGRN_FORGET_DIM = HGRN_HEADS * HGRN_EXPAND
HGRN_IN_DIM = D_MODEL // HGRN_HEADS

N_ATTN_LAYERS = (DEPTH + 3) // N_MIXERS
N_GLA_LAYERS = (DEPTH + 2) // N_MIXERS
N_RWKV_LAYERS = (DEPTH + 1) // N_MIXERS
N_HGRN_LAYERS = DEPTH // N_MIXERS


def rms_norm(x, gain):
    xf = x.astype(jnp.float32)
    y = xf * lax.rsqrt(jnp.mean(xf * xf, axis=-1, keepdims=True) + NORM_EPS)
    return (y * gain.astype(jnp.float32)).astype(x.dtype)

def modulate(x, gain, shift, scale):
    return rms_norm(x, gain) * (1 + scale) + shift

def channel_mlp(h, w_in, w_out):
    return jnp.square(jax.nn.relu(h @ w_in)) @ w_out

def axial_rope_tables(rows):
    inv_freq = ROPE_BASE ** (-jnp.arange(ROPE_FREQS, dtype=jnp.float32) * 2.0 / ROPE_AXIS_DIM)
    pos = jnp.arange(rows * GRID_W)
    row = (pos // GRID_W).astype(jnp.float32)
    col = (pos % GRID_W).astype(jnp.float32)
    ang = jnp.stack([row[:, None] * inv_freq, col[:, None] * inv_freq], axis=1)
    return jnp.cos(ang), jnp.sin(ang)

def apply_axial_rope(x, cos, sin):
    lead = x.shape[:-1]
    xr = x.reshape(lead + (2, 2, ROPE_FREQS))
    x1, x2 = xr[..., 0, :], xr[..., 1, :]
    bshape = (1, x.shape[1]) + (1,) * (x.ndim - 3) + cos.shape[1:]
    cb = cos.reshape(bshape).astype(x.dtype)
    sb = sin.reshape(bshape).astype(x.dtype)
    out = jnp.stack([x1 * cb - x2 * sb, x2 * cb + x1 * sb], axis=-2)
    return out.reshape(x.shape)

def softmax_with_sink(s, sink):
    sk = sink.astype(jnp.float32)[None, :, :, None, None]
    m = jnp.maximum(jnp.max(s, axis=-1, keepdims=True), sk)
    e = jnp.exp(s - m)
    return e / (jnp.sum(e, axis=-1, keepdims=True) + jnp.exp(sk - m))

def windowed_gqa_sink(h_lat, h_ctx, w_qkv, w_o, sink, cos, sin, need_ctx):
    B, L, _ = h_lat.shape
    nb = L // ATTN_BLOCK
    q_cols = ATTN_HEADS * HEAD_DIM
    kv_cols = ATTN_KV_HEADS * HEAD_DIM

    def project(h):
        T = h.shape[1]
        qkv = h @ w_qkv
        q = qkv[..., :q_cols].reshape(B, T, ATTN_KV_HEADS, ATTN_GROUP, HEAD_DIM) * (HEAD_DIM ** -0.5)
        k = qkv[..., q_cols:q_cols + kv_cols].reshape(B, T, ATTN_KV_HEADS, HEAD_DIM)
        v = qkv[..., q_cols + kv_cols:].reshape(B, T, ATTN_KV_HEADS, HEAD_DIM)
        return q, k, v

    q_lat, k_lat, v_lat = project(h_lat)
    q_ctx, k_ctx, v_ctx = project(h_ctx)
    q_lat = apply_axial_rope(q_lat, cos, sin)
    k_lat = apply_axial_rope(k_lat, cos, sin)
    sink_g = sink.reshape(ATTN_KV_HEADS, ATTN_GROUP)

    def band(t):
        tp = jnp.pad(t, ((0, 0), (ATTN_BLOCK, ATTN_BLOCK), (0, 0), (0, 0)))
        tp = tp.reshape(B, nb + 2, ATTN_BLOCK, ATTN_KV_HEADS, HEAD_DIM)
        return jnp.moveaxis(jnp.concatenate([tp[:, :-2], tp[:, 1:-1], tp[:, 2:]], axis=2), 1, 0)

    k_band, v_band = band(k_lat), band(v_lat)
    q_blocks = jnp.moveaxis(q_lat.reshape(B, nb, ATTN_BLOCK, ATTN_KV_HEADS, ATTN_GROUP, HEAD_DIM), 1, 0)
    n_loc = 3 * ATTN_BLOCK
    rel = jnp.arange(n_loc)[None, :] - ATTN_BLOCK - jnp.arange(ATTN_BLOCK)[:, None]
    in_window = jnp.abs(rel) <= WINDOW

    def attend_block(args):
        q, k, v, blk = args
        key_pos = blk * ATTN_BLOCK - ATTN_BLOCK + jnp.arange(n_loc)
        ok = in_window & ((key_pos >= 0) & (key_pos < L))[None, :]
        s_lat = jnp.einsum('bqhgd,bkhd->bhgqk', q, k).astype(jnp.float32)
        s_lat = jnp.where(ok, s_lat, NEG_INF)
        s_ctx = jnp.einsum('bqhgd,bkhd->bhgqk', q, k_ctx).astype(jnp.float32)
        p = softmax_with_sink(jnp.concatenate([s_lat, s_ctx], axis=-1), sink_g).astype(v.dtype)
        return (jnp.einsum('bhgqk,bkhd->bqhgd', p[..., :n_loc], v)
                + jnp.einsum('bhgqk,bkhd->bqhgd', p[..., n_loc:], v_ctx))

    o_lat = lax.map(attend_block, (q_blocks, k_band, v_band, jnp.arange(nb)))
    o_lat = jnp.moveaxis(o_lat, 0, 1).reshape(B, L, q_cols)
    y_lat = o_lat @ w_o
    if not need_ctx:
        return y_lat, None
    s_c = jnp.einsum('bqhgd,bkhd->bhgqk', q_ctx, k_ctx).astype(jnp.float32)
    p_c = softmax_with_sink(s_c, sink_g).astype(v_ctx.dtype)
    o_ctx = jnp.einsum('bhgqk,bkhd->bqhgd', p_c, v_ctx).reshape(B, h_ctx.shape[1], q_cols)
    return y_lat, o_ctx @ w_o

def reverse_segments(t, n_ctx):
    return jnp.concatenate([t[:, :n_ctx][:, ::-1], t[:, n_ctx:][:, ::-1]], axis=1)

def chunk_gated_scan(q, k, v, log_g):
    B, T, H, dk = q.shape
    dv = v.shape[-1]
    n = T // SCAN_CHUNK

    def chunks(t):
        return jnp.moveaxis(t.astype(jnp.float32).reshape(B, n, SCAN_CHUNK, H, t.shape[-1]), 1, 0)

    lower = jnp.tril(jnp.ones((SCAN_CHUNK, SCAN_CHUNK), dtype=bool))

    def step(S, xs):
        qc, kc, vc, gc = xs
        b = jnp.cumsum(gc, axis=1)
        q_dec = qc * jnp.exp(b)
        k_inv = kc * jnp.exp(-b)
        A = jnp.where(lower, jnp.einsum('bqhd,bkhd->bhqk', q_dec, k_inv), 0.0)
        o = jnp.einsum('bhqk,bkhv->bqhv', A, vc) + jnp.einsum('bqhd,bhdv->bqhv', q_dec, S)
        b_last = b[:, -1]
        k_end = kc * jnp.exp(b_last[:, None] - b)
        S = jnp.exp(b_last)[..., None] * S + jnp.einsum('bkhd,bkhv->bhdv', k_end, vc)
        return S, o

    S0 = jnp.zeros((B, H, dk, dv), jnp.float32)
    _, o = lax.scan(step, S0, (chunks(q), chunks(k), chunks(v), chunks(log_g)))
    return jnp.moveaxis(o, 0, 1).reshape(B, T, H, dv).astype(v.dtype)

def bidir_gated_scan(q, v, k_fwd, g_fwd, k_bwd, g_bwd, n_ctx):
    rev = lambda t: reverse_segments(t, n_ctx)
    o_f = chunk_gated_scan(q, k_fwd, v, g_fwd)
    o_b = chunk_gated_scan(rev(q), rev(k_bwd), rev(v), rev(g_bwd))
    return o_f + rev(o_b)

def gla_mixer(h_lat, h_ctx, w_in, w_gate_down, w_gate_up, gate_bias, g_norm, w_o, need_ctx):
    n_ctx = h_ctx.shape[1]
    h = jnp.concatenate([h_ctx, h_lat], axis=1)
    B, T, _ = h.shape
    z = h @ w_in
    q = z[..., :GLA_KEY_DIM].reshape(B, T, GLA_HEADS, GLA_DK) * (GLA_DK ** -0.5)
    k = z[..., GLA_KEY_DIM:2 * GLA_KEY_DIM].reshape(B, T, GLA_HEADS, GLA_DK)
    v = z[..., 2 * GLA_KEY_DIM:2 * GLA_KEY_DIM + GLA_VAL_DIM].reshape(B, T, GLA_HEADS, GLA_DV)
    out_gate = z[..., 2 * GLA_KEY_DIM + GLA_VAL_DIM:]

    def log_decay(d):
        zg = (h @ w_gate_down[d]) @ w_gate_up[d] + gate_bias[d]
        return (jax.nn.log_sigmoid(zg.astype(jnp.float32)) / GLA_TAU).reshape(B, T, GLA_HEADS, GLA_DK)

    o = bidir_gated_scan(q, v, k, log_decay(0), k, log_decay(1), n_ctx)
    o = rms_norm(o, g_norm).reshape(B, T, GLA_VAL_DIM) * jax.nn.silu(out_gate)
    y_lat = o[:, n_ctx:] @ w_o
    y_ctx = o[:, :n_ctx] @ w_o if need_ctx else None
    return y_lat, y_ctx

def centred_shift(h):
    hp = jnp.pad(h, ((0, 0), (1, 1), (0, 0)))
    return 0.5 * (hp[:, :-2] + hp[:, 2:]) - h

def rwkv7_scan(r, decay, kk, a, k, v):
    B, T, H, N = r.shape

    def step(S, xs):
        r_t, w_t, kk_t, a_t, k_t, v_t = xs
        sa = jnp.einsum('bhvk,bhk->bhv', S, -kk_t)
        S = (S * w_t[:, :, None, :] + sa[..., None] * (kk_t * a_t)[:, :, None, :]
             + v_t[..., None] * k_t[:, :, None, :])
        return S, jnp.einsum('bhvk,bhk->bhv', S, r_t)

    tm = lambda t: jnp.moveaxis(t.astype(jnp.float32), 1, 0)
    S0 = jnp.zeros((B, H, N, N), jnp.float32)
    _, y = lax.scan(step, S0, (tm(r), tm(decay), tm(kk), tm(a), tm(k), tm(v)))
    return jnp.moveaxis(y, 0, 1)

def rwkv7_mixer(h_lat, h_ctx, mix, w_rkv, w0, w_down, w_up, a0, a_down, a_up, g_down, g_up,
                k_k, k_a, r_k, ln_w, ln_b, w_o, need_ctx):
    n_ctx = h_ctx.shape[1]
    h = jnp.concatenate([h_ctx, h_lat], axis=1)
    dx = jnp.concatenate([centred_shift(h_ctx), centred_shift(h_lat)], axis=1)
    B, T, D = h.shape
    hm = h[None] + dx[None] * mix[:, None, None, :]
    r, k, v = jnp.einsum('nbtd,nde->nbte', hm[:3], w_rkv)
    hw, ha, hg = hm[3], hm[4], hm[5]
    heads = lambda t: t.reshape(B, T, RWKV_HEADS, RWKV_HEAD_SIZE)
    g = jax.nn.sigmoid(hg @ g_down) @ g_up
    kk = heads((k * k_k).astype(jnp.float32))
    kk = kk / jnp.maximum(jnp.sqrt(jnp.sum(kk * kk, axis=-1, keepdims=True)), L2_EPS)

    def direction(d):
        w_log = -jax.nn.softplus(-(w0[d] + jnp.tanh(hw @ w_down[d]) @ w_up[d]).astype(jnp.float32)) - 0.5
        a = jax.nn.sigmoid((a0[d] + (ha @ a_down[d]) @ a_up[d]).astype(jnp.float32))
        return heads(jnp.exp(-jnp.exp(w_log))), heads(a), heads(k * (1 + (a - 1) * k_a))

    dec_f, a_f, k_f = direction(0)
    dec_b, a_b, k_b = direction(1)
    r_h, v_h = heads(r), heads(v)
    rev = lambda t: reverse_segments(t, n_ctx)
    y = (rwkv7_scan(r_h, dec_f, kk, a_f, k_f, v_h)
         + rev(rwkv7_scan(rev(r_h), rev(dec_b), rev(kk), rev(a_b), rev(k_b), rev(v_h))))
    mu = jnp.mean(y, axis=-1, keepdims=True)
    var = jnp.mean(jnp.square(y - mu), axis=-1, keepdims=True)
    yn = ((y - mu) * lax.rsqrt(var + RWKV_LN_EPS) * ln_w.reshape(RWKV_HEADS, RWKV_HEAD_SIZE)
          + ln_b.reshape(RWKV_HEADS, RWKV_HEAD_SIZE))
    bonus = jnp.sum(r_h * (0.5 * (k_f + k_b)) * r_k, axis=-1, keepdims=True) * v_h
    out = (yn + bonus).reshape(B, T, D).astype(h.dtype) * g
    y_lat = out[:, n_ctx:] @ w_o
    y_ctx = out[:, :n_ctx] @ w_o if need_ctx else None
    return y_lat, y_ctx

def hgrn_lower_bound(lb_param, layer):
    p = jax.nn.softmax(lb_param.astype(jnp.float32), axis=0)
    return (jnp.cumsum(p, axis=0) - p[0])[layer]

def hgrn2_mixer(h_lat, h_ctx, w_in, w_f, lower_bound, g_norm, w_o, need_ctx):
    n_ctx = h_ctx.shape[1]
    h = jnp.concatenate([h_ctx, h_lat], axis=1)
    B, T, _ = h.shape
    z = h @ w_in
    q = jax.nn.silu(z[..., :HGRN_FORGET_DIM]).reshape(B, T, HGRN_HEADS, HGRN_EXPAND)
    i_in = z[..., HGRN_FORGET_DIM:HGRN_FORGET_DIM + D_MODEL].reshape(B, T, HGRN_HEADS, HGRN_IN_DIM)
    out_gate = z[..., HGRN_FORGET_DIM + D_MODEL:]

    def gates(d):
        f = lower_bound + (1 - lower_bound) * jax.nn.sigmoid((h @ w_f[d]).astype(jnp.float32))
        f = f.reshape(B, T, HGRN_HEADS, HGRN_EXPAND)
        return 1 - f, jnp.log(f)

    k_fwd, g_fwd = gates(0)
    k_bwd, g_bwd = gates(1)
    o = bidir_gated_scan(q, i_in, k_fwd, g_fwd, k_bwd, g_bwd, n_ctx)
    o = rms_norm(o, g_norm).reshape(B, T, D_MODEL) * jax.nn.silu(out_gate)
    y_lat = o[:, n_ctx:] @ w_o
    y_ctx = o[:, :n_ctx] @ w_o if need_ctx else None
    return y_lat, y_ctx

def first_inputs(seed: int = 0) -> dict:
    key = jax.random.key(seed)
    keys = iter(jax.random.split(key, 48))
    D = D_MODEL

    def normal(shape, scale):
        return jax.random.normal(next(keys), shape, jnp.float32) * scale

    def gain(shape):
        return 1.0 + normal(shape, 0.02)

    nA, nB, nC, nH = N_ATTN_LAYERS, N_GLA_LAYERS, N_RWKV_LAYERS, N_HGRN_LAYERS
    return {
        "x": normal((BATCH, SEQ, D), 1.0),
        "c": normal((BATCH, D), 1.0),
        "ctx": normal((BATCH, CTX_LEN, D), 1.0),
        "c_ctx": normal((D,), 1.0),
        "w_mod": normal((DEPTH, D, N_MOD * D), 0.5 * D ** -0.5),
        "b_mod": normal((DEPTH, N_MOD * D), 0.01),
        "g_pre_mix": gain((DEPTH, D)),
        "g_post_mix": gain((DEPTH, D)),
        "g_pre_mlp": gain((DEPTH, D)),
        "g_post_mlp": gain((DEPTH, D)),
        "w_mlp_in": normal((DEPTH, D, MLP_HIDDEN), D ** -0.5),
        "w_mlp_out": normal((DEPTH, MLP_HIDDEN, D), MLP_HIDDEN ** -0.5),
        "attn_w_qkv": normal((nA, D, (ATTN_HEADS + 2 * ATTN_KV_HEADS) * HEAD_DIM), D ** -0.5),
        "attn_w_o": normal((nA, ATTN_HEADS * HEAD_DIM, D), (ATTN_HEADS * HEAD_DIM) ** -0.5),
        "attn_sink": normal((nA, ATTN_HEADS), 0.5),
        "gla_w_in": normal((nB, D, 2 * GLA_KEY_DIM + 2 * GLA_VAL_DIM), D ** -0.5),
        "gla_w_gate_down": normal((nB, 2, D, GLA_GATE_RANK), D ** -0.5),
        "gla_w_gate_up": normal((nB, 2, GLA_GATE_RANK, GLA_KEY_DIM), GLA_GATE_RANK ** -0.5),
        "gla_gate_bias": normal((nB, 2, GLA_KEY_DIM), 0.1),
        "gla_g_norm": gain((nB, GLA_DV)),
        "gla_w_o": normal((nB, GLA_VAL_DIM, D), GLA_VAL_DIM ** -0.5),
        "rwkv_mix": jax.random.uniform(next(keys), (nC, 6, D), jnp.float32),
        "rwkv_w_rkv": normal((nC, 3, D, D), D ** -0.5),
        "rwkv_w0": -1.5 + normal((nC, 2, D), 0.5),
        "rwkv_w_down": normal((nC, 2, D, RWKV_DECAY_RANK), D ** -0.5),
        "rwkv_w_up": normal((nC, 2, RWKV_DECAY_RANK, D), 0.1 * RWKV_DECAY_RANK ** -0.5),
        "rwkv_a0": normal((nC, 2, D), 0.1),
        "rwkv_a_down": normal((nC, 2, D, RWKV_AAA_RANK), D ** -0.5),
        "rwkv_a_up": normal((nC, 2, RWKV_AAA_RANK, D), RWKV_AAA_RANK ** -0.5),
        "rwkv_g_down": normal((nC, D, RWKV_GATE_RANK), D ** -0.5),
        "rwkv_g_up": normal((nC, RWKV_GATE_RANK, D), RWKV_GATE_RANK ** -0.5),
        "rwkv_k_k": 0.85 + normal((nC, D), 0.02),
        "rwkv_k_a": gain((nC, D)),
        "rwkv_r_k": normal((nC, RWKV_HEADS, RWKV_HEAD_SIZE), 0.1),
        "rwkv_ln_w": gain((nC, D)),
        "rwkv_ln_b": normal((nC, D), 0.02),
        "rwkv_w_o": normal((nC, D, D), D ** -0.5),
        "hgrn_w_in": normal((nH, D, HGRN_FORGET_DIM + 2 * D), D ** -0.5),
        "hgrn_w_f": normal((nH, 2, D, HGRN_FORGET_DIM), D ** -0.5),
        "hgrn_lb": normal((DEPTH, HGRN_FORGET_DIM), 0.1),
        "hgrn_g_norm": gain((nH, HGRN_IN_DIM)),
        "hgrn_w_o": normal((nH, D, D), D ** -0.5),
    }

def first_block(x, c, ctx, c_ctx, w_mod, b_mod, g_pre_mix, g_post_mix, g_pre_mlp, g_post_mlp,
              w_mlp_in, w_mlp_out, attn_w_qkv, attn_w_o, attn_sink,
              gla_w_in, gla_w_gate_down, gla_w_gate_up, gla_gate_bias, gla_g_norm, gla_w_o,
              rwkv_mix, rwkv_w_rkv, rwkv_w0, rwkv_w_down, rwkv_w_up, rwkv_a0, rwkv_a_down,
              rwkv_a_up, rwkv_g_down, rwkv_g_up, rwkv_k_k, rwkv_k_a, rwkv_r_k, rwkv_ln_w,
              rwkv_ln_b, rwkv_w_o, hgrn_w_in, hgrn_w_f, hgrn_lb, hgrn_g_norm, hgrn_w_o):
    n_latent = x.shape[1]
    rows = n_latent // GRID_W
    cos, sin = axial_rope_tables(rows)
    c_lat = jax.nn.silu(c)
    c_con = jax.nn.silu(c_ctx)
    x_lat, x_ctx = x, ctx
    for i in range(DEPTH):
        kind, j = i % N_MIXERS, i // N_MIXERS
        need_ctx = i < DEPTH - 1
        m_lat = jnp.split((c_lat @ w_mod[i] + b_mod[i])[:, None, :], N_MOD, axis=-1)
        m_ctx = jnp.split(c_con @ w_mod[i] + b_mod[i], N_MOD, axis=-1)
        h_lat = modulate(x_lat, g_pre_mix[i], m_lat[0], m_lat[1])
        h_ctx = modulate(x_ctx, g_pre_mix[i], m_ctx[0], m_ctx[1])
        if kind == 0:
            y_lat, y_ctx = windowed_gqa_sink(h_lat, h_ctx, attn_w_qkv[j], attn_w_o[j], attn_sink[j],
                                             cos, sin, need_ctx)
        elif kind == 1:
            y_lat, y_ctx = gla_mixer(h_lat, h_ctx, gla_w_in[j], gla_w_gate_down[j], gla_w_gate_up[j],
                                     gla_gate_bias[j], gla_g_norm[j], gla_w_o[j], need_ctx)
        elif kind == 2:
            y_lat, y_ctx = rwkv7_mixer(h_lat, h_ctx, rwkv_mix[j], rwkv_w_rkv[j], rwkv_w0[j],
                                       rwkv_w_down[j], rwkv_w_up[j], rwkv_a0[j], rwkv_a_down[j],
                                       rwkv_a_up[j], rwkv_g_down[j], rwkv_g_up[j], rwkv_k_k[j],
                                       rwkv_k_a[j], rwkv_r_k[j], rwkv_ln_w[j], rwkv_ln_b[j],
                                       rwkv_w_o[j], need_ctx)
        else:
            y_lat, y_ctx = hgrn2_mixer(h_lat, h_ctx, hgrn_w_in[j], hgrn_w_f[j],
                                       hgrn_lower_bound(hgrn_lb, i), hgrn_g_norm[j], hgrn_w_o[j],
                                       need_ctx)
        x_lat = x_lat + m_lat[2] * rms_norm(y_lat, g_post_mix[i])
        f_lat = channel_mlp(modulate(x_lat, g_pre_mlp[i], m_lat[3], m_lat[4]), w_mlp_in[i], w_mlp_out[i])
        x_lat = x_lat + m_lat[5] * rms_norm(f_lat, g_post_mlp[i])
        if need_ctx:
            x_ctx = x_ctx + m_ctx[2] * rms_norm(y_ctx, g_post_mix[i])
            f_ctx = channel_mlp(modulate(x_ctx, g_pre_mlp[i], m_ctx[3], m_ctx[4]), w_mlp_in[i], w_mlp_out[i])
            x_ctx = x_ctx + m_ctx[5] * rms_norm(f_ctx, g_post_mlp[i])
    return x_lat


DEPTH_2 = 1

CHUNK = 64
LEFT_CHUNKS = 8
BAND = LEFT_CHUNKS + 1
ATTN_HEADS_2 = 8
HEAD_DIM_2 = 64
D_ATTN = ATTN_HEADS_2 * HEAD_DIM_2
MAX_REL = 256
REL_FUTURE = CHUNK - 1
N_REL = REL_FUTURE + MAX_REL + 1
D_SSM = D_MODEL // 2
SSM_GROUP = 16
SSM_GROUPS = D_SSM // SSM_GROUP
SSM_STATE = 64
STEP_MIN = 0.001
STEP_MAX = 0.1
N_BRANCH = 2
D_IN = 3 * D_ATTN + D_SSM + N_BRANCH * D_MODEL
N_GROUPS = 4
EXPERTS_PER_GROUP = 4
N_EXPERTS = N_GROUPS * EXPERTS_PER_GROUP
TOP_K = 2
D_EXPERT = D_MODEL // 4
EPS = 1e-6
NEG_INF_2 = -1e30


def rms_norm_2(x, gain):
    xf = x.astype(jnp.float32)
    y = xf * lax.rsqrt(jnp.mean(xf * xf, axis=-1, keepdims=True) + EPS)
    return (y * gain.astype(jnp.float32)).astype(x.dtype)

def chunked_relpos_attention(q, k, v, q_gain, k_gain, rel_bias):
    b, l = q.shape[0], q.shape[1]
    nc = l // CHUNK
    q = rms_norm_2(q, q_gain)
    k = rms_norm_2(k, k_gain)
    pad = ((0, 0), (LEFT_CHUNKS * CHUNK, 0), (0, 0), (0, 0))
    kp = jnp.pad(k, pad).reshape(b, nc + LEFT_CHUNKS, CHUNK, ATTN_HEADS_2, HEAD_DIM_2)
    vp = jnp.pad(v, pad).reshape(b, nc + LEFT_CHUNKS, CHUNK, ATTN_HEADS_2, HEAD_DIM_2)
    band = jnp.arange(nc)[:, None] + jnp.arange(BAND)[None, :]
    kb = kp[:, band].reshape(b, nc, BAND * CHUNK, ATTN_HEADS_2, HEAD_DIM_2)
    vb = vp[:, band].reshape(b, nc, BAND * CHUNK, ATTN_HEADS_2, HEAD_DIM_2)
    qc = q.reshape(b, nc, CHUNK, ATTN_HEADS_2, HEAD_DIM_2)
    s = jnp.einsum('bnqhd,bnkhd->bhnqk', qc, kb).astype(jnp.float32) * (HEAD_DIM_2 ** -0.5)
    q_off = jnp.arange(CHUNK)[:, None] + LEFT_CHUNKS * CHUNK
    k_off = jnp.arange(BAND * CHUNK)[None, :]
    rel_idx = jnp.clip(q_off - k_off, -REL_FUTURE, MAX_REL) + REL_FUTURE
    bias = rel_bias.astype(jnp.float32)[:, rel_idx]
    key_pos = (jnp.arange(nc)[:, None] - LEFT_CHUNKS) * CHUNK + k_off
    valid = key_pos >= 0
    s = jnp.where(valid[None, None, :, None, :], s + bias[None, :, None], NEG_INF_2)
    p = jax.nn.softmax(s, axis=-1).astype(v.dtype)
    o = jnp.einsum('bhnqk,bnkhd->bnqhd', p, vb)
    return o.reshape(b, l, D_ATTN)

def _complex_linear_combine(e1, e2):
    a1r, a1i, b1r, b1i = e1
    a2r, a2i, b2r, b2i = e2
    ar = a2r * a1r - a2i * a1i
    ai = a2r * a1i + a2i * a1r
    br = a2r * b1r - a2i * b1i + b2r
    bi = a2r * b1i + a2i * b1r + b2i
    return (ar, ai, br, bi)

def s5_ssm_glu(u, lambda_re, lambda_im, log_step, b_re, b_im, c_re, c_im, d_skip, w_glu, b_glu):
    bsz, l = u.shape[0], u.shape[1]
    uf = u.astype(jnp.float32).reshape(bsz, l, SSM_GROUPS, SSM_GROUP)
    lre = lambda_re.astype(jnp.float32)
    lim = lambda_im.astype(jnp.float32)
    step = jnp.exp(log_step.astype(jnp.float32))[:, None]
    mag = jnp.exp(lre * step)
    ang = lim * step
    a_re = mag * jnp.cos(ang)
    a_im = mag * jnp.sin(ang)
    num_re = a_re - 1.0
    num_im = a_im
    den = lre * lre + lim * lim
    f_re = (num_re * lre + num_im * lim) / den
    f_im = (num_im * lre - num_re * lim) / den
    br = b_re.astype(jnp.float32)
    bi = b_im.astype(jnp.float32)
    bb_re = f_re[..., None] * br - f_im[..., None] * bi
    bb_im = f_re[..., None] * bi + f_im[..., None] * br
    bu_re = jnp.einsum('blgc,gpc->blgp', uf, bb_re)
    bu_im = jnp.einsum('blgc,gpc->blgp', uf, bb_im)
    a_re_t = jnp.broadcast_to(a_re[None, None], (1, l, SSM_GROUPS, SSM_STATE))
    a_im_t = jnp.broadcast_to(a_im[None, None], (1, l, SSM_GROUPS, SSM_STATE))
    _, _, s_re, s_im = lax.associative_scan(
        _complex_linear_combine, (a_re_t, a_im_t, bu_re, bu_im), axis=1)
    y = (jnp.einsum('blgp,gcp->blgc', s_re, c_re.astype(jnp.float32))
         - jnp.einsum('blgp,gcp->blgc', s_im, c_im.astype(jnp.float32))
         + d_skip.astype(jnp.float32).reshape(SSM_GROUPS, SSM_GROUP) * uf)
    y = y.reshape(bsz, l, D_SSM).astype(u.dtype)
    z = jax.nn.gelu(y)
    return z * jax.nn.sigmoid(z @ w_glu + b_glu)

def hierarchical_moe(h, w_group_router, group_bias, w_expert_router, expert_bias, w_e_gate, w_e_up, w_e_down):
    bsz, l, d = h.shape
    t = bsz * l
    ht = h.reshape(t, d)
    group_logits = (ht @ w_group_router).astype(jnp.float32) + group_bias.astype(jnp.float32)
    group_prob = jax.nn.softmax(group_logits, axis=-1)
    g_prob, g_idx = lax.top_k(group_prob, 1)
    expert_logits = (ht @ w_expert_router).astype(jnp.float32) + expert_bias.astype(jnp.float32)
    expert_logits = expert_logits.reshape(t, N_GROUPS, EXPERTS_PER_GROUP)
    in_group = jnp.take_along_axis(expert_logits, g_idx[:, :, None], axis=1)[:, 0]
    e_prob = jax.nn.softmax(in_group, axis=-1)
    e_val, e_loc = lax.top_k(e_prob, TOP_K)
    e_val = e_val / jnp.sum(e_val, axis=-1, keepdims=True)
    weights = g_prob * e_val
    e_glob = g_idx * EXPERTS_PER_GROUP + e_loc
    gates = jnp.sum(jax.nn.one_hot(e_glob, N_EXPERTS, dtype=jnp.float32) * weights[..., None], axis=1)
    gates = gates.astype(h.dtype)
    a = jnp.einsum('td,edf->tef', ht, w_e_gate)
    u = jnp.einsum('td,edf->tef', ht, w_e_up)
    hid = jax.nn.silu(a) * u * gates[:, :, None]
    out = hid.reshape(t, N_EXPERTS * D_EXPERT) @ w_e_down.reshape(N_EXPERTS * D_EXPERT, d)
    return out.reshape(bsz, l, d)

def second_inputs(seed: int = 0) -> dict:
    key = jax.random.key(seed)
    ks = jax.random.split(key, 32)
    f32 = jnp.float32

    def nrm(k, shape, scale):
        return jax.random.normal(k, shape, f32) * scale

    n_idx = jnp.arange(SSM_STATE, dtype=f32)
    return {
        'x': nrm(ks[0], (BATCH, SEQ, D_MODEL), 1.0),
        'mix_norm_gain': 1.0 + nrm(ks[1], (DEPTH_2, D_MODEL), 0.02),
        'w_in': nrm(ks[2], (DEPTH_2, D_MODEL, D_IN), D_MODEL ** -0.5),
        'b_gate': nrm(ks[3], (DEPTH_2, N_BRANCH * D_MODEL), 0.02),
        'q_gain': 1.0 + nrm(ks[4], (DEPTH_2, HEAD_DIM_2), 0.02),
        'k_gain': 1.0 + nrm(ks[5], (DEPTH_2, HEAD_DIM_2), 0.02),
        'rel_bias': nrm(ks[6], (DEPTH_2, ATTN_HEADS_2, N_REL), 0.1),
        'ssm_lambda_re': -0.5 + nrm(ks[7], (DEPTH_2, SSM_GROUPS, SSM_STATE), 0.01),
        'ssm_lambda_im': math.pi * n_idx[None, None, :] + nrm(ks[8], (DEPTH_2, SSM_GROUPS, SSM_STATE), 0.01),
        'ssm_log_step': jax.random.uniform(ks[9], (DEPTH_2, SSM_GROUPS), f32, math.log(STEP_MIN), math.log(STEP_MAX)),
        'ssm_b_re': nrm(ks[10], (DEPTH_2, SSM_GROUPS, SSM_STATE, SSM_GROUP), (2 * SSM_GROUP) ** -0.5),
        'ssm_b_im': nrm(ks[11], (DEPTH_2, SSM_GROUPS, SSM_STATE, SSM_GROUP), (2 * SSM_GROUP) ** -0.5),
        'ssm_c_re': nrm(ks[12], (DEPTH_2, SSM_GROUPS, SSM_GROUP, SSM_STATE), (2 * SSM_STATE) ** -0.5),
        'ssm_c_im': nrm(ks[13], (DEPTH_2, SSM_GROUPS, SSM_GROUP, SSM_STATE), (2 * SSM_STATE) ** -0.5),
        'ssm_d': nrm(ks[14], (DEPTH_2, D_SSM), 1.0),
        'w_glu': nrm(ks[15], (DEPTH_2, D_SSM, D_SSM), D_SSM ** -0.5),
        'b_glu': nrm(ks[16], (DEPTH_2, D_SSM), 0.02),
        'w_branch': nrm(ks[17], (DEPTH_2, D_ATTN + D_SSM, D_MODEL), D_ATTN ** -0.5),
        'w_out': nrm(ks[18], (DEPTH_2, D_MODEL, D_MODEL), D_MODEL ** -0.5),
        'ffn_norm_gain': 1.0 + nrm(ks[19], (DEPTH_2, D_MODEL), 0.02),
        'w_group_router': nrm(ks[20], (DEPTH_2, D_MODEL, N_GROUPS), D_MODEL ** -0.5),
        'group_bias': nrm(ks[21], (DEPTH_2, N_GROUPS), 0.01),
        'w_expert_router': nrm(ks[22], (DEPTH_2, D_MODEL, N_EXPERTS), D_MODEL ** -0.5),
        'expert_bias': nrm(ks[23], (DEPTH_2, N_EXPERTS), 0.01),
        'w_e_gate': nrm(ks[24], (DEPTH_2, N_EXPERTS, D_MODEL, D_EXPERT), D_MODEL ** -0.5),
        'w_e_up': nrm(ks[25], (DEPTH_2, N_EXPERTS, D_MODEL, D_EXPERT), D_MODEL ** -0.5),
        'w_e_down': nrm(ks[26], (DEPTH_2, N_EXPERTS, D_EXPERT, D_MODEL), D_EXPERT ** -0.5),
    }

def second_block(x, mix_norm_gain, w_in, b_gate, q_gain, k_gain, rel_bias,
              ssm_lambda_re, ssm_lambda_im, ssm_log_step, ssm_b_re, ssm_b_im,
              ssm_c_re, ssm_c_im, ssm_d, w_glu, b_glu, w_branch, w_out,
              ffn_norm_gain, w_group_router, group_bias, w_expert_router, expert_bias,
              w_e_gate, w_e_up, w_e_down):
    bsz, l, _ = x.shape
    for i in range(DEPTH_2):
        h = rms_norm_2(x, mix_norm_gain[i])
        proj = h @ w_in[i]
        q = proj[..., :D_ATTN].reshape(bsz, l, ATTN_HEADS_2, HEAD_DIM_2)
        k = proj[..., D_ATTN:2 * D_ATTN].reshape(bsz, l, ATTN_HEADS_2, HEAD_DIM_2)
        v = proj[..., 2 * D_ATTN:3 * D_ATTN].reshape(bsz, l, ATTN_HEADS_2, HEAD_DIM_2)
        u = proj[..., 3 * D_ATTN:3 * D_ATTN + D_SSM]
        gate = jax.nn.sigmoid(proj[..., 3 * D_ATTN + D_SSM:] + b_gate[i])
        gate = gate.reshape(bsz, l, N_BRANCH, D_MODEL)
        y_attn = chunked_relpos_attention(q, k, v, q_gain[i], k_gain[i], rel_bias[i])
        y_ssm = s5_ssm_glu(u, ssm_lambda_re[i], ssm_lambda_im[i], ssm_log_step[i],
                           ssm_b_re[i], ssm_b_im[i], ssm_c_re[i], ssm_c_im[i],
                           ssm_d[i], w_glu[i], b_glu[i])
        wb = w_branch[i]
        merged = (gate[:, :, 0] * (y_attn @ wb[:D_ATTN])
                  + gate[:, :, 1] * (y_ssm @ wb[D_ATTN:]))
        x = x + merged @ w_out[i]
        h = rms_norm_2(x, ffn_norm_gain[i])
        x = x + hierarchical_moe(h, w_group_router[i], group_bias[i], w_expert_router[i],
                                 expert_bias[i], w_e_gate[i], w_e_up[i], w_e_down[i])
    return x


def setup_inputs(seed=0):
    out = dict(first_inputs(seed))
    for name, value in second_inputs(seed + 1).items():
        if name != "x":
            out[name + "_2"] = value
    return out


def reference(
    x, c, ctx, c_ctx, w_mod, b_mod, g_pre_mix, g_post_mix, g_pre_mlp, g_post_mlp, w_mlp_in,
    w_mlp_out, attn_w_qkv, attn_w_o, attn_sink, gla_w_in, gla_w_gate_down, gla_w_gate_up,
    gla_gate_bias, gla_g_norm, gla_w_o, rwkv_mix, rwkv_w_rkv, rwkv_w0, rwkv_w_down, rwkv_w_up,
    rwkv_a0, rwkv_a_down, rwkv_a_up, rwkv_g_down, rwkv_g_up, rwkv_k_k, rwkv_k_a, rwkv_r_k,
    rwkv_ln_w, rwkv_ln_b, rwkv_w_o, hgrn_w_in, hgrn_w_f, hgrn_lb, hgrn_g_norm, hgrn_w_o,
    mix_norm_gain_2, w_in_2, b_gate_2, q_gain_2, k_gain_2, rel_bias_2, ssm_lambda_re_2,
    ssm_lambda_im_2, ssm_log_step_2, ssm_b_re_2, ssm_b_im_2, ssm_c_re_2, ssm_c_im_2, ssm_d_2,
    w_glu_2, b_glu_2, w_branch_2, w_out_2, ffn_norm_gain_2, w_group_router_2, group_bias_2,
    w_expert_router_2, expert_bias_2, w_e_gate_2, w_e_up_2, w_e_down_2,
):
    x = first_block(
        x, c, ctx, c_ctx, w_mod, b_mod, g_pre_mix, g_post_mix, g_pre_mlp, g_post_mlp, w_mlp_in,
        w_mlp_out, attn_w_qkv, attn_w_o, attn_sink, gla_w_in, gla_w_gate_down, gla_w_gate_up,
        gla_gate_bias, gla_g_norm, gla_w_o, rwkv_mix, rwkv_w_rkv, rwkv_w0, rwkv_w_down,
        rwkv_w_up, rwkv_a0, rwkv_a_down, rwkv_a_up, rwkv_g_down, rwkv_g_up, rwkv_k_k, rwkv_k_a,
        rwkv_r_k, rwkv_ln_w, rwkv_ln_b, rwkv_w_o, hgrn_w_in, hgrn_w_f, hgrn_lb, hgrn_g_norm,
        hgrn_w_o,
    )
    return second_block(
        x, mix_norm_gain_2, w_in_2, b_gate_2, q_gain_2, k_gain_2, rel_bias_2, ssm_lambda_re_2,
        ssm_lambda_im_2, ssm_log_step_2, ssm_b_re_2, ssm_b_im_2, ssm_c_re_2, ssm_c_im_2,
        ssm_d_2, w_glu_2, b_glu_2, w_branch_2, w_out_2, ffn_norm_gain_2, w_group_router_2,
        group_bias_2, w_expert_router_2, expert_bias_2, w_e_gate_2, w_e_up_2, w_e_down_2,
    )


_drawn_inputs = setup_inputs


def setup_inputs(seed=0):
    import zlib

    import numpy as np

    out = dict(_drawn_inputs(seed))
    spreads = {}
    factors = {'g_post_mix': 3.098,
     'g_pre_mlp': 3.933,
     'g_post_mlp': 3.417,
     'attn_sink': 8.0,
     'gla_g_norm': 5.267,
     'mix_norm_gain_2': 5.508,
     'b_gate_2': 8.0,
     'q_gain_2': 8.0,
     'k_gain_2': 8.0,
     'rel_bias_2': 7.785,
     'ssm_lambda_re_2': 188.592,
     'ssm_lambda_im_2': 10.226,
     'ssm_log_step_2': 3.302,
     'ssm_b_re_2': 23.326,
     'ssm_b_im_2': 21.641,
     'ssm_c_re_2': 23.464,
     'ssm_c_im_2': 23.508,
     'b_glu_2': 36.629,
     'group_bias_2': 64.0,
     'expert_bias_2': 64.0,
     'ffn_norm_gain_2': 8.0}
    for name, (base, spread) in spreads.items():
        noise = np.random.default_rng([zlib.crc32(name.encode()), seed]).standard_normal(out[name].shape)
        drawn = base * np.exp(spread * noise) if base else spread * noise
        out[name] = jnp.asarray(drawn.astype(out[name].dtype))
    for name, factor in factors.items():
        out[name] = (out[name] * factor).astype(out[name].dtype)
    return out
```

```python
from contextlib import ExitStack

import concourse.bass as bass
import numpy as np
from concourse import mybir

F32 = mybir.dt.float32
FR = mybir.dt.float32r
I32 = mybir.dt.int32
ALU = mybir.AluOpType
ACT = mybir.ActivationFunctionType
AX = mybir.AxisListType

P = 128
D = 1024
KT = D // P
LAT, CTX = 512, 256
T = LAT + CTX
EPS = 1e-6
NEG = -1e30
HD = 64
HEADS, KV_HEADS, GROUP = 16, 4, 4
MLP_STEPS = 4
GLA_HEADS, GLA_DV = 4, 256
CHUNK = 64
TILE = KT * P
RING, WRING, BANKS = 4, 2, 4
EXPERT_GROUPS, EXPERTS_PER = 4, 4

VEC = {}
_at = 0
for _name, _n in [("c", 8), ("c_ctx", 8), ("b_mod", 96), ("g_pre_mix", 16), ("g_post_mix", 16), ("g_pre_mlp", 16),
                  ("g_post_mlp", 16), ("gate_bias", 8), ("gla_g", 2), ("mix_gain", 8), ("b_gate", 16), ("q_gain", 1),
                  ("k_gain", 1), ("ssm_d", 4), ("b_glu", 4), ("ffn_gain", 8), ("lam_re", 16), ("lam_im", 16),
                  ("log_step", 16)]:
    VEC[_name] = (_at, _n)
    _at += _n
NVEC = _at
ROW = {"sink": (0, 16), "group_bias": (16, 4), "expert_bias": (20, 16)}
NROW = 36


def schedule():
    tiles = []

    def mod(layer, t):
        tiles.append((False, "w_mod", layer, 0, t * P))

    def dense(name, col, which=0, row=0):
        tiles.append((True, name, which, row, col))

    for t in range(16):
        mod(0, t)
    for t in range(8, 12):
        dense("attn_w_qkv", t * P)
    for g in range(KV_HEADS):
        dense("attn_w_qkv", 2 * g * P)
        dense("attn_w_qkv", (2 * g + 1) * P)
        for t in range(8):
            mod(0, 16 + 8 * g + t)
    for t in range(KT):
        dense("attn_w_o", t * P)
    for i in range(MLP_STEPS):
        for t in range(16):
            if t < 8:
                dense("w_mlp_in", (8 * i + t) * P)
            else:
                dense("w_mlp_out", (t - 8) * P, row=i * D)
            if t < 12:
                mod(1, 12 * i + t)
    for h in range(GLA_HEADS):
        for col in (h * P, 512 + h * P, D + h * GLA_DV, D + h * GLA_DV + P, 2 * D + h * GLA_DV, 2 * D + h * GLA_DV + P):
            dense("gla_w_in", col)
    for t in range(KT):
        dense("gla_w_o", t * P)
    for i in range(MLP_STEPS):
        for t in range(KT):
            dense("w_mlp_in", (8 * i + t) * P, 1)
        for t in range(KT):
            dense("w_mlp_out", t * P, 1, i * D)
    for t in range(4):
        dense("w_in_2", 1536 + t * P)
    for t in range(4):
        for part in range(3):
            dense("w_in_2", 512 * part + t * P)
    for t in range(16):
        dense("w_in_2", 2048 + t * P)
    for t in range(2):
        dense("w_glu_2", 2 * t * P)
    for t in range(KT):
        dense("w_branch_2", t * P)
    for t in range(KT):
        dense("w_out_2", t * P)
    for g in range(EXPERT_GROUPS):
        for e in range(EXPERTS_PER):
            for t in range(2):
                dense("w_e_gate_2", t * P, EXPERTS_PER * g + e)
                dense("w_e_up_2", t * P, EXPERTS_PER * g + e)
        for t in range(KT):
            dense("w_e_down_2", t * P, 0, g * D)
    return tiles


class At:

    def __init__(self, kinds):
        self.kinds = kinds
        self.u = self.d = self.n = 0
        self.it = None
        self.per = (0, 0, 0)

    def enter(self, it, u, d, n):
        self.it, self.per = it, (u, d, n)

    def leave(self, trips):
        self.u += (trips - 1) * self.per[0]
        self.d += (trips - 1) * self.per[1]
        self.n += (trips - 1) * self.per[2]
        self.it, self.per = None, (0, 0, 0)

    def next_dense(self):
        self.u += 1
        self.d += 1
        self.to_dense()

    def to_dense(self):
        while self.u < len(self.kinds) and not self.kinds[self.u]:
            self.u += 1

    def _times(self, static, per, mod):
        if self.it is None or per == 0:
            return static
        assert per % mod == 0
        return self.it * (per // mod) + static

    def tile(self, add=1):
        return self._times(self.u // RING + add, self.per[0], RING)

    def landed(self):
        if self.it is None:
            return 16 * (self.u // RING + 1)
        return self.it * (16 * (self.per[0] // RING)) + 16 * (self.u // RING + 1)

    def dense(self, add):
        return self._times(self.d + add, self.per[1], 1)

    def group(self, add=1):
        return self._times(self.n + add, self.per[2], 1)

    def bank_uses(self):
        return self._times(self.n // BANKS, self.per[2], BANKS)


def parts_of(tokens):
    return [(0, LAT, 0), (LAT, T, 1)] if tokens == T else [(0, LAT, 0)]


def cuts_of(tokens):
    return [(0, 384), (384, 768)] if tokens == T else [(0, 512)]


def trips(engine, n):
    return engine.Fori(0, n)


def backbone_kernel(nc, a, out_d, upto=99):
    ctx = ExitStack()
    kinds = [t[0] for t in schedule()]
    with ctx:
        sem_cache = {}

        def sem(name):
            if name not in sem_cache:
                sem_cache[name] = ctx.enter_context(nc.semaphore(name))
            return sem_cache[name]

        def sb(stack, name, shape, dt=F32):
            return stack.enter_context(nc.sbuf_tensor(name, shape, dt))

        X = sb(ctx, "X", [P, KT, T])
        HH = sb(ctx, "HH", [P, KT, T], FR)
        HL = sb(ctx, "HL", [P, KT, T], FR)
        AH = sb(ctx, "AH", [P, KT, T], FR)
        AL = sb(ctx, "AL", [P, KT, T], FR)
        RAW = sb(ctx, "RAW", [P, RING, TILE])
        WH = sb(ctx, "WH", [P, WRING, TILE], FR)
        WL = sb(ctx, "WL", [P, WRING, TILE], FR)
        TQ = sb(ctx, "TQ", [P, 2, T])
        TR = sb(ctx, "TR", [P, T])
        VECS = sb(ctx, "VECS", [P, NVEC])
        ROWS = sb(ctx, "ROWS", [P, NROW])
        CONST = sb(ctx, "CONST", [P, 4 * P])
        MOD = sb(ctx, "MOD", [P, 96, 2])
        COND = sb(ctx, "COND", [P, KT, 2])
        CEXP = sb(ctx, "CEXP", [P, 2, KT, 2])
        AMP = sb(ctx, "AMP", [P, 4, KT, 2])
        GATE = sb(ctx, "GATE", [P, 4, KT, 2])
        EPSV = sb(ctx, "EPSV", [P, 1])
        SSMP = sb(ctx, "SSMP", [P, 13, 16])
        NIL = sb(ctx, "NIL", [P, 1])
        IDENT, ONES, SWAP, HALVES = (CONST[:, i * P:(i + 1) * P] for i in range(4))

        def vec(name, i=0, n=1):
            at = VEC[name][0] + i
            return VECS[:, at:at + n]

        with ExitStack() as s1:
            KD = sb(s1, "KD", [P, KV_HEADS, T])
            V = sb(s1, "V", [P, T // P, KV_HEADS * HD])
            QG = sb(s1, "QG", [P, 2, T])
            COS = sb(s1, "COS", [P, LAT])
            SIN = sb(s1, "SIN", [P, LAT])
            BAND = sb(s1, "BAND", [P, 3 * P])
            PB = sb(s1, "PB", [P, 2, 640])
            PTS = sb(s1, "PTS", [P, 2, 5, 2 * P])
            ST = sb(s1, "ST", [P, 2, 8])
        with ExitStack() as s3:
            QT = sb(s3, "QT", [P, T])
            KEYS = sb(s3, "KEYS", [P, T])
            VT = sb(s3, "VT", [P, T // P, GLA_DV])
            B = sb(s3, "B", [P, 2, T])
            BC = sb(s3, "BC", [P, T])
            QD = sb(s3, "QD", [P, LAT])
            KI = sb(s3, "KI", [P, LAT])
            KEF = sb(s3, "KEF", [P, T])
            KE = sb(s3, "KE", [P, T // P, P])
            O = sb(s3, "O", [P, 2, LAT])
            S = sb(s3, "S", [P, 4, GLA_DV])
            ATM = sb(s3, "ATM", [P, 2, 2, P])
            LOW = sb(s3, "LOW", [64, T])
            WU = sb(s3, "WU", [64, 512])
            WDH = sb(s3, "WDH", [P, 512], FR)
            WDL = sb(s3, "WDL", [P, 512], FR)
            CAUSAL = sb(s3, "CAUSAL", [P, 2, P])
            TOT = sb(s3, "TOT", [P, 2, T // CHUNK])
            DEC = sb(s3, "DEC", [P, 2, T // CHUNK])
        with ExitStack() as s4:
            QN = sb(s4, "QN", [P, LAT])
            KN = sb(s4, "KN", [P, LAT])
            V2 = sb(s4, "V2", [P, LAT // P, P])
            SS = sb(s4, "SS", [P, 2, LAT])
            PB2 = sb(s4, "PB2", [P, 2, LAT])
            PTS2 = sb(s4, "PTS2", [P, 2, 4, 2 * P])
            SQ2 = sb(s4, "SQ2", [P, 2, LAT])
            QR = sb(s4, "QR", [P, 2, LAT])
            RS = sb(s4, "RS", [P, 2, LAT])
            BW = sb(s4, "BW", [P, 2, 2, LAT])
            ST2 = sb(s4, "ST2", [P, 2, 8])
        with ExitStack() as s5:
            GATES = sb(s5, "GATES", [P, 16, LAT])
            TRIG = sb(s5, "TRIG", [P, 2, 2, LAT])
            PR = sb(s5, "PR", [P, 4, LAT])
            MATS = sb(s5, "MATS", [P, 2, 4, P])
            TURN = sb(s5, "TURN", [P, LAT])
            IOTA = sb(s5, "IOTA", [P, LAT])
        with ExitStack() as s6:
            RW = sb(s6, "RW", [P, KT * 20])
            RWH = sb(s6, "RWH", [P, KT * 20], FR)
            RWL = sb(s6, "RWL", [P, KT * 20], FR)
            SEL = sb(s6, "SEL", [P, 4, P])
            GT = sb(s6, "GT", [P, 4 * LAT])
            GTS = sb(s6, "GTS", [P, 4, 16])
            GB = sb(s6, "GB", [P, 2, LAT])
            SG = sb(s6, "SG", [P, 2, LAT])
            RT = sb(s6, "RT", [P, 14, 16])
            EL = sb(s6, "EL", [P, 4, 16])
            PREF = sb(s6, "PREF", [P, 4])

        def PV(i):
            return SSMP[:, i, :]

        def UT(t):
            return X[:, 2 * t:2 * t + 2, LAT:T]

        def CM(i):
            return TQ[:, i // 2, LAT + P * (i % 2):LAT + P * (i % 2) + P]

        def nil(k, s):
            return NIL[:, 0:1]

        TWO_PI = 6.283185
        SSM_PREP = 27
        MN = TQ
        SCAN_TILES = [[4, 5, 0, 1, 2, 3], [5, 4, 3, 2, 1, 0]]
        Y = sb(ctx, "Y", [P, KT, T])

        SQ = sb(ctx, "SQ", [P, 2, 512])

        DP = ctx.enter_context(nc.psum_tensor("DP", [P, BANKS, 512], F32))
        XP = ctx.enter_context(nc.psum_tensor("XP", [P, 4, 512], F32))
        XPF = XP[:, :, :].rearrange("p b n -> p (b n)")
        DPF = DP[:, :, :].rearrange("p b n -> p (b n)")
        MODP = XP[:, 3, 256:288].rearrange("p (t s) -> p t s", s=2)

        raw_full = [sem(f"weight_landed{i}") for i in range(RING)]
        raw_done = [sem(f"weight_taken{i}") for i in range(RING)]
        hi_done = sem("weight_high")
        mm_done = sem("group_written")
        bank_free = [sem(f"bank_read{i}") for i in range(BANKS)]
        loads = sem("small_loads")
        rope_loads = sem("rope_loads")
        cond_done = sem("cond_done")
        mods_read = sem("modulation_read")
        amp_done = sem("amplitude_ready")
        NLOADS = 3
        QUERY = HD ** -0.5
        AMP_NORMS = [(0, 1, "g_pre_mix", 0), (0, 4, "g_pre_mlp", 0), (1, 1, "g_pre_mix", 8), (1, 4, "g_pre_mlp", 8)]
        GATE_NORMS = [(0, 2, "g_post_mix", 0), (0, 5, "g_post_mlp", 0), (1, 2, "g_post_mix", 8), (1, 5, "g_post_mlp", 8)]

        def mod_chunk(layer, chunk, s):
            return MOD[:, layer * 48 + chunk * 8:layer * 48 + chunk * 8 + 8, s]

        def shift(layer, chunk):
            return lambda k, s: MOD[:, layer * 48 + chunk * 8 + k, s:s + 1]

        def amp(i):
            return lambda k, s: AMP[:, i, k, s:s + 1]

        def gate(i):
            return lambda k, s: GATE[:, i, k, s:s + 1]

        ALL_GROUPS = (2 * 2 + 2 * 6) + 4 * 4 + 16 + 4 * 32 + 4 * (4 + 12 + 2) + 8 + 64 + 4 + 4 * 6 + 16 + 4 + 16 + 8 + 4 * 24

        def bank(at):
            return at.n % BANKS

        def wait_group(e, at):
            e.wait_ge(mm_done, at.group())

        def wait_read(e, at, back=0):
            e.wait_ge(bank_free[(at.n - back) % BANKS], at._times((at.n - back) // BANKS + 1, at.per[2], BANKS))

        def split_high(act, at, nxt):
            if nxt.u >= len(kinds):
                return
            act.wait_ge(raw_full[nxt.u % RING], nxt.landed())
            if at is not None and at.n:
                act.wait_ge(mm_done, at.group(0))
            act.activation(WH[:, nxt.d % WRING, :], RAW[:, nxt.u % RING, :], ACT.Copy).then_inc(hi_done, 1)
            nxt.next_dense()

        def split_low(dve, nxt):
            if nxt.u >= len(kinds):
                return
            w = nxt.d % WRING
            dve.wait_ge(hi_done, nxt.dense(1))
            dve.tensor_tensor(WL[:, w, :], RAW[:, nxt.u % RING, :], WH[:, w, :].bitcast(F32), ALU.subtract
                              ).then_inc(raw_done[nxt.u % RING], 1)
            nxt.next_dense()

        def three(pe, out, ah, al, bh, bl, first, last):
            pe.matmul(out, al, bh, start=first, stop=False)
            pe.matmul(out, ah, bh, start=False, stop=False)
            return pe.matmul(out, ah, bl, start=False, stop=last)

        def group_begin(pe, at):
            if at.n >= BANKS:
                pe.wait_ge(bank_free[at.n % BANKS], at.bank_uses())

        def tile_begin(pe, at):
            pe.wait_ge(raw_done[at.u % RING], at.tile())

        def feature_group(pe, at, xh, xl, cut, ready=None, ks=range(KT), wk=0):
            w = at.d % WRING
            group_begin(pe, at)
            for i, k in enumerate(ks):
                if ready is not None:
                    ready(pe, k)
                kk = (wk + i) * P
                last = three(pe, DP[:, bank(at), 0:cut[1] - cut[0]], WH[:, w, kk:kk + P], WL[:, w, kk:kk + P],
                             xh[:, k, cut[0]:cut[1]], xl[:, k, cut[0]:cut[1]], i == 0, i == len(ks) - 1)
            last.then_inc(mm_done, 1)
            at.n += 1

        def feature_tile(pe, at, xh, xl, cuts, ready=None):
            tile_begin(pe, at)
            for c, cut in enumerate(cuts):
                feature_group(pe, at, xh, xl, cut, ready if c == 0 else None)
            at.u += 1
            at.d += 1

        def token_tile(pe, at, tiles):
            w = at.d % WRING
            tile_begin(pe, at)
            for m in range(tiles):
                group_begin(pe, at)
                for k in range(KT):
                    last = three(pe, DP[:, bank(at), 0:P], HH[:, k, m * P:(m + 1) * P], HL[:, k, m * P:(m + 1) * P],
                                 WH[:, w, k * P:(k + 1) * P], WL[:, w, k * P:(k + 1) * P], k == 0, k == KT - 1)
                last.then_inc(mm_done, 1)
                at.n += 1
            at.u += 1
            at.d += 1

        def mod_tile(pe, at, col):
            pe.wait_ge(raw_full[at.u % RING], at.landed())
            for k in range(KT):
                last = pe.matmul(MODP[:, col, :], RAW[:, at.u % RING, k * P:(k + 1) * P], COND[:, k, :],
                                 start=(k == 0), stop=(k == KT - 1))
            last.then_inc(raw_done[at.u % RING], 1)
            at.u += 1

        def mod_evacuate(dve, at, n, dst):
            at.u -= 1
            dve.wait_ge(raw_done[at.u % RING], at.tile())
            at.u += 1
            for s in range(2):
                ins = dve.tensor_tensor(MOD[:, dst(n), s], MODP[:, 0:n, s],
                                        VECS[:, dst(n, VEC["b_mod"][0])], ALU.add)
            ins.then_inc(mods_read, 1)

        NORMS = [("pre0", T, "product"), ("post0", T, "sum"), ("pre1", T, "product"), ("post1", T, "sum"),
                 ("pre2", T, "product"), ("post2", LAT, "sum"), ("pre3", LAT, "product"), ("post3", LAT, "sum"),
                 ("mix", LAT, "product"), ("ffn", LAT, "product")]

        def norm_count(nm, step, count):
            for name, tokens, kind in NORMS:
                if name == nm:
                    return count
                parts = KT * len(parts_of(tokens))
                if step in ("squared", "summed"):
                    count += KT
                elif step == "rstd":
                    count += 2
                elif kind == "product" and step in ("scaled", "high", "low"):
                    count += parts
                elif kind == "sum" and step in ("term", "x"):
                    count += parts if step == "term" else KT

        def norm_wait(e, nm, step, count):
            e.wait_ge(sem("norm_" + step), norm_count(nm, step, count))

        def norm_square(act, nm, src, tokens, k):
            if k >= 2:
                norm_wait(act, nm, "summed", k - 1)
            act.activation(TQ[:, k % 2, 0:tokens], src(k), ACT.Square).then_inc(sem("norm_squared"), 1)

        def norm_sum(pe, nm, tokens, k, tiles=KT):
            norm_wait(pe, nm, "squared", k + 1)
            for c, (a0, b0) in enumerate(cuts_of(tokens)):
                last = pe.matmul(XP[:, c, 0:b0 - a0], ONES, TQ[:, k % 2, a0:b0],
                                 start=(k == 0), stop=(k == tiles - 1))
            last.then_inc(sem("norm_summed"), 1)

        def norm_rstd(act, nm, tokens, tiles=KT, n=D):
            norm_wait(act, nm, "summed", tiles)
            cuts = cuts_of(tokens)
            w = cuts[0][1]
            act.activation(TR[:, 0:tokens].rearrange("p (c n) -> p c n", n=w), XP[:, 0:len(cuts), 0:w], ACT.Ln,
                           scale=1.0 / n, bias=EPSV[:, 0:1]).then_inc(sem("norm_rstd"), 1)
            norm_wait(act, nm, "rstd", 1)
            act.activation(TR[:, 0:tokens], TR[:, 0:tokens], ACT.Exp, scale=-0.5).then_inc(sem("norm_rstd"), 1)

        def norm_low(dve, nm, k, np_, tokens, sh):
            norm_wait(dve, nm, "high", np_ * (k + 1))
            for a0, b0, s in parts_of(tokens):
                dve.scalar_tensor_tensor(HL[:, k, a0:b0], TQ[:, k % 2, a0:b0], sh(k, s), HH[:, k, a0:b0].bitcast(F32),
                                         ALU.add, ALU.subtract).then_inc(sem("norm_low"), 1)

        def norm_scale(dve, nm, src, tokens, am, sh):
            norm_wait(dve, nm, "rstd", 2)
            np_ = len(parts_of(tokens))
            for k in range(KT):
                if k >= 2:
                    norm_wait(dve, nm, "low", np_ * (k - 1))
                for a0, b0, s in parts_of(tokens):
                    dve.scalar_tensor_tensor(TQ[:, k % 2, a0:b0], src(k)[:, a0:b0], am(k, s), TR[:, a0:b0],
                                             ALU.mult, ALU.mult).then_inc(sem("norm_scaled"), 1)
                if k >= 1:
                    norm_low(dve, nm, k - 1, np_, tokens, sh)
            norm_low(dve, nm, KT - 1, np_, tokens, sh)

        def norm_high(act, nm, tokens, sh):
            np_ = len(parts_of(tokens))
            for k in range(KT):
                for i, (a0, b0, s) in enumerate(parts_of(tokens)):
                    norm_wait(act, nm, "scaled", np_ * k + i + 1)
                    act.activation(HH[:, k, a0:b0], TQ[:, k % 2, a0:b0], ACT.Identity, bias=sh(k, s)
                                   ).then_inc(sem("norm_high"), 1)

        def norm_ready(nm, tokens):
            np_ = len(parts_of(tokens))
            return lambda pe, k: norm_wait(pe, nm, "low", np_ * (k + 1))

        def residual(dve, nm, tokens, am):
            norm_wait(dve, nm, "rstd", 2)
            np_ = len(parts_of(tokens))
            for k in range(KT + 1):
                if k < KT:
                    for a0, b0, s in parts_of(tokens):
                        dve.scalar_tensor_tensor(Y[:, k, a0:b0], Y[:, k, a0:b0], am(k, s), TR[:, a0:b0],
                                                 ALU.mult, ALU.mult).then_inc(sem("norm_term"), 1)
                if k >= 1:
                    norm_wait(dve, nm, "term", np_ * k)
                    dve.tensor_tensor(X[:, k - 1, 0:tokens], X[:, k - 1, 0:tokens], Y[:, k - 1, 0:tokens],
                                      ALU.add).then_inc(sem("norm_x"), 1)

        def after(name, per=1, base=0):
            return lambda e, k: e.wait_ge(sem(name), base + per * (k + 1))

        def Xk(tokens):
            return lambda k: X[:, k, 0:tokens]

        def Yk(tokens):
            return lambda k: Y[:, k, 0:tokens]

        def blocks(g):
            for b in range(T // P):
                lat = b < LAT // P
                near = [kb for kb in (b - 1, b, b + 1) if 0 <= kb < LAT // P] if lat else []
                for hh in range(GROUP):
                    yield g * 24 + b * 4 + hh, b, hh, near

        block = ctx.enter_context(nc.Block())

        @block.sync
        def _(sp):
            sp.dma_start(VECS[:, :], a["vec"]).then_inc(loads, 16)
            sp.dma_start(CONST[:, :], a["const"]).then_inc(loads, 16)
            sp.dma_start(ROWS[:, :], a["row"]).then_inc(loads, 16)
            for k in range(KT):
                sp.dma_start(X[:, k, :], a["x"][:, k, :]).then_inc(sem(f"x_landed{k // 2}"), 16)
            for i in range(RING):
                sp.dma_start(RAW[:, i, :], a["stream"][i]).then_inc(raw_full[i], 16)
            sp.dma_start(COS[:, :], a["rope"][:, 0:LAT]).then_inc(rope_loads, 16)
            sp.dma_start(SIN[:, :], a["rope"][:, LAT:2 * LAT]).then_inc(rope_loads, 16)
            sp.dma_start(BAND[:, :], a["rope"][:, 2 * LAT:]).then_inc(rope_loads, 16)
            rounds = len(kinds) // RING
            with sp.Fori(1, rounds) as r:
                for i in range(RING):
                    sp.wait_ge(raw_done[i], r)
                    sp.dma_start(RAW[:, i, :], a["stream"][bass.ds(r * RING + i, 1)].rearrange("o p n -> (o p) n")
                                 ).then_inc(raw_full[i], 16)
            for t in range(RING * rounds, len(kinds) + 1):
                sp.wait_ge(raw_done[t % RING], t // RING)
                sp.dma_start(RAW[:, t % RING, :], a["stream"][min(t, len(kinds) - 1)]).then_inc(raw_full[t % RING], 16)
            at = At(kinds)
            at.n = ALL_GROUPS - KT
            for k in range(KT):
                wait_read(sp, at)
                sp.dma_start(out_d[:, k, :], X[:, k, 0:LAT]).then_inc(sem("stored"), 16)
                at.n += 1
            sp.wait_ge(sem("stored"), 16 * KT)

        @block.gpsimd
        def _(pool):
            pool.memset(EPSV[:, :], EPS).then_inc(sem("eps_set"), 1)
            norm_wait(pool, "post0", "x", KT)
            for k in range(KT):
                pool.memset(Y[:, k, :], 0.0).then_inc(sem("y_zero"), 1)

            norm_wait(pool, "post2", "x", KT)
            for k in range(KT):
                pool.memset(Y[:, k, 0:LAT], 0.0).then_inc(sem("y_zero"), 1)

            pool.wait_ge(sem("ssm_prep"), SSM_PREP)
            pool.wait_ge(sem("ssm_loads"), 16)
            MAGIC = 1.5 * 2.0 ** 23

            def turns(i):
                for h in range(2):
                    n = 2 * i + h
                    if n:
                        pool.wait_ge(sem("ssm_trig"), n)
                    pool.tensor_scalar(TURN[:, :], IOTA[:, :], PV(3)[:, i:i + 1], 0.25 * h, ALU.mult, ALU.add
                                       ).then_inc(sem("turn_steps"), 1)
                    pool.wait_ge(sem("turn_steps"), 2 * n + 1)
                    pool.tensor_scalar(TR[:, 0:LAT], TURN[:, :], MAGIC, MAGIC, ALU.add, ALU.subtract
                                       ).then_inc(sem("turn_steps"), 1)
                    pool.wait_ge(sem("turn_steps"), 2 * n + 2)
                    pool.tensor_tensor(TURN[:, :], TURN[:, :], TR[:, 0:LAT], ALU.subtract).then_inc(sem("ssm_turns"), 1)
                    pool.wait_ge(sem("ssm_turns"), n + 1)

            def outputs_scaled(i):
                pool.wait_ge(sem(f"ssm_mats{i % 2}"), 16 * (i // 2 + 1))
                if i:
                    pool.wait_ge(sem("ssm_out"), i)
                cr, ci = MATS[:, i % 2, 2, :], MATS[:, i % 2, 3, :]
                fr, fi = PV(11)[:, i:i + 1], PV(12)[:, i:i + 1]
                count = [7 * i]

                def step(ins):
                    ins.then_inc(sem("c_steps"), 1)
                    count[0] += 1
                    pool.wait_ge(sem("c_steps"), count[0])

                step(pool.tensor_scalar(CM(0), cr, fr, None, ALU.mult))
                step(pool.tensor_scalar(CM(3), ci, fi, None, ALU.mult))
                step(pool.tensor_tensor(CM(1), CM(3), CM(0), ALU.subtract))
                step(pool.tensor_tensor(CM(0), CM(0), CM(3), ALU.subtract))
                step(pool.tensor_scalar(CM(2), cr, fi, None, ALU.mult))
                step(pool.tensor_scalar(CM(3), ci, fr, None, ALU.mult))
                step(pool.tensor_tensor(CM(2), CM(2), CM(3), ALU.add))
                pool.tensor_scalar(CM(2), CM(2), -1.0, None, ALU.mult).then_inc(sem("ssm_c"), 1)
                pool.wait_ge(sem("ssm_c"), i + 1)

            turns(0)
            for i in range(16):
                if i < 15:
                    turns(i + 1)
                outputs_scaled(i)

            pool.wait_ge(sem("merged_low"), KT)
            pool.memset(GT[:, :], 0.0).then_inc(sem("gate_rows_zero"), 1)
        @block.tensor
        def _(pe):
            at = At(kinds)
            c768, c512 = cuts_of(T), cuts_of(LAT)

            pe.wait_ge(loads, 16 * NLOADS)
            for k in range(KT):
                norm_sum(pe, "pre0", T, k)
            pe.wait_ge(cond_done, 5)
            for t in range(16):
                mod_tile(pe, at, t)
            rope = 0

            def rotate(r):
                if r >= 1:
                    pe.wait_ge(sem("rope_sine"), r)
                for c in range(2):
                    wait_read(pe, at, 2 * (2 - r % 2) - c if r % 2 == 0 else 2 - c)
                pe.matmul(XP[:, 0, :], SWAP, TQ[:, r % 2, 0:LAT], start=True, stop=True).then_inc(sem("rope_swapped"), 1)

            feature_tile(pe, at, HH, HL, c768, norm_ready("pre0", T))
            feature_tile(pe, at, HH, HL, c768)
            rotate(0)
            rotate(1)
            token_tile(pe, at, T // P)
            token_tile(pe, at, T // P)

            def scores(aa, b, hh, near, g):
                p, j, rows = aa % 2, hh // 2, slice(64 * (hh % 2), 64 * (hh % 2) + 64)
                q = QG[rows, j, b * P:(b + 1) * P]
                if near:
                    pe.matmul(DPF[:, p * 1024 + 512 - P * len(near):p * 1024 + 512], q,
                              KD[rows, g, near[0] * P:(near[-1] + 1) * P], start=True, stop=True)
                pe.matmul(DPF[:, p * 1024 + 512:p * 1024 + 768], q, KD[rows, g, LAT:T], start=True, stop=True
                          ).then_inc(sem("scored"), 1)

            def transposes(aa, near):
                p = aa % 2
                pe.wait_ge(sem("probabilities"), aa + 1)
                if aa >= 1:
                    pe.wait_ge(sem("transposes_copied"), aa)
                for i in range(len(near) + 2):
                    last = pe.transpose(XPF[:, i * P:(i + 1) * P], PB[:, p, i * P:(i + 1) * P], IDENT)
                last.then_inc(sem("transposed"), 1)

            def weighted_values(q, near, g):
                pe.wait_ge(sem("transposes_copied"), 2 * q + 2)
                if q >= 1:
                    pe.wait_ge(sem("mixed_low"), q)
                keys = near + [4, 5]
                for e in range(2):
                    for i, kt in enumerate(keys):
                        last = pe.matmul(XP[64 * e:64 * e + 64, 2, 0:P],
                                         V[:, kt, g * HD:(g + 1) * HD], PTS[:, q % 2, i, e * P:(e + 1) * P],
                                         start=(i == 0), stop=(i == len(keys) - 1))
                last.then_inc(sem("attended"), 1)

            for g in range(KV_HEADS):
                feature_tile(pe, at, HH, HL, c768)
                feature_tile(pe, at, HH, HL, c768)
                rotate(2 + 2 * g)
                rotate(3 + 2 * g)
                work = list(blocks(g))
                pe.wait_ge(sem("rope_done"), 16 + 4 * (g + 1))
                pe.wait_ge(mods_read, g + 1)
                scores(*work[0], g)
                scores(*work[1], g)
                for i, (aa, b, hh, near) in enumerate(work):
                    transposes(aa, near)
                    if i + 2 < len(work):
                        scores(*work[i + 2], g)
                    if i >= 2 and i % 2 == 0:
                        weighted_values(aa // 2 - 1, work[i - 2][3], g)
                    if i % 3 == 2:
                        mod_tile(pe, at, i // 3)
                weighted_values(aa // 2, near, g)

            pe.wait_ge(sem("mixed_low"), 48)
            for t in range(KT):
                feature_tile(pe, at, AH, AL, c768)
                if t >= 1:
                    norm_sum(pe, "post0", T, t - 1)
            norm_sum(pe, "post0", T, KT - 1)
            for k in range(KT):
                norm_sum(pe, "pre1", T, k)

            tile_begin(pe, at)
            for k in range(KT):
                norm_ready("pre1", T)(pe, k)
            with pe.Fori(0, MLP_STEPS) as it:
                at.enter(it, 28, 16, 32)
                for t in range(2 * KT):
                    if t < KT:
                        feature_tile(pe, at, HH, HL, c768)
                    else:
                        feature_tile(pe, at, AH, AL, c768, (lambda e, k: e.wait_ge(sem("hid0_low"), it * 16 + 2 * (k + 1)))
                                     if t == KT else None)
                    if t == 0:
                        pe.wait_ge(mods_read, it + 5)
                    if t < 12:
                        mod_tile(pe, at, t)
                at.leave(MLP_STEPS)
            for k in range(KT):
                norm_sum(pe, "post1", T, k)

            for k in range(KT):
                norm_sum(pe, "pre2", T, k)

            pe.wait_ge(sem("gate_down_split"), 2)
            for c, (a0, b0) in enumerate(c768):
                for k in range(KT):
                    if c == 0:
                        norm_ready("pre2", T)(pe, k)
                    last = three(pe, XP[0:64, c, 0:384], WDH[:, k * 64:(k + 1) * 64], WDL[:, k * 64:(k + 1) * 64],
                                 HH[:, k, a0:b0], HL[:, k, a0:b0], k == 0, k == KT - 1)
            last.then_inc(sem("gate_low_made"), 1)

            def gate_product(h, d):
                if h == 0 and d == 0:
                    pe.wait_ge(sem("gate_low_read"), 1)
                else:
                    pe.wait_ge(sem("gate_logits_read"), 2 * h + d)
                if h and not d:
                    pe.wait_ge(sem("out_rstd"), 2 * h)
                rows = slice(32 * d, 32 * d + 32)
                for c, (a0, b0) in enumerate(c768):
                    last = pe.matmul(XP[:, c, 0:384], WU[rows, h * P:(h + 1) * P], LOW[rows, a0:b0], start=True, stop=True)
                last.then_inc(sem("gate_logits_made"), 1)

            def key_transposes(h, d):
                s = 2 * h + d
                pe.wait_ge(sem("keys_decayed"), s + 1)
                pe.wait_ge(sem("gate_logits_read"), 2 * h + 2)
                if s:
                    pe.wait_ge(sem("keys_turned_copied"), s)
                for m in range(T // P):
                    last = pe.transpose(XP[:, m // 3, (m % 3) * P:(m % 3 + 1) * P], KEF[:, m * P:(m + 1) * P], IDENT)
                last.then_inc(sem("keys_turned"), 1)

            def scan(h, d):
                s = 2 * h + d
                order = SCAN_TILES[d]
                halves = (0, 1) if d == 0 else (1, 0)

                def mixing(i):
                    m = order[i]
                    if m < LAT // P:
                        j = i - 2
                        n = s * 4 + j
                        if n >= 2:
                            pe.wait_ge(sem("mixing_masked"), n - 1)
                        pe.matmul(DP[:, 2 + j % 2, 0:P], KI[:, m * P:(m + 1) * P], QD[:, m * P:(m + 1) * P],
                                  start=True, stop=True).then_inc(sem("mixing_made"), 1)

                def updates(i):
                    m = order[i]
                    for e, half in enumerate(halves):
                        c = 2 * i + e
                        if c == 11:
                            continue
                        n = s * 11 + c
                        rows = slice(64 * half, 64 * half + 64)
                        if n >= 2:
                            pe.wait_ge(sem("state_updated"), n - 1 if c >= 1 else n)
                        pe.matmul(XP[:, 2 + c % 2, 0:GLA_DV], KE[rows, m, :], VT[rows, m, :], start=True, stop=True
                                  ).then_inc(sem("update_made"), 1)

                def output(i):
                    m = order[i]
                    if m >= LAT // P:
                        return
                    j = i - 2
                    n = s * 4 + j
                    pe.wait_ge(sem("mixing_masked"), n + 1)
                    pe.wait_ge(sem("state_updated"), s * 11 + 2 * i + 1)
                    if n >= 2:
                        pe.wait_ge(sem("mixed_out_read"), n - 1)
                    for v in range(2):
                        for e, half in enumerate(halves):
                            c = 2 * i + e
                            cols = slice(64 * half, 64 * half + 64)
                            out = DP[:, j % 2, v * P + 64 * half:v * P + 64 * half + 64]
                            pe.matmul(out, VT[:, m, v * P:(v + 1) * P], ATM[:, d, j % 2, cols], start=True, stop=False)
                            last = pe.matmul(out, S[:, c % 4, v * P:(v + 1) * P],
                                             QD[:, m * P + 64 * half:m * P + 64 * half + 64], start=False, stop=True)
                    last.then_inc(sem("mixed_out_made"), 1)

                pe.wait_ge(sem("queries_decayed"), s + 1)
                pe.wait_ge(sem("keys_turned_copied"), s + 1)
                mixing(0)
                updates(0)
                for i in range(6):
                    if i < 5:
                        mixing(i + 1)
                        updates(i + 1)
                    output(i)

            for h in range(GLA_HEADS):
                if h:
                    pe.wait_ge(sem("mixed_out_read"), 8 * h)
                feature_tile(pe, at, HH, HL, c768)
                feature_tile(pe, at, HH, HL, c768)
                gate_product(h, 0)
                gate_product(h, 1)
                token_tile(pe, at, T // P)
                token_tile(pe, at, T // P)
                for b in range(BANKS):
                    wait_read(pe, at, b + 1)
                for d in range(2):
                    key_transposes(h, d)
                    scan(h, d)
                pe.wait_ge(sem("keys_turned_copied"), 2 * h + 2)
                for v in range(2):
                    pe.wait_ge(sem("out_squared"), 2 * h + v + 1)
                    last = pe.matmul(XP[:, 0, :], ONES, TQ[:, v, 0:LAT], start=(v == 0), stop=(v == 1))
                last.then_inc(sem("out_summed"), 1)
                pe.wait_ge(sem("mixed_out_read"), 8 * (h + 1))
                for v in range(2):
                    feature_tile(pe, at, HH, HL, c512)

            pe.wait_ge(sem("gla_low"), 8)
            for t in range(KT):
                feature_tile(pe, at, AH, AL, c512)
                if t >= 1:
                    norm_sum(pe, "post2", LAT, t - 1)
            norm_sum(pe, "post2", LAT, KT - 1)
            for k in range(KT):
                norm_sum(pe, "pre3", LAT, k)

            for k in range(KT):
                norm_ready("pre3", LAT)(pe, k)
            with pe.Fori(0, MLP_STEPS) as it:
                at.enter(it, 16, 16, 16)
                for t in range(2 * KT):
                    if t < KT:
                        feature_tile(pe, at, HH, HL, c512)
                    else:
                        feature_tile(pe, at, AH, AL, c512, (lambda e, k: e.wait_ge(sem("hid1_low"), it * 8 + (k + 1)))
                                     if t == KT else None)
                at.leave(MLP_STEPS)
            for k in range(KT):
                norm_sum(pe, "post3", LAT, k)

            for k in range(KT):
                norm_sum(pe, "mix", LAT, k)
            for t in range(4):
                feature_tile(pe, at, HH, HL, c512, norm_ready("mix", LAT) if t == 0 else None)

            def scores2(n, p, b, e):
                rows = slice(64 * e, 64 * e + 64)
                pe.matmul(XP[:, 2 + e, 0:P * (b + 1)], QN[rows, b * P:(b + 1) * P], KN[rows, 0:P * (b + 1)],
                          start=True, stop=True).then_inc(sem("scored2"), 1)

            def transposes2(n, b, e):
                pe.wait_ge(sem("probabilities2"), n + 1)
                if n:
                    pe.wait_ge(sem("transposes_copied2"), n)
                for i in range(b + 1):
                    last = pe.transpose(XP[:, 0, i * P:(i + 1) * P], PB2[:, e, i * P:(i + 1) * P], IDENT)
                last.then_inc(sem("transposed2"), 1)

            def values2(q, b):
                pe.wait_ge(sem("transposes_copied2"), 2 * q + 2)
                if q:
                    pe.wait_ge(sem("mixed_low2"), q)
                for e in range(2):
                    for i in range(b + 1):
                        last = pe.matmul(XP[64 * e:64 * e + 64, 1, 0:P], V2[:, i, e * HD:(e + 1) * HD],
                                         PTS2[:, q % 2, i, e * P:(e + 1) * P], start=(i == 0), stop=(i == b))
                last.then_inc(sem("attended2"), 1)

            for p in range(4):
                feature_tile(pe, at, HH, HL, c512)
                feature_tile(pe, at, HH, HL, c512)
                if p:
                    pe.wait_ge(sem("transposes_copied2"), 8 * p)
                    pe.wait_ge(sem("mixed_low2"), 4 * p)
                for i in range(2):
                    pe.wait_ge(sem("head_squared"), 2 * p + i + 1)
                    pe.matmul(XP[:, i, :], HALVES, SQ2[:, i, :], start=True, stop=True).then_inc(sem("head_summed"), 1)
                token_tile(pe, at, LAT // P)
                for b in range(BANKS):
                    wait_read(pe, at, b + 1)
                pe.wait_ge(sem("head_normed"), 2 * p + 2)
                work = [(p * 8 + 2 * b + e, b, e) for b in range(4) for e in range(2)]
                for n, b, e in work[:2]:
                    scores2(n, p, b, e)
                for i, (n, b, e) in enumerate(work):
                    transposes2(n, b, e)
                    if i + 2 < len(work):
                        n2, b2, e2 = work[i + 2]
                        scores2(n2, p, b2, e2)
                    if i >= 2 and i % 2 == 0:
                        values2(n // 2 - 1, b - 1)
                values2(n // 2, b)

            def ssm_inputs(i):
                pe.wait_ge(sem(f"ssm_mats{i % 2}"), 16 * (i // 2 + 1))
                if i:
                    pe.wait_ge(sem("ssm_turned"), 4 * i)
                u = UT(i // 4)
                for z in range(2):
                    last = pe.matmul(XP[:, z, :].rearrange("p (a n) -> p a n", a=2), MATS[:, i % 2, z, :], u,
                                     start=True, stop=True)
                last.then_inc(sem("ssm_driven"), 1)

            def ssm_outputs(i):
                pe.wait_ge(sem("ssm_c"), i + 1)
                t, j = i // 4, i % 4
                if t >= 2 and j == 0:
                    pe.wait_ge(sem("ssm_y"), t - 1)
                for q, (c, k) in enumerate([(0, 0), (1, 1), (2, 2), (2, 3)]):
                    pe.wait_ge(sem("ssm_products"), 4 * i + q + 1)
                    last = pe.matmul(XP[:, 2 + t % 2, :], CM(c), PR[:, k, :], start=(j == 0 and q == 0), stop=(j == 3 and q == 3))
                last.then_inc(sem("ssm_out"), 1)

            pe.wait_ge(sem("mixed_low2"), 16)
            ssm_inputs(0)
            for i in range(16):
                feature_tile(pe, at, HH, HL, c512)
                if i < 15:
                    ssm_inputs(i + 1)
                ssm_outputs(i)

            def ZT(x, k):
                return x[:, 2 * k:2 * k + 2, LAT:T]

            for t in range(2):
                w = at.d % WRING
                tile_begin(pe, at)
                for jj in range(2):
                    group_begin(pe, at)
                    for k in range(4):
                        if t == 0 and jj == 0:
                            pe.wait_ge(sem("z_low"), k + 1)
                        kk = (4 * jj + k) * P
                        last = three(pe, DP[:, bank(at), :].rearrange("p (a n) -> p a n", a=2), WH[:, w, kk:kk + P],
                                     WL[:, w, kk:kk + P], ZT(AH, k), ZT(AL, k), k == 0, k == 3)
                    last.then_inc(mm_done, 1)
                    at.n += 1
                at.u, at.d = at.u + 1, at.d + 1

            for t in range(KT):
                tile_begin(pe, at)
                for half in range(2):
                    if half and t == 0:
                        pe.wait_ge(sem("ssm_low"), 4)
                    feature_group(pe, at, AH, AL, (0, LAT), ks=range(4 * half, 4 * half + 4), wk=4 * half)
                at.u, at.d = at.u + 1, at.d + 1

            for t in range(KT):
                feature_tile(pe, at, HH, HL, c512, after("merged_low") if t == 0 else None)
                if t >= 1:
                    norm_sum(pe, "ffn", LAT, t - 1)
            norm_sum(pe, "ffn", LAT, KT - 1)

            for m in range(4):
                for k in range(KT):
                    if m == 0:
                        norm_ready("ffn", LAT)(pe, k)
                        pe.wait_ge(sem("router_split"), 2)
                    last = three(pe, XP[:, 0, m * 20:(m + 1) * 20], HH[:, k, m * P:(m + 1) * P], HL[:, k, m * P:(m + 1) * P],
                                 RWH[:, k * 20:(k + 1) * 20], RWL[:, k * 20:(k + 1) * 20], k == 0, k == KT - 1)
            last.then_inc(sem("router_made"), 1)
            pe.wait_ge(sem("expert_low"), 1)
            for g in range(EXPERT_GROUPS):
                for m in range(4):
                    last = pe.transpose(XP[0:4, g, m * P:(m + 1) * P], GTS[:, m, 4 * g:4 * g + 4], IDENT)
            last.then_inc(sem("gates_turned"), 1)

            with pe.Fori(0, EXPERT_GROUPS) as g:
                at.enter(g, 24, 24, 24)
                for e in range(EXPERTS_PER):
                    pe.wait_ge(sem("gate_row_read"), g * 4 + (e + 1))
                    pe.matmul(XP[:, e % 2, :], SEL[:, e, :], GT[:, bass.ds(g * 512, 512)], start=True, stop=True
                              ).then_inc(sem("gate_row_made"), 1)
                    for j in range(4):
                        feature_tile(pe, at, HH, HL, c512)
                for t in range(KT):
                    feature_tile(pe, at, AH, AL, c512, (lambda q, k: q.wait_ge(sem("expert_low"), g * 8 + (k + 2)))
                                 if t == 0 else None)
                at.leave(EXPERT_GROUPS)

        @block.scalar
        def _(act):
            at, nxt = At(kinds), At(kinds)
            nxt.to_dense()

            act.wait_ge(loads, 16 * NLOADS)
            conds = VECS[:, 0:16].rearrange("p (s k) -> p k s", s=2)
            act.activation(CEXP[:, 0, :, :], conds, ACT.Exp, scale=-1.0).then_inc(cond_done, 1)
            for k in range(KT):
                act.wait_ge(sem(f"x_landed{k // 2}"), 32)
                norm_square(act, "pre0", Xk(T), T, k)
            act.wait_ge(sem("eps_set"), 1)
            norm_rstd(act, "pre0", T)
            norm_high(act, "pre0", T, shift(0, 0))
            at.u = 16

            def copy_group(out, scale=1.0):
                wait_group(act, at)
                act.activation(out, DP[:, bank(at), 0:384] if out.shape[-1] == 384 else DP[:, bank(at), 0:out.shape[-1]],
                               ACT.Copy, scale=scale).then_inc(bank_free[bank(at)], 1)
                at.n += 1

            def copy_feature(r, scale):
                for c in range(2):
                    copy_group(TQ[:, r % 2, 384 * c:384 * c + 384], scale)
                at.u += 1
                at.d += 1

            split_high(act, at, nxt)
            split_high(act, None, nxt)
            copy_feature(0, 1.0)
            split_high(act, at, nxt)
            copy_feature(1, 1.0)
            for v in range(2):
                split_high(act, at, nxt)
                for m in range(T // P):
                    copy_group(V[:, m, v * P:(v + 1) * P])
                at.u += 1
                at.d += 1

            def exps(aa, b, hh, near, g):
                p, n = aa % 2, P * (len(near) + 2)
                act.wait_ge(sem("shift_ready"), aa + 1)
                if aa >= 2:
                    act.wait_ge(sem("transposed"), aa - 1)
                act.activation(PB[:, p, 0:n], DPF[:, p * 1024 + 768 - n:p * 1024 + 768], ACT.Exp, bias=ST[:, p, 1:2],
                               accum_out=ST[:, p, 2:3]).then_inc(sem("exponentials"), 1)
                head = GROUP * g + hh
                act.activation(ST[:, p, 3:4], ROWS[:, head:head + 1], ACT.Exp, bias=ST[:, p, 1:2]
                               ).then_inc(sem("exponentials"), 1)

            def copy_transposes(aa, near):
                p, q, e, n = aa % 2, aa // 2, aa % 2, len(near) + 2
                act.wait_ge(sem("transposed"), aa + 1)
                if q >= 2:
                    act.wait_ge(sem("attended"), q - 1)
                act.activation(PTS[:, q % 2, 0:n, e * P:(e + 1) * P],
                               XPF[:, 0:n * P].rearrange("p (k n) -> p k n", n=P), ACT.Copy
                               ).then_inc(sem("transposes_copied"), 1)

            def mixed_high(q, b, j, g):
                act.wait_ge(sem("attended"), q + 1)
                act.activation(AH[:, 2 * g + j, b * P:(b + 1) * P], XP[:, 2, 0:P], ACT.Copy
                               ).then_inc(sem("mixed_high"), 1)

            for g in range(KV_HEADS):
                for j in range(2):
                    if j == 0:
                        split_high(act, at, nxt)
                    if g == 0 and j == 0:
                        act.wait_ge(sem("rope_done"), 8)
                    if g == 0 and j == 1:
                        act.wait_ge(sem("rope_done"), 16)
                    copy_feature(2 + 2 * g + j, QUERY)
                work = list(blocks(g))
                exps(*work[0], g)
                for i, (aa, b, hh, near) in enumerate(work):
                    if i + 1 < len(work):
                        exps(*work[i + 1], g)
                    copy_transposes(aa, near)
                    if i >= 2 and i % 2 == 0:
                        mixed_high(aa // 2 - 1, work[i - 2][1], work[i - 2][2] // 2, g)
                mixed_high(aa // 2, b, hh // 2, g)
                at.u += 8
                split_high(act, at, nxt)

            for t in range(KT):
                split_high(act, at, nxt)
                for c in range(2):
                    copy_group(Y[:, t, 384 * c:384 * c + 384])
                at.u += 1
                at.d += 1
                wait_read(act, at, 1)
                norm_square(act, "post0", Yk(T), T, t)
            norm_rstd(act, "post0", T)
            for k in range(KT):
                norm_wait(act, "post0", "x", k + 1)
                norm_square(act, "pre1", Xk(T), T, k)
            norm_rstd(act, "pre1", T)
            norm_high(act, "pre1", T, shift(0, 3))

            with act.Fori(0, MLP_STEPS) as it:
                at.enter(it, 28, 16, 32)
                nxt.enter(it, 28, 16, 32)
                for t in range(2 * KT):
                    split_high(act, at, nxt)
                    if t < KT:
                        for c in range(2):
                            i = 2 * t + c
                            wait_read(act, at, 0)
                            if i >= 2:
                                act.wait_ge(sem("hid0_low"), it * 16 + (i - 1))
                            r = TQ[:, i % 2, 0:384]
                            act.activation(SQ[:, i % 2, 0:384], r, ACT.Square)
                            act.activation(AH[:, t, 384 * c:384 * c + 384], r, ACT.Square).then_inc(sem("hid0_high"), 1)
                            at.n += 1
                    else:
                        at.n += 2
                    at.u += 1
                    at.d += 1
                    if t < 12:
                        at.u += 1
                at.leave(MLP_STEPS)
                nxt.leave(MLP_STEPS)
                nxt.u = at.u + 1
            for b in range(BANKS):
                wait_read(act, at, b + 1)
            for k in range(KT):
                norm_square(act, "post1", Yk(T), T, k)
            norm_rstd(act, "post1", T)

            for k in range(KT):
                norm_wait(act, "post1", "x", k + 1)
                norm_square(act, "pre2", Xk(T), T, k)
            act.dma_start(QD[:, :], a["gla_down"]).then_inc(sem("gla_loads"), 16)
            act.dma_start(WU[:, :], a["gla_up"]).then_inc(sem("gla_loads"), 16)
            act.dma_start(CAUSAL[:, :, :], a["causal"]).then_inc(sem("gla_loads"), 16)
            norm_rstd(act, "pre2", T)
            act.wait_ge(sem("gla_loads"), 48)
            act.activation(WDH[:, :], QD[:, :], ACT.Copy).then_inc(sem("gate_down_split"), 1)
            norm_high(act, "pre2", T, shift(1, 0))
            act.wait_ge(sem("gate_low_made"), 1)
            act.activation(LOW[:, :].rearrange("p (c n) -> p c n", n=384), XP[0:64, 0:2, 0:384], ACT.Copy
                           ).then_inc(sem("gate_low_read"), 1)
            INV = 1.0 / 16.0
            exps_n = [0]

            def gate_exps(h, d):
                s = 2 * h + d
                act.wait_ge(sem("gate_folded"), s + 1)
                act.activation(B[:, d, :], B[:, d, :], ACT.Exp).then_inc(sem("gate_exp"), 1)
                act.wait_ge(sem("gate_exp"), s + 1)
                act.activation(B[:, d, :], B[:, d, :], ACT.Ln, bias=1.0).then_inc(sem("gate_log"), 1)

            def decay_exps(h, d):
                s = 2 * h + d
                act.wait_ge(sem("decays_summed"), s + 1)
                if s:
                    act.wait_ge(sem("mixed_out_made"), 4 * s)
                act.activation(B[:, d, :], B[:, d, :], ACT.Exp, scale=INV).then_inc(sem("decay_exps"), 1)
                act.activation(QD[:, :], BC[:, 0:LAT], ACT.Exp, scale=INV).then_inc(sem("decay_exps"), 1)
                act.activation(KI[:, :], BC[:, 0:LAT], ACT.Exp, scale=-INV).then_inc(sem("decay_exps"), 1)
                act.activation(DEC[:, d, :], TOT[:, d, :], ACT.Exp, scale=INV).then_inc(sem("decay_exps"), 1)

            def scan_outputs(h, d):
                s = 2 * h + d
                act.wait_ge(sem("keys_turned"), s + 1)
                if s:
                    act.wait_ge(sem("update_made"), 11 * s)
                act.activation(KE[:, :, :].rearrange("p (c m) n -> p c (m n)", c=2), XP[:, 0:2, 0:384], ACT.Copy
                               ).then_inc(sem("keys_turned_copied"), 1)
                if d == 0:
                    for i in range(2, 6):
                        m, n = SCAN_TILES[d][i], 4 * s + i - 2
                        act.wait_ge(sem("mixed_out_made"), n + 1)
                        if h and i == 2:
                            act.wait_ge(sem("gla_high"), 2 * h)
                        act.activation(O[:, :, m * P:(m + 1) * P], DP[:, i % 2, 0:2 * P].rearrange("p (v n) -> p v n", v=2),
                                       ACT.Copy).then_inc(sem("mixed_out_read"), 1)

            for h in range(GLA_HEADS):
                split_high(act, at, nxt)
                for c in range(2):
                    copy_group(QT[:, 384 * c:384 * c + 384], P ** -0.5)
                at.u, at.d = at.u + 1, at.d + 1
                split_high(act, at, nxt)
                for c in range(2):
                    copy_group(KEYS[:, 384 * c:384 * c + 384])
                at.u, at.d = at.u + 1, at.d + 1
                gate_exps(h, 0)
                gate_exps(h, 1)
                for v in range(2):
                    split_high(act, at, nxt)
                    for m in range(T // P):
                        copy_group(VT[:, m, v * P:(v + 1) * P])
                    at.u, at.d = at.u + 1, at.d + 1
                for d in range(2):
                    decay_exps(h, d)
                    scan_outputs(h, d)
                for v in range(2):
                    act.wait_ge(sem("mixed_out_read"), 8 * (h + 1))
                    act.activation(TQ[:, v, 0:LAT], O[:, v, :], ACT.Square).then_inc(sem("out_squared"), 1)
                act.wait_ge(sem("out_summed"), h + 1)
                act.activation(TR[:, 0:LAT], XP[:, 0, :], ACT.Ln, scale=1.0 / GLA_DV, bias=EPSV[:, 0:1]
                               ).then_inc(sem("out_rstd"), 1)
                act.wait_ge(sem("out_rstd"), 2 * h + 1)
                act.activation(TR[:, 0:LAT], TR[:, 0:LAT], ACT.Exp, scale=-0.5).then_inc(sem("out_rstd"), 1)
                for v in range(2):
                    split_high(act, at, nxt)
                    n = 2 * h + v
                    wait_group(act, at)
                    act.activation(TQ[:, v, 0:LAT], DP[:, bank(at), :], ACT.Sigmoid).then_inc(sem("gla_sigmoid"), 1)
                    at.n, at.u, at.d = at.n + 1, at.u + 1, at.d + 1
                for v in range(2):
                    n = 2 * h + v
                    act.wait_ge(sem("gla_gated"), n + 1)
                    act.activation(AH[:, n, 0:LAT], O[:, v, :], ACT.Copy).then_inc(sem("gla_high"), 1)

            for t in range(KT):
                split_high(act, at, nxt)
                copy_group(Y[:, t, 0:LAT])
                at.u, at.d = at.u + 1, at.d + 1
                wait_read(act, at, 1)
                norm_square(act, "post2", Yk(LAT), LAT, t)
            norm_rstd(act, "post2", LAT)
            for k in range(KT):
                norm_wait(act, "post2", "x", k + 1)
                norm_square(act, "pre3", Xk(LAT), LAT, k)
            norm_rstd(act, "pre3", LAT)
            norm_high(act, "pre3", LAT, shift(1, 3))

            with act.Fori(0, MLP_STEPS) as it:
                at.enter(it, 16, 16, 16)
                nxt.enter(it, 16, 16, 16)
                for t in range(2 * KT):
                    split_high(act, at, nxt)
                    if t < KT:
                        wait_read(act, at, 0)
                        if t >= 2:
                            act.wait_ge(sem("hid1_low"), it * 8 + (t - 1))
                        r = TQ[:, t % 2, 0:LAT]
                        act.activation(SQ[:, t % 2, :], r, ACT.Square)
                        act.activation(AH[:, t, 0:LAT], r, ACT.Square).then_inc(sem("hid1_high"), 1)
                    at.n, at.u, at.d = at.n + 1, at.u + 1, at.d + 1
                at.leave(MLP_STEPS)
                nxt.leave(MLP_STEPS)
            for b in range(BANKS):
                wait_read(act, at, b + 1)
            for k in range(KT):
                norm_square(act, "post3", Yk(LAT), LAT, k)
            norm_rstd(act, "post3", LAT)

            for k in range(KT):
                norm_wait(act, "post3", "x", k + 1)
                norm_square(act, "mix", Xk(LAT), LAT, k)
            for p in range(2):
                act.dma_start(BW[:, p, :, :], a["rel"][p]).then_inc(sem(f"bias_landed{p}"), 16)
            norm_rstd(act, "mix", LAT)
            norm_high(act, "mix", LAT, nil)
            act.activation(PV(0), vec("log_step", 0, 16), ACT.Exp).then_inc(sem("ssm_prep"), 1)
            act.wait_ge(sem("ssm_prep"), 3)
            act.activation(PV(2), PV(1), ACT.Exp).then_inc(sem("ssm_prep"), 1)

            for t in range(4):
                split_high(act, at, nxt)
                wait_group(act, at)
                act.activation(UT(t), DP[:, bank(at), :].rearrange("p (a n) -> p a n", a=2), ACT.Copy
                               ).then_inc(bank_free[bank(at)], 1)
                at.n, at.u, at.d = at.n + 1, at.u + 1, at.d + 1

            def exps2(n, b, e):
                act.wait_ge(sem("shift_ready2"), n + 1)
                if n >= 2:
                    act.wait_ge(sem("transposed2"), n - 1)
                w = P * (b + 1)
                act.activation(PB2[:, e, 0:w], SS[:, e, 0:w], ACT.Exp, bias=ST2[:, e, 1:2], accum_out=ST2[:, e, 2:3]
                               ).then_inc(sem("exponentials2"), 1)

            def copy_transposes2(n, b, e):
                act.wait_ge(sem("transposed2"), n + 1)
                q = n // 2
                if q >= 2:
                    act.wait_ge(sem("attended2"), q - 1)
                act.activation(PTS2[:, q % 2, 0:b + 1, e * P:(e + 1) * P],
                               XP[:, 0, 0:P * (b + 1)].rearrange("p (k n) -> p k n", n=P), ACT.Copy
                               ).then_inc(sem("transposes_copied2"), 1)

            def mixed_high2(q, p, b):
                act.wait_ge(sem("attended2"), q + 1)
                act.activation(AH[:, p, b * P:(b + 1) * P], XP[:, 1, 0:P], ACT.Copy).then_inc(sem("mixed_high2"), 1)

            for p in range(4):
                for i in range(2):
                    split_high(act, at, nxt)
                    wait_group(act, at)
                    if p:
                        act.wait_ge(sem("head_normed"), 2 * p)
                    act.activation(SQ2[:, i, :], DP[:, bank(at), :], ACT.Square).then_inc(sem("head_squared"), 1)
                    act.activation(QR[:, i, :], DP[:, bank(at), :], ACT.Copy).then_inc(bank_free[bank(at)], 1)
                    at.n, at.u, at.d = at.n + 1, at.u + 1, at.d + 1
                for i in range(2):
                    act.wait_ge(sem("head_summed"), 2 * p + i + 1)
                    act.activation(RS[:, i, :], XP[:, i, :], ACT.Ln, scale=1.0 / HD, bias=EPSV[:, 0:1]
                                   ).then_inc(sem("head_ln"), 1)
                    act.wait_ge(sem("head_ln"), 2 * p + i + 1)
                    act.activation(RS[:, i, :], RS[:, i, :], ACT.Exp, scale=-0.5).then_inc(sem("head_rstd"), 1)
                split_high(act, at, nxt)
                if p:
                    act.wait_ge(sem("attended2"), 4 * p)
                for m in range(LAT // P):
                    copy_group(V2[:, m, :])
                at.u, at.d = at.u + 1, at.d + 1
                work = [(p * 8 + 2 * b + e, b, e) for b in range(4) for e in range(2)]
                exps2(*work[0])
                for i, (n, b, e) in enumerate(work):
                    if i + 1 < len(work):
                        exps2(*work[i + 1])
                    copy_transposes2(n, b, e)
                    if i >= 2 and i % 2 == 0:
                        mixed_high2(n // 2 - 1, p, b - 1)
                mixed_high2(n // 2, p, b)
                if p < 2:
                    act.wait_ge(sem("bias_used"), 8 * (p + 1))
                    act.dma_start(BW[:, p, :, :], a["rel"][p + 2]).then_inc(sem(f"bias_landed{p}"), 16)

            act.wait_ge(sem("attended2"), 16)
            act.wait_ge(sem("mixed_low2"), 16)
            act.dma_start(IOTA[:, :], a["iota"]).then_inc(sem("ssm_loads"), 16)
            act.dma_start(MATS[:, 0, :, :], a["ssm"][0]).then_inc(sem("ssm_mats0"), 16)
            act.wait_ge(sem("ssm_prep"), 12)
            act.activation(PV(7), PV(5), ACT.Sin, scale=TWO_PI).then_inc(sem("ssm_trig0"), 1)
            act.activation(PV(8), PV(6), ACT.Sin, scale=TWO_PI).then_inc(sem("ssm_trig0"), 1)

            def trig(i):
                if i >= 2:
                    act.wait_ge(sem("ssm_products"), 4 * (i - 1))
                for h in range(2):
                    act.wait_ge(sem("ssm_turns"), 2 * i + h + 1)
                    act.activation(TRIG[:, i % 2, h, :], TURN[:, :], ACT.Sin, scale=TWO_PI).then_inc(sem("ssm_trig"), 1)

            trig(0)
            for i in range(16):
                split_high(act, at, nxt)
                if i < 15:
                    if i >= 1:
                        act.wait_ge(sem("ssm_c"), i)
                        act.wait_ge(sem("ssm_driven"), i)
                    act.dma_start(MATS[:, (i + 1) % 2, :, :], a["ssm"][i + 1]).then_inc(sem(f"ssm_mats{(i + 1) % 2}"), 16)
                    trig(i + 1)
                wait_group(act, at)
                act.activation(GATES[:, i, :], DP[:, bank(at), :], ACT.Sigmoid, bias=vec("b_gate", i)
                               ).then_inc(bank_free[bank(at)], 1)
                at.n, at.u, at.d = at.n + 1, at.u + 1, at.d + 1
            for t in range(4):
                act.wait_ge(sem("gelu_inner"), t + 1)
                act.activation(PR[:, t, :], PR[:, t, :], ACT.Sigmoid, scale=2.0 * 0.7978845608028654
                               ).then_inc(sem("gelu_sigmoid"), 1)
            for t in range(4):
                act.wait_ge(sem("z_made"), t + 1)
                act.activation(AH[:, 2 * t:2 * t + 2, LAT:T], UT(t), ACT.Copy).then_inc(sem("z_high"), 1)
            for t in range(2):
                split_high(act, at, nxt)
                for jj in range(2):
                    j = 2 * t + jj
                    wait_group(act, at)
                    act.activation(PR[:, j, :], DP[:, bank(at), :], ACT.Sigmoid, bias=vec("b_glu", j)
                                   ).then_inc(bank_free[bank(at)], 1)
                    at.n += 1
                at.u, at.d = at.u + 1, at.d + 1
            for j in range(4):
                act.wait_ge(sem("ssm_gated"), j + 1)
                act.activation(AH[:, 4 + j, 0:LAT], PR[:, j, :], ACT.Copy).then_inc(sem("ssm_high"), 1)

            for t in range(KT):
                split_high(act, at, nxt)
                act.wait_ge(sem("merged"), t + 1)
                act.activation(HH[:, t, 0:LAT], TQ[:, t % 2, 0:LAT], ACT.Copy).then_inc(sem("merged_high"), 1)
                at.n, at.u, at.d = at.n + 2, at.u + 1, at.d + 1
            act.wait_ge(sem("merged_low"), KT)
            act.dma_start(RW[:, :], a["router"]).then_inc(sem("moe_loads"), 16)
            act.dma_start(SEL[:, :, :], a["select"]).then_inc(sem("moe_loads"), 16)
            for t in range(KT):
                if t == 2:
                    act.wait_ge(sem("moe_loads"), 32)
                    act.activation(RWH[:, :], RW[:, :], ACT.Copy).then_inc(sem("router_split"), 1)
                split_high(act, at, nxt)
                wait_read(act, at, 0)
                norm_square(act, "ffn", Xk(LAT), LAT, t)
                at.n, at.u, at.d = at.n + 1, at.u + 1, at.d + 1
            norm_rstd(act, "ffn", LAT)
            norm_high(act, "ffn", LAT, nil)
            act.wait_ge(sem("route"), 3)
            act.activation(RT[:, 1, 0:16], RT[:, 1, 0:16], ACT.Exp).then_inc(sem("route_exp"), 1)
            act.wait_ge(sem("route"), 12)
            act.activation(RT[:, 6, 0:16], RT[:, 6, 0:16], ACT.Exp).then_inc(sem("route_exp"), 1)
            act.wait_ge(sem("gates_turned"), 1)
            act.wait_ge(sem("gate_rows_zero"), 1)
            act.activation(GT[0:4, :].rearrange("p (g n) -> p g n", g=4), XP[0:4, :, :], ACT.Copy
                           ).then_inc(sem("gate_row_read"), 1)

            with act.Fori(0, EXPERT_GROUPS) as g:
                at.enter(g, 24, 24, 24)
                nxt.enter(g, 24, 24, 24)
                for e in range(EXPERTS_PER):
                    act.wait_ge(sem("gate_row_made"), g * 4 + (e + 1))
                    act.wait_ge(sem("expert_low"), g * 8 + max(1, 2 * e - 1))
                    act.activation(GB[:, e % 2, :], XP[:, e % 2, :], ACT.Copy).then_inc(sem("gate_row_read"), 1)
                    for j in range(2):
                        f = 2 * e + j
                        split_high(act, at, nxt)
                        wait_group(act, at)
                        if f >= 2:
                            act.wait_ge(sem("expert_low"), g * 8 + f)
                        act.activation(SG[:, j, :], DP[:, bank(at), :], ACT.Sigmoid).then_inc(sem("expert_sigmoid"), 1)
                        at.n, at.u, at.d = at.n + 1, at.u + 1, at.d + 1
                        split_high(act, at, nxt)
                        at.n, at.u, at.d = at.n + 1, at.u + 1, at.d + 1
                        wait_read(act, at, 1)
                        act.activation(AH[:, f, 0:LAT], SG[:, j, :], ACT.Copy).then_inc(sem("expert_high"), 1)
                for t in range(KT):
                    split_high(act, at, nxt)
                    at.n, at.u, at.d = at.n + 1, at.u + 1, at.d + 1
                at.leave(EXPERT_GROUPS)
                nxt.leave(EXPERT_GROUPS)

        @block.vector
        def _(dve):
            at, nxt = At(kinds), At(kinds)
            nxt.to_dense()
            dve.memset(NIL[:, :], 0.0).then_inc(sem("nil_set"), 1)
            dve.wait_ge(cond_done, 1)
            dve.tensor_scalar(CEXP[:, 1, :, :], CEXP[:, 0, :, :], 1.0, None, ALU.add).then_inc(cond_done, 1)
            dve.wait_ge(cond_done, 2)
            dve.reciprocal(CEXP[:, 0, :, :], CEXP[:, 1, :, :]).then_inc(cond_done, 1)
            dve.wait_ge(cond_done, 3)
            dve.tensor_tensor(COND[:, :, :], CEXP[:, 0, :, :], VECS[:, 0:16].rearrange("p (s k) -> p k s", s=2),
                              ALU.mult).then_inc(cond_done, 2)

            def amplitude(i):
                layer, chunk, name, off = AMP_NORMS[i]
                for s in range(2):
                    dve.scalar_tensor_tensor(AMP[:, i, :, s], mod_chunk(layer, chunk, s), 1.0, vec(name, off, 8),
                                             ALU.add, ALU.mult).then_inc(amp_done, 1)

            def gating(i):
                layer, chunk, name, off = GATE_NORMS[i]
                for s in range(2):
                    dve.tensor_tensor(GATE[:, i, :, s], mod_chunk(layer, chunk, s), vec(name, off, 8), ALU.mult
                                      ).then_inc(amp_done, 1)

            at.u = 16
            mod_evacuate(dve, at, 16, lambda n, o=0: slice(o, o + n))
            dve.wait_ge(mods_read, 1)
            amplitude(0)
            dve.wait_ge(amp_done, 2)
            norm_scale(dve, "pre0", Xk(T), T, amp(0), shift(0, 0))
            split_low(dve, nxt)
            split_low(dve, nxt)

            def groups(n):
                at.n += n
                at.u += 1
                at.d += 1

            def rope_products(r):
                dve.wait_ge(sem("rope_swapped"), r + 1)
                if r >= 1:
                    dve.wait_ge(sem("rope_done"), 8 * r if r <= 2 else 12 + 2 * r)
                dve.tensor_tensor(TR[:, 0:LAT], XP[:, 0, :], SIN[:, :], ALU.mult).then_inc(sem("rope_sine"), 1)
                dve.tensor_tensor(TQ[:, r % 2, 0:LAT], TQ[:, r % 2, 0:LAT], COS[:, :], ALU.mult).then_inc(sem("rope_cosine"), 1)
                dve.wait_ge(sem("rope_sine"), r + 1)
                dve.wait_ge(sem("rope_cosine"), r + 1)

            groups(2)
            split_low(dve, nxt)
            groups(2)
            dve.wait_ge(rope_loads, 48)
            for j in range(2):
                rope_products(j)
                for e in range(2):
                    rows = slice(64 * e, 64 * e + 64)
                    for half in range(2):
                        to = slice(64 * half, 64 * half + 64)
                        dve.tensor_tensor(KD[to, 2 * j + e, 0:LAT], TQ[rows, j, 0:LAT], TR[rows, 0:LAT], ALU.add
                                          ).then_inc(sem("rope_done"), 1)
                        dve.tensor_copy(KD[to, 2 * j + e, LAT:T], TQ[rows, j, LAT:T]).then_inc(sem("rope_done"), 1)
            for v in range(2):
                split_low(dve, nxt)
                groups(6)

            def maxima(aa, b, hh, near, g):
                p, n = aa % 2, P * (len(near) + 2)
                dve.wait_ge(sem("scored"), aa + 1)
                s = DPF[:, p * 1024 + 768 - n:p * 1024 + 768]
                if near:
                    band = s[:, 0:P * len(near)]
                    first = (near[0] - (b - 1)) * P
                    dve.tensor_tensor(band, band, BAND[:, first:first + P * len(near)], ALU.add).then_inc(sem("masked"), 1)
                    dve.wait_ge(sem("masked"), (aa // 24) * 16 + aa % 24 + 1)
                dve.tensor_reduce(ST[:, p, 0:1], s, AX.X, ALU.max).then_inc(sem("row_max"), 1)
                dve.wait_ge(sem("row_max"), aa + 1)
                head = GROUP * g + hh
                dve.tensor_scalar(ST[:, p, 1:2], ST[:, p, 0:1], ROWS[:, head:head + 1], -1.0, ALU.max, ALU.mult
                                  ).then_inc(sem("shift_ready"), 1)

            def normalise(aa, near):
                p, n = aa % 2, P * (len(near) + 2)
                dve.wait_ge(sem("exponentials"), 2 * aa + 2)
                dve.tensor_tensor(ST[:, p, 4:5], ST[:, p, 2:3], ST[:, p, 3:4], ALU.add).then_inc(sem("denominator"), 1)
                dve.wait_ge(sem("denominator"), 2 * aa + 1)
                dve.reciprocal(ST[:, p, 5:6], ST[:, p, 4:5]).then_inc(sem("denominator"), 1)
                dve.wait_ge(sem("denominator"), 2 * aa + 2)
                dve.tensor_scalar(PB[:, p, 0:n], PB[:, p, 0:n], ST[:, p, 5:6], None, ALU.mult
                                  ).then_inc(sem("probabilities"), 1)

            def mixed_low(q, b, j, g):
                dve.wait_ge(sem("mixed_high"), q + 1)
                dve.tensor_tensor(AL[:, 2 * g + j, b * P:(b + 1) * P], XP[:, 2, 0:P],
                                  AH[:, 2 * g + j, b * P:(b + 1) * P].bitcast(F32), ALU.subtract
                                  ).then_inc(sem("mixed_low"), 1)

            for g in range(KV_HEADS):
                split_low(dve, nxt)
                groups(2)
                groups(2)
                for j in range(2):
                    r = 2 + 2 * g + j
                    rope_products(r)
                    dve.tensor_tensor(QG[:, j, 0:LAT], TQ[:, j, 0:LAT], TR[:, 0:LAT], ALU.add
                                      ).then_inc(sem("rope_done"), 1)
                    dve.tensor_copy(QG[:, j, LAT:T], TQ[:, j, LAT:T]).then_inc(sem("rope_done"), 1)
                work = list(blocks(g))
                maxima(*work[0], g)
                for i, (aa, b, hh, near) in enumerate(work):
                    if i + 1 < len(work):
                        maxima(*work[i + 1], g)
                    normalise(aa, near)
                    if i >= 2 and i % 2 == 0:
                        mixed_low(aa // 2 - 1, work[i - 2][1], work[i - 2][2] // 2, g)
                mixed_low(aa // 2, b, hh // 2, g)
                at.u += 8
                mod_evacuate(dve, at, 8, lambda n, o=0: slice(o + 16 + 8 * g, o + 16 + 8 * g + n))
                split_low(dve, nxt)
            dve.wait_ge(mods_read, 5)
            gating(0)
            amplitude(1)
            gating(1)
            dve.wait_ge(amp_done, 8)

            for t in range(KT):
                split_low(dve, nxt)
                groups(2)
            residual(dve, "post0", T, gate(0))
            norm_scale(dve, "pre1", Xk(T), T, amp(1), shift(0, 3))

            with dve.Fori(0, MLP_STEPS) as it:
                at.enter(it, 28, 16, 32)
                nxt.enter(it, 28, 16, 32)

                def hidden_low(i):
                    t, c = i // 2, i % 2
                    out = slice(384 * c, 384 * c + 384)
                    dve.wait_ge(sem("hid0_high"), it * 16 + (i + 1))
                    dve.tensor_tensor(AL[:, t, out], SQ[:, i % 2, 0:384], AH[:, t, out].bitcast(F32), ALU.subtract
                                      ).then_inc(sem("hid0_low"), 1)

                for t in range(2 * KT):
                    split_low(dve, nxt)
                    for c in range(2):
                        i = 2 * t + c
                        wait_group(dve, at)
                        if t < KT:
                            if i >= 2:
                                dve.wait_ge(sem("hid0_high"), it * 16 + (i - 1))
                            dve.tensor_scalar(TQ[:, i % 2, 0:384], DP[:, bank(at), 0:384], 0.0, None, ALU.max
                                              ).then_inc(bank_free[bank(at)], 1)
                            if i >= 1:
                                hidden_low(i - 1)
                            if i == 15:
                                hidden_low(i)
                        else:
                            k = t - KT
                            if k == 0 and c == 0:
                                dve.wait_ge(sem("y_zero"), KT)
                            y = Y[:, k, 384 * c:384 * c + 384]
                            dve.tensor_tensor(y, DP[:, bank(at), 0:384], y, ALU.add).then_inc(bank_free[bank(at)], 1)
                        at.n += 1
                    at.u += 1
                    at.d += 1
                    if t < 12:
                        at.u += 1
                    if t == 11:
                        mod_evacuate(dve, at, 12, lambda n, o=0: bass.ds(it * 12 + (o + 48), n))
                at.leave(MLP_STEPS)
                nxt.leave(MLP_STEPS)
                nxt.u = at.u + 1
            dve.wait_ge(mods_read, 9)
            for i in (2, 3):
                gating(i)
                amplitude(i)
            dve.wait_ge(amp_done, 16)
            residual(dve, "post1", T, gate(1))
            dve.wait_ge(sem("gate_down_split"), 1)
            dve.tensor_tensor(WDL[:, :], QD[:, :], WDH[:, :].bitcast(F32), ALU.subtract).then_inc(sem("gate_down_split"), 1)
            dve.memset(ATM[:, :, :, :], 0.0).then_inc(sem("mixing_zero"), 1)
            dve.wait_ge(sem("mixing_zero"), 1)
            norm_scale(dve, "pre2", Xk(T), T, amp(2), shift(1, 0))
            dve.wait_ge(sem("gla_loads"), 48)
            CH = T // CHUNK

            def gate_logs(h, d):
                s = 2 * h + d
                dve.wait_ge(sem("gate_logits_made"), s + 1)
                dve.tensor_scalar(B[:, d, :].rearrange("p (c n) -> p c n", n=384), XP[:, 0:2, 0:384],
                                  vec("gate_bias", 2 * h + d), None, ALU.add).then_inc(sem("gate_logits_read"), 1)
                dve.wait_ge(sem("gate_logits_read"), s + 1)
                dve.tensor_scalar(MN[:, d, :], B[:, d, :], 0.0, None, ALU.min).then_inc(sem("gate_min"), 1)
                dve.wait_ge(sem("gate_min"), s + 1)
                dve.scalar_tensor_tensor(B[:, d, :], MN[:, d, :], 2.0, B[:, d, :], ALU.mult, ALU.subtract
                                         ).then_inc(sem("gate_folded"), 1)

            def decays(h, d):
                s = 2 * h + d
                dve.wait_ge(sem("gate_log"), s + 1)
                dve.tensor_tensor(B[:, d, :], MN[:, d, :], B[:, d, :], ALU.subtract).then_inc(sem("log_decay"), 1)
                dve.wait_ge(sem("log_decay"), s + 1)
                if s:
                    dve.wait_ge(sem("decay_exps"), 4 * s)
                for c in range(CH):
                    cols = slice(c * CHUNK, (c + 1) * CHUNK)
                    dve.tensor_tensor_scan(BC[:, cols], ONES[:, 0:CHUNK], B[:, d, cols], 0.0, ALU.mult, ALU.add
                                           ).then_inc(sem("scanned"), 1)
                dve.wait_ge(sem("scanned"), CH * (s + 1))
                last_of = BC[:, :].rearrange("p (c n) -> p c n", n=CHUNK)[:, :, CHUNK - 1:CHUNK]
                dve.tensor_copy(TOT[:, d, :], last_of.rearrange("p c o -> p (c o)")).then_inc(sem("chunk_total"), 1)
                dve.wait_ge(sem("chunk_total"), s + 1)
                tot = TOT[:, d, :].unsqueeze(2).to_broadcast((P, CH, CHUNK))
                bc = BC[:, :].rearrange("p (c n) -> p c n", n=CHUNK)
                bd = B[:, d, :].rearrange("p (c n) -> p c n", n=CHUNK)
                if d == 0:
                    dve.tensor_tensor(bd, tot, bc, ALU.subtract).then_inc(sem("decays_summed"), 1)
                else:
                    dve.tensor_tensor(bd, bc, bd, ALU.subtract).then_inc(sem("end_decay"), 1)
                    dve.wait_ge(sem("end_decay"), h + 1)
                    dve.tensor_tensor(bc, tot, bd, ALU.subtract).then_inc(sem("decays_summed"), 1)
                dve.wait_ge(sem("decay_exps"), 4 * s + 1)
                if s:
                    dve.wait_ge(sem("keys_turned"), s)
                dve.tensor_tensor(KEF[:, :], KEYS[:, :], B[:, d, :], ALU.mult).then_inc(sem("keys_decayed"), 1)
                dve.wait_ge(sem("decay_exps"), 4 * s + 3)
                dve.tensor_tensor(QD[:, :], QD[:, :], QT[:, 0:LAT], ALU.mult)
                dve.tensor_tensor(KI[:, :], KI[:, :], KEYS[:, 0:LAT], ALU.mult).then_inc(sem("queries_decayed"), 1)

            def scan_steps(h, d):
                s = 2 * h + d
                order = SCAN_TILES[d]
                halves = (0, 1) if d == 0 else (1, 0)
                dve.wait_ge(sem("decay_exps"), 4 * s + 4)

                def mask(i):
                    if order[i] >= LAT // P:
                        return
                    j = i - 2
                    n = 4 * s + j
                    dve.wait_ge(sem("mixing_made"), n + 1)
                    if n >= 2:
                        dve.wait_ge(sem("mixed_out_made"), n - 1)
                    dve.copy_predicated(ATM[:, d, j % 2, :], CAUSAL[:, d, :].bitcast(I32), DP[:, 2 + j % 2, 0:P]
                                        ).then_inc(sem("mixing_masked"), 1)

                def state(i):
                    for e, half in enumerate(halves):
                        c = 2 * i + e
                        if c == 11:
                            continue
                        n = 11 * s + c
                        dve.wait_ge(sem("update_made"), n + 1)
                        if n:
                            dve.wait_ge(sem("state_updated"), n)
                        done = 4 * s + max(0, (c - 3) // 2 - 2 + 1)
                        if done:
                            dve.wait_ge(sem("mixed_out_made"), done)
                        out, u = S[:, (c + 1) % 4, :], XP[:, 2 + c % 2, 0:GLA_DV]
                        if c == 0:
                            dve.tensor_copy(out, u).then_inc(sem("state_updated"), 1)
                        else:
                            ch = 2 * order[i] + half
                            dve.scalar_tensor_tensor(out, S[:, c % 4, :], DEC[:, d, ch:ch + 1], u, ALU.mult, ALU.add
                                                     ).then_inc(sem("state_updated"), 1)

                def add_output(i):
                    if d == 0 or order[i] >= LAT // P:
                        return
                    m, n = order[i], 4 * s + i - 2
                    dve.wait_ge(sem("mixed_out_made"), n + 1)
                    o = O[:, :, m * P:(m + 1) * P]
                    dve.tensor_tensor(o, DP[:, i % 2, 0:2 * P].rearrange("p (v n) -> p v n", v=2), o, ALU.add
                                      ).then_inc(sem("mixed_out_read"), 1)

                if d == 1:
                    dve.wait_ge(sem("mixed_out_read"), 8 * h + 4)
                mask(0)
                state(0)
                for i in range(6):
                    if i < 5:
                        mask(i + 1)
                        state(i + 1)
                    add_output(i)

            for h in range(GLA_HEADS):
                split_low(dve, nxt)
                groups(2)
                split_low(dve, nxt)
                groups(2)
                if h:
                    dve.wait_ge(sem("decay_exps"), 8 * h)
                gate_logs(h, 0)
                gate_logs(h, 1)
                for v in range(2):
                    split_low(dve, nxt)
                    groups(6)
                for d in range(2):
                    decays(h, d)
                    scan_steps(h, d)
                dve.wait_ge(sem("out_rstd"), 2 * h + 2)
                for v in range(2):
                    dve.scalar_tensor_tensor(O[:, v, :], O[:, v, :], vec("gla_g", v), TR[:, 0:LAT], ALU.mult, ALU.mult
                                             ).then_inc(sem("out_normed"), 1)
                for v in range(2):
                    split_low(dve, nxt)
                    n = 2 * h + v
                    dve.wait_ge(sem("gla_sigmoid"), n + 1)
                    dve.tensor_tensor(TQ[:, v, 0:LAT], DP[:, bank(at), :], TQ[:, v, 0:LAT], ALU.mult
                                      ).then_inc(bank_free[bank(at)], 1)
                    groups(1)
                    wait_read(dve, at, 1)
                    dve.wait_ge(sem("out_normed"), n + 1)
                    dve.tensor_tensor(O[:, v, :], O[:, v, :], TQ[:, v, 0:LAT], ALU.mult).then_inc(sem("gla_gated"), 1)
                for v in range(2):
                    n = 2 * h + v
                    dve.wait_ge(sem("gla_high"), n + 1)
                    dve.tensor_tensor(AL[:, n, 0:LAT], O[:, v, :], AH[:, n, 0:LAT].bitcast(F32), ALU.subtract
                                      ).then_inc(sem("gla_low"), 1)

            for t in range(KT):
                split_low(dve, nxt)
                groups(1)
            residual(dve, "post2", LAT, gate(2))
            norm_scale(dve, "pre3", Xk(LAT), LAT, amp(3), shift(1, 3))

            with dve.Fori(0, MLP_STEPS) as it:
                at.enter(it, 16, 16, 16)
                nxt.enter(it, 16, 16, 16)

                def hidden_low1(t):
                    dve.wait_ge(sem("hid1_high"), it * 8 + (t + 1))
                    dve.tensor_tensor(AL[:, t, 0:LAT], SQ[:, t % 2, :], AH[:, t, 0:LAT].bitcast(F32), ALU.subtract
                                      ).then_inc(sem("hid1_low"), 1)

                for t in range(2 * KT):
                    split_low(dve, nxt)
                    wait_group(dve, at)
                    if t < KT:
                        if t >= 2:
                            dve.wait_ge(sem("hid1_high"), it * 8 + (t - 1))
                        dve.tensor_scalar(TQ[:, t % 2, 0:LAT], DP[:, bank(at), :], 0.0, None, ALU.max
                                          ).then_inc(bank_free[bank(at)], 1)
                        if t >= 1:
                            hidden_low1(t - 1)
                        if t == KT - 1:
                            hidden_low1(t)
                    else:
                        if t == KT:
                            dve.wait_ge(sem("y_zero"), 2 * KT)
                        y = Y[:, t - KT, 0:LAT]
                        dve.tensor_tensor(y, DP[:, bank(at), :], y, ALU.add).then_inc(bank_free[bank(at)], 1)
                    at.n, at.u, at.d = at.n + 1, at.u + 1, at.d + 1
                at.leave(MLP_STEPS)
                nxt.leave(MLP_STEPS)
            residual(dve, "post3", LAT, gate(3))

            norm_scale(dve, "mix", Xk(LAT), LAT, lambda k, s: vec("mix_gain", k), nil)
            lre, lim = vec("lam_re", 0, 16), vec("lam_im", 0, 16)
            steps = [1]

            def prep(ins):
                ins.then_inc(sem("ssm_prep"), 1)
                steps[0] += 1
                dve.wait_ge(sem("ssm_prep"), steps[0])

            MAGIC = 1.5 * 2.0 ** 23
            dve.wait_ge(sem("ssm_prep"), 1)
            prep(dve.tensor_tensor(PV(1), lre, PV(0), ALU.mult))
            prep(dve.tensor_tensor(PV(3), lim, PV(0), ALU.mult))
            steps[0] += 1
            prep(dve.tensor_scalar(PV(3), PV(3), 1.0 / (2.0 * np.pi), None, ALU.mult))
            prep(dve.tensor_scalar(PV(4), PV(3), MAGIC, MAGIC, ALU.add, ALU.subtract))
            prep(dve.tensor_tensor(PV(3), PV(3), PV(4), ALU.subtract))
            prep(dve.tensor_scalar(PV(4), PV(3), MAGIC, MAGIC, ALU.add, ALU.subtract))
            prep(dve.tensor_tensor(PV(5), PV(3), PV(4), ALU.subtract))
            prep(dve.tensor_scalar(PV(6), PV(3), 0.25, None, ALU.add))
            prep(dve.tensor_scalar(PV(4), PV(6), MAGIC, MAGIC, ALU.add, ALU.subtract))
            prep(dve.tensor_tensor(PV(6), PV(6), PV(4), ALU.subtract))
            for t in range(4):
                split_low(dve, nxt)
                groups(1)

            def maxima2(n, p, b, e):
                w = P * (b + 1)
                dve.wait_ge(sem("scored2"), n + 1)
                if n >= 2:
                    dve.wait_ge(sem("exponentials2"), n - 1)
                dve.scalar_tensor_tensor(SS[:, e, 0:w], XP[:, 2 + e, 0:w], QUERY, BW[:, p % 2, e, 512 - w:512],
                                         ALU.mult, ALU.add).then_inc(sem("bias_used"), 1)
                dve.wait_ge(sem("bias_used"), n + 1)
                dve.tensor_reduce(ST2[:, e, 0:1], SS[:, e, 0:w], AX.X, ALU.max).then_inc(sem("row_max2"), 1)
                dve.wait_ge(sem("row_max2"), n + 1)
                dve.tensor_scalar(ST2[:, e, 1:2], ST2[:, e, 0:1], -1.0, None, ALU.mult).then_inc(sem("shift_ready2"), 1)

            def normalise2(n, b, e):
                dve.wait_ge(sem("exponentials2"), n + 1)
                dve.reciprocal(ST2[:, e, 5:6], ST2[:, e, 2:3]).then_inc(sem("denominator2"), 1)
                dve.wait_ge(sem("denominator2"), n + 1)
                w = P * (b + 1)
                dve.tensor_scalar(PB2[:, e, 0:w], PB2[:, e, 0:w], ST2[:, e, 5:6], None, ALU.mult
                                  ).then_inc(sem("probabilities2"), 1)

            def mixed_low2(q, p, b):
                dve.wait_ge(sem("mixed_high2"), q + 1)
                dve.tensor_tensor(AL[:, p, b * P:(b + 1) * P], XP[:, 1, 0:P], AH[:, p, b * P:(b + 1) * P].bitcast(F32),
                                  ALU.subtract).then_inc(sem("mixed_low2"), 1)

            for p in range(4):
                split_low(dve, nxt)
                groups(1)
                split_low(dve, nxt)
                groups(1)
                for i, (out, gain) in enumerate([(QN, "q_gain"), (KN, "k_gain")]):
                    dve.wait_ge(sem("head_rstd"), 2 * p + i + 1)
                    wait_read(dve, at, 2 - i)
                    dve.scalar_tensor_tensor(out[:, :], QR[:, i, :], vec(gain), RS[:, i, :], ALU.mult, ALU.mult
                                             ).then_inc(sem("head_normed"), 1)
                split_low(dve, nxt)
                groups(4)
                dve.wait_ge(sem(f"bias_landed{p % 2}"), 16 * (p // 2 + 1))
                dve.memset(BW[0:64, p % 2, :, 448:512], NEG).then_inc(sem("bias_masked"), 1)
                dve.wait_ge(sem("bias_masked"), p + 1)
                work = [(p * 8 + 2 * b + e, b, e) for b in range(4) for e in range(2)]
                maxima2(work[0][0], p, 0, 0)
                for i, (n, b, e) in enumerate(work):
                    if i + 1 < len(work):
                        n2, b2, e2 = work[i + 1]
                        maxima2(n2, p, b2, e2)
                    normalise2(n, b, e)
                    if i >= 2 and i % 2 == 0:
                        mixed_low2(n // 2 - 1, p, b - 1)
                mixed_low2(n // 2, p, b)

            dve.wait_ge(sem("ssm_trig0"), 2)
            prep(dve.tensor_tensor(PV(8), PV(2), PV(8), ALU.mult))
            prep(dve.tensor_tensor(PV(7), PV(2), PV(7), ALU.mult))
            prep(dve.tensor_scalar(PV(8), PV(8), -1.0, None, ALU.add))
            prep(dve.tensor_tensor(PV(9), lre, lre, ALU.mult))
            prep(dve.tensor_tensor(PV(10), lim, lim, ALU.mult))
            prep(dve.tensor_tensor(PV(9), PV(9), PV(10), ALU.add))
            prep(dve.reciprocal(PV(10), PV(9)))
            prep(dve.tensor_tensor(PV(4), PV(8), lre, ALU.mult))
            prep(dve.tensor_tensor(PV(5), PV(7), lim, ALU.mult))
            prep(dve.tensor_tensor(PV(4), PV(4), PV(5), ALU.add))
            prep(dve.tensor_tensor(PV(11), PV(4), PV(10), ALU.mult))
            prep(dve.tensor_tensor(PV(4), PV(7), lre, ALU.mult))
            prep(dve.tensor_tensor(PV(5), PV(8), lim, ALU.mult))
            prep(dve.tensor_tensor(PV(4), PV(4), PV(5), ALU.subtract))
            prep(dve.tensor_tensor(PV(12), PV(4), PV(10), ALU.mult))
            assert steps[0] == SSM_PREP

            def ssm_y(t):
                dve.wait_ge(sem("ssm_out"), 4 * (t + 1))
                dve.scalar_tensor_tensor(UT(t), UT(t), vec("ssm_d", t), XP[:, 2 + t % 2, :].rearrange("p (a n) -> p a n", a=2),
                                         ALU.mult, ALU.add).then_inc(sem("ssm_y"), 1)

            def turned(i):
                dve.wait_ge(sem("ssm_driven"), i + 1)
                dve.wait_ge(sem("ssm_trig"), 2 * i + 2)
                if i:
                    dve.wait_ge(sem("ssm_products"), 4 * i)
                    dve.wait_ge(sem("ssm_out"), i)
                sin, cos = TRIG[:, i % 2, 0, :], TRIG[:, i % 2, 1, :]
                for k, (w, q) in enumerate([(0, cos), (1, sin), (1, cos), (0, sin)]):
                    dve.tensor_tensor(PR[:, k, :], XP[:, w, :], q, ALU.mult).then_inc(sem("ssm_turned"), 1)
                dve.wait_ge(sem("ssm_turned"), 4 * i + 4)
                for z, op in ((0, ALU.add), (1, ALU.subtract)):
                    dve.tensor_tensor(TQ[:, z, 0:LAT], PR[:, 2 * z, :], PR[:, 2 * z + 1, :], op).then_inc(sem("ssm_v"), 1)
                dve.wait_ge(sem("ssm_v"), 2 * i + 2)
                for z in range(2):
                    dve.tensor_tensor_scan(TQ[:, z, 0:LAT], PV(2)[:, i:i + 1].to_broadcast((P, LAT)), TQ[:, z, 0:LAT], 0.0,
                                           ALU.mult, ALU.add).then_inc(sem("ssm_z"), 1)
                dve.wait_ge(sem("ssm_z"), 2 * i + 2)
                for k, (z, q) in enumerate([(0, cos), (1, sin), (0, sin), (1, cos)]):
                    dve.tensor_tensor(PR[:, k, :], TQ[:, z, 0:LAT], q, ALU.mult).then_inc(sem("ssm_products"), 1)

            for i in range(16):
                split_low(dve, nxt)
                turned(i)
                groups(1)
                if i % 4 == 0 and i:
                    ssm_y(i // 4 - 1)
            ssm_y(3)
            for t in range(4):
                dve.wait_ge(sem("ssm_out"), 16)
                pr = PR[:, t, :].rearrange("p (a n) -> p a n", a=2)
                dve.wait_ge(sem("ssm_y"), t + 1)
                dve.tensor_tensor(pr, UT(t), UT(t), ALU.mult).then_inc(sem("gelu_a"), 1)
                dve.wait_ge(sem("gelu_a"), 2 * t + 1)
                dve.tensor_scalar(PR[:, t, :], PR[:, t, :], 0.044715, 1.0, ALU.mult, ALU.add).then_inc(sem("gelu_a"), 1)
                dve.wait_ge(sem("gelu_a"), 2 * t + 2)
                dve.tensor_tensor(pr, pr, UT(t), ALU.mult).then_inc(sem("gelu_inner"), 1)
            for t in range(4):
                dve.wait_ge(sem("gelu_sigmoid"), t + 1)
                pr = PR[:, t, :].rearrange("p (a n) -> p a n", a=2)
                dve.tensor_tensor(UT(t), UT(t), pr, ALU.mult).then_inc(sem("z_made"), 1)
            for t in range(4):
                dve.wait_ge(sem("z_high"), t + 1)
                dve.tensor_tensor(AL[:, 2 * t:2 * t + 2, LAT:T], UT(t), AH[:, 2 * t:2 * t + 2, LAT:T].bitcast(F32),
                                  ALU.subtract).then_inc(sem("z_low"), 1)
            for t in range(2):
                split_low(dve, nxt)
                for jj in range(2):
                    j = 2 * t + jj
                    wait_read(dve, at, 0)
                    pr = PR[:, j, :].rearrange("p (a n) -> p a n", a=2)
                    dve.tensor_tensor(pr, pr, UT(j), ALU.mult).then_inc(sem("ssm_gated"), 1)
                    at.n += 1
                at.u, at.d = at.u + 1, at.d + 1
            for j in range(4):
                dve.wait_ge(sem("ssm_high"), j + 1)
                dve.tensor_tensor(AL[:, 4 + j, 0:LAT], PR[:, j, :], AH[:, 4 + j, 0:LAT].bitcast(F32), ALU.subtract
                                  ).then_inc(sem("ssm_low"), 1)

            for t in range(KT):
                split_low(dve, nxt)
                if t >= 1:
                    dve.wait_ge(sem("merged_low"), t)
                for half in range(2):
                    wait_group(dve, at)
                    out = TQ[:, t % 2, 0:LAT] if half == 0 else TR[:, 0:LAT]
                    dve.tensor_tensor(out, DP[:, bank(at), :], GATES[:, 8 * half + t, :], ALU.mult
                                      ).then_inc(bank_free[bank(at)], 1)
                    at.n += 1
                at.u, at.d = at.u + 1, at.d + 1
                wait_read(dve, at, 1)
                wait_read(dve, at, 2)
                dve.tensor_tensor(TQ[:, t % 2, 0:LAT], TQ[:, t % 2, 0:LAT], TR[:, 0:LAT], ALU.add).then_inc(sem("merged"), 1)
                dve.wait_ge(sem("merged_high"), t + 1)
                dve.tensor_tensor(HL[:, t, 0:LAT], TQ[:, t % 2, 0:LAT], HH[:, t, 0:LAT].bitcast(F32), ALU.subtract
                                  ).then_inc(sem("merged_low"), 1)

            def add_to_x(t):
                dve.tensor_tensor(X[:, t, 0:LAT], DP[:, bank(at), :], X[:, t, 0:LAT], ALU.add
                                  ).then_inc(bank_free[bank(at)], 1)

            for t in range(KT):
                split_low(dve, nxt)
                wait_group(dve, at)
                add_to_x(t)
                at.n, at.u, at.d = at.n + 1, at.u + 1, at.d + 1
            dve.wait_ge(sem("router_split"), 1)
            dve.tensor_tensor(RWL[:, :], RW[:, :], RWH[:, :].bitcast(F32), ALU.subtract).then_inc(sem("router_split"), 1)
            norm_scale(dve, "ffn", Xk(LAT), LAT, lambda k, s: vec("ffn_gain", k), nil)

            steps = [0]

            def route(ins):
                ins.then_inc(sem("route"), 1)
                steps[0] += 1
                dve.wait_ge(sem("route"), steps[0])

            def r4(i):
                return RT[:, i, 0:16].rearrange("p (m g) -> p m g", g=4)

            def r1(i):
                return RT[:, i, 0:4].unsqueeze(2)

            def over4(i):
                return RT[:, i, 0:4].unsqueeze(2).to_broadcast((P, 4, 4))

            pref = PREF[:, :].unsqueeze(1).to_broadcast((P, 4, 4))

            def first_of(src, top, out):
                route(dve.tensor_tensor(r4(out), r4(src), over4(top), ALU.is_ge))
                route(dve.tensor_tensor(r4(out), r4(out), pref, ALU.mult))
                route(dve.tensor_reduce(r1(13), r4(out), AX.X, ALU.max))
                route(dve.tensor_tensor(r4(out), r4(out), over4(13), ALU.is_ge))

            dve.wait_ge(sem("router_made"), 1)
            logits = XP[:, 0, 0:80].rearrange("p (m n) -> p m n", n=20)
            bias_g = ROWS[:, 16:20].unsqueeze(1).to_broadcast((P, 4, 4))
            bias_e = ROWS[:, 20:36].unsqueeze(1).to_broadcast((P, 4, 16))
            for i in range(4):
                ins = dve.memset(PREF[:, i:i + 1], float(4 - i))
            ins.then_inc(sem("preference"), 1)
            dve.wait_ge(sem("preference"), 1)
            dve.tensor_tensor(EL[:, :, :], logits[:, :, 4:20], bias_e, ALU.add).then_inc(sem("expert_logits"), 1)
            route(dve.tensor_tensor(r4(0), logits[:, :, 0:4], bias_g, ALU.add))
            route(dve.tensor_reduce(r1(2), r4(0), AX.X, ALU.max))
            route(dve.tensor_tensor(r4(1), r4(0), over4(2), ALU.subtract))
            first_of(0, 2, 3)
            dve.wait_ge(sem("expert_logits"), 1)
            elg = EL[:, :, :].rearrange("p m (g e) -> p (m g) e", g=4)
            ohg = RT[:, 3, 0:16].unsqueeze(2).to_broadcast((P, 16, 4))
            route(dve.tensor_tensor(elg, elg, ohg, ALU.mult))
            el = EL[:, :, :].rearrange("p m (g e) -> p m g e", g=4)
            route(dve.tensor_tensor(r4(4), el[:, :, 0, :], el[:, :, 1, :], ALU.add))
            route(dve.tensor_tensor(r4(5), el[:, :, 2, :], el[:, :, 3, :], ALU.add))
            route(dve.tensor_tensor(r4(4), r4(4), r4(5), ALU.add))
            steps_before = steps[0]
            assert steps_before == 11
            dve.tensor_reduce(r1(7), r4(4), AX.X, ALU.max).then_inc(sem("route_top"), 1)
            dve.wait_ge(sem("route_top"), 1)
            route(dve.tensor_tensor(r4(6), r4(4), over4(7), ALU.subtract))
            first_of(4, 7, 8)
            route(dve.scalar_tensor_tensor(RT[:, 9, 0:16], RT[:, 8, 0:16], NEG, RT[:, 4, 0:16], ALU.mult, ALU.add))
            route(dve.tensor_reduce(r1(10), r4(9), AX.X, ALU.max))
            first_of(9, 10, 11)
            route(dve.tensor_tensor(r4(8), r4(8), r4(11), ALU.add))
            dve.wait_ge(sem("route_exp"), 2)
            route(dve.tensor_reduce(r1(2), r4(1), AX.X, ALU.add))
            route(dve.tensor_tensor(r4(6), r4(6), r4(8), ALU.mult))
            route(dve.tensor_reduce(r1(7), r4(6), AX.X, ALU.add))
            route(dve.tensor_tensor(r1(7), r1(7), r1(2), ALU.mult))
            route(dve.reciprocal(r1(10), r1(7)))
            route(dve.tensor_tensor(r4(6), r4(6), over4(10), ALU.mult))
            gts = GTS[:, :, :].rearrange("p m (g e) -> p m g e", g=4)
            for g in range(4):
                ins = dve.tensor_tensor(gts[:, :, g, :], r4(6), r4(3)[:, :, g:g + 1].to_broadcast((P, 4, 4)), ALU.mult)
            ins.then_inc(sem("expert_low"), 1)

            with dve.Fori(0, EXPERT_GROUPS) as g:
                at.enter(g, 24, 24, 24)
                nxt.enter(g, 24, 24, 24)
                for e in range(EXPERTS_PER):
                    for j in range(2):
                        f = 2 * e + j
                        split_low(dve, nxt)
                        dve.wait_ge(sem("expert_sigmoid"), g * 8 + (f + 1))
                        dve.tensor_tensor(SG[:, j, :], DP[:, bank(at), :], SG[:, j, :], ALU.mult
                                          ).then_inc(bank_free[bank(at)], 1)
                        at.n, at.u, at.d = at.n + 1, at.u + 1, at.d + 1
                        wait_read(dve, at, 1)
                        dve.wait_ge(sem("gate_row_read"), g * 4 + (e + 2))
                        dve.tensor_tensor(SG[:, j, :], SG[:, j, :], GB[:, e % 2, :], ALU.mult).then_inc(sem("expert_weighed"), 1)
                        split_low(dve, nxt)
                        wait_group(dve, at)
                        dve.wait_ge(sem("expert_weighed"), g * 8 + (f + 1))
                        dve.tensor_tensor(SG[:, j, :], DP[:, bank(at), :], SG[:, j, :], ALU.mult
                                          ).then_inc(bank_free[bank(at)], 1)
                        at.n, at.u, at.d = at.n + 1, at.u + 1, at.d + 1
                        wait_read(dve, at, 1)
                        dve.wait_ge(sem("expert_high"), g * 8 + (f + 1))
                        dve.tensor_tensor(AL[:, f, 0:LAT], SG[:, j, :], AH[:, f, 0:LAT].bitcast(F32), ALU.subtract
                                          ).then_inc(sem("expert_low"), 1)
                for t in range(KT):
                    split_low(dve, nxt)
                    wait_group(dve, at)
                    add_to_x(t)
                    at.n, at.u, at.d = at.n + 1, at.u + 1, at.d + 1
                at.leave(EXPERT_GROUPS)
                nxt.leave(EXPERT_GROUPS)



def feature_major(v):
    return np.ascontiguousarray(v.reshape(-1, P).T)


def kernel(**inputs):
    import concourse.bacc as _bacc
    from concourse.bass_utils import run_bass_kernel_spmd as _run

    x = {k: np.ascontiguousarray(v) for k, v in inputs.items()}
    w = {
        "w_mod": x["w_mod"], "attn_w_qkv": x["attn_w_qkv"], "attn_w_o": x["attn_w_o"], "w_mlp_in": x["w_mlp_in"],
        "w_mlp_out": x["w_mlp_out"], "gla_w_in": x["gla_w_in"], "gla_w_o": x["gla_w_o"], "w_in_2": x["w_in_2"],
        "w_branch_2": x["w_branch_2"], "w_out_2": x["w_out_2"], "w_e_gate_2": x["w_e_gate_2"][0],
        "w_e_up_2": x["w_e_up_2"][0], "w_e_down_2": x["w_e_down_2"].reshape(1, -1, D),
    }
    tiles = schedule()
    stream = np.zeros((len(tiles), P, TILE), np.float32)
    for i, (_, name, which, row, col) in enumerate(tiles):
        if name == "w_glu_2":
            two = x[name][0][:, col:col + 2 * P].reshape(4, P, 2, P)
            stream[i] = two.transpose(1, 2, 0, 3).reshape(P, TILE)
        else:
            stream[i] = w[name][which, row:row + D, col:col + P].reshape(KT, P, P).transpose(1, 0, 2).reshape(P, TILE)

    gla_bias = x["gla_gate_bias"][0].reshape(2, 4, P).transpose(2, 1, 0).reshape(P, 8)
    vec = np.concatenate([
        feature_major(x["c"]), feature_major(x["c_ctx"]), feature_major(x["b_mod"]), feature_major(x["g_pre_mix"]),
        feature_major(x["g_post_mix"]), feature_major(x["g_pre_mlp"]), feature_major(x["g_post_mlp"]), gla_bias,
        feature_major(x["gla_g_norm"]), feature_major(x["mix_norm_gain_2"]), feature_major(x["b_gate_2"]),
        np.tile(x["q_gain_2"][0], 2)[:, None], np.tile(x["k_gain_2"][0], 2)[:, None], feature_major(x["ssm_d_2"]),
        feature_major(x["b_glu_2"]), feature_major(x["ffn_norm_gain_2"]), feature_major(x["ssm_lambda_re_2"]),
        feature_major(x["ssm_lambda_im_2"]), feature_major(np.repeat(x["ssm_log_step_2"][0], HD)),
    ], axis=1)
    row = np.concatenate([x["attn_sink"][0], x["group_bias_2"][0], x["expert_bias_2"][0]])
    row = np.ascontiguousarray(np.broadcast_to(row[None], (P, NROW)))

    i = np.arange(P)
    const = np.concatenate([np.eye(P), np.ones((P, P)), i[:, None] == (i ^ 16)[None], (i[:, None] // HD) == (i[None] // HD)],
                           axis=1).astype(np.float32)
    pos = np.arange(LAT)
    inv = np.float32(10000.0) ** (-np.arange(16, dtype=np.float32) * np.float32(2.0) / np.float32(32))
    r = i % HD
    where = np.where((r // 32 == 0)[:, None], (pos // HD)[None], (pos % HD)[None]).astype(np.float32)
    angle = where * inv[r % 16][:, None]
    sign = np.where(r % 32 < 16, -1.0, 1.0)[:, None]
    j = np.arange(3 * P)
    band = np.where(np.abs(j[None] - P - i[:, None]) <= P, 0.0, NEG)
    rope = np.concatenate([np.cos(angle), sign * np.sin(angle), band], axis=1).astype(np.float32)
    same = (i[:, None] // CHUNK) == (i[None] // CHUNK)
    causal = np.stack([same & (i[:, None] <= i[None]), same & (i[:, None] >= i[None])], axis=1).astype(np.float32)
    gla_down = np.zeros((P, KT, 64), np.float32)
    gla_up = np.zeros((64, 512), np.float32)
    for d in range(2):
        gla_down[:, :, 32 * d:32 * d + 16] = x["gla_w_gate_down"][0, d].reshape(KT, P, 16).transpose(1, 0, 2)
        gla_up[32 * d:32 * d + 16] = x["gla_w_gate_up"][0, d]
    c = np.arange(LAT)
    distance = np.clip(i[:, None] - c[None] + 384, -63, 256) + 63
    rel = x["rel_bias_2"][0][:, distance].reshape(4, 2, P, LAT).transpose(0, 2, 1, 3)
    ssm = np.zeros((16, P, 4, P), np.float32)
    for t in range(16):
        for g in range(2):
            group, at = 2 * t + g, 32 * (t % 4) + 16 * g
            states = slice(HD * g, HD * g + HD)
            for z, (b, cc) in enumerate([("ssm_b_re_2", "ssm_c_re_2"), ("ssm_b_im_2", "ssm_c_im_2")]):
                ssm[t, at:at + 16, z, states] = x[b][0, group].T
                ssm[t, states, 2 + z, at:at + 16] = x[cc][0, group].T
    router = np.concatenate([x["w_group_router_2"][0], x["w_expert_router_2"][0]], axis=1)
    select = np.zeros((P, 4, P), np.float32)
    for e in range(4):
        select[e, e] = 1.0
    both = np.concatenate([x["x"][0], x["ctx"][0]], axis=0)
    arrays = {
        "stream": stream, "vec": np.ascontiguousarray(vec), "row": row, "const": const, "rope": rope,
        "causal": causal, "gla_down": gla_down.reshape(P, 512), "gla_up": gla_up,
        "rel": np.ascontiguousarray(rel), "ssm": ssm, "select": select,
        "iota": np.ascontiguousarray(np.broadcast_to(np.arange(LAT, dtype=np.float32)[None], (P, LAT))),
        "router": np.ascontiguousarray(router.reshape(KT, P, 20).transpose(1, 0, 2).reshape(P, KT * 20)),
        "x": np.ascontiguousarray(both.T.reshape(KT, P, T).transpose(1, 0, 2)),
    }
    nc = _bacc.Bacc("TRN2", target_bir_lowering=False, num_devices=1, dynamic_dma_scratch_size=1024)
    args = {name: nc.dram_tensor("in_" + name, v.shape, mybir.dt.from_np(v.dtype), kind="ExternalInput").ap()
            for name, v in arrays.items()}
    out = nc.dram_tensor("out", (P, KT, LAT), F32, kind="ExternalOutput").ap()
    backbone_kernel(nc, args, out)
    result = _run(nc, [{"in_" + k: v for k, v in arrays.items()}], core_ids=[0]).results[0]["out"]
    return np.ascontiguousarray(result.transpose(2, 1, 0).reshape(1, LAT, D))
```

```python
from contextlib import ExitStack

import concourse.bass as bass
import numpy as np
from concourse import mybir

F32 = mybir.dt.float32
FR = mybir.dt.float32r
I32 = mybir.dt.int32
ALU = mybir.AluOpType
ACT = mybir.ActivationFunctionType
AX = mybir.AxisListType

P = 128
D = 1024
KT = D // P
LAT, CTX = 512, 256
T = LAT + CTX
EPS = 1e-6
NEG = -1e30
HD = 64
HEADS, KV_HEADS, GROUP = 16, 4, 4
MLP_STEPS = 4
GLA_HEADS, GLA_DV = 4, 256
CHUNK = 64
TILE = KT * P
RING, WRING, BANKS = 4, 2, 4
EXPERT_GROUPS, EXPERTS_PER = 4, 4

VEC = {}
_at = 0
for _name, _n in [("b_mod", 96), ("g_pre_mix", 16), ("g_post_mix", 16), ("g_pre_mlp", 16),
                  ("g_post_mlp", 16), ("gate_bias", 8), ("gla_g", 2), ("mix_gain", 8), ("b_gate", 16), ("q_gain", 1),
                  ("k_gain", 1), ("ssm_d", 4), ("b_glu", 4), ("ffn_gain", 8), ("lam_re", 16), ("lam_im", 16),
                  ("log_step", 16)]:
    VEC[_name] = (_at, _n)
    _at += _n
NVEC = _at
ROW = {"sink": (0, 16), "group_bias": (16, 4), "expert_bias": (20, 16)}
NROW = 36


def schedule():
    tiles = []

    def mod(layer, t):
        tiles.append((False, "w_mod", layer, 0, t * P))

    def dense(name, col, which=0, row=0):
        tiles.append((True, name, which, row, col))

    for t in range(16):
        mod(0, t)
    for t in (8, 9, 0, 1, 2, 3, 4, 5, 6, 7, 10, 11):
        dense("attn_w_qkv", t * P)
    for t in range(32):
        mod(0, 16 + t)
    for t in range(KT):
        dense("attn_w_o", t * P)
    for i in range(MLP_STEPS):
        for t in range(16):
            if t < 8:
                dense("w_mlp_in", (8 * i + t) * P)
            else:
                dense("w_mlp_out", (t - 8) * P, row=i * D)
            if t < 12:
                mod(1, 12 * i + t)
    for h in range(GLA_HEADS):
        for col in (h * P, 512 + h * P, D + h * GLA_DV, D + h * GLA_DV + P, 2 * D + h * GLA_DV, 2 * D + h * GLA_DV + P):
            dense("gla_w_in", col)
    for t in range(KT):
        dense("gla_w_o", t * P)
    for i in range(MLP_STEPS):
        for t in range(KT):
            dense("w_mlp_in", (8 * i + t) * P, 1)
        for t in range(KT):
            dense("w_mlp_out", t * P, 1, i * D)
    for t in range(4):
        dense("w_in_2", 1536 + t * P)
    for t in range(4):
        dense("w_in_2", t * P)
        dense("w_in_2", 512 + t * P)
        if t % 2 == 0:
            dense("w_in_2", 1024 + t * P)
            dense("w_in_2", 1024 + (t + 1) * P)
    for t in range(16):
        dense("w_in_2", 2048 + t * P)
    for t in range(2):
        dense("w_glu_2", 2 * t * P)
    for t in range(KT):
        dense("w_branch_2", t * P)
    for t in range(KT):
        dense("w_out_2", t * P)
    for g in range(EXPERT_GROUPS):
        for e in range(EXPERTS_PER):
            for t in range(2):
                dense("w_e_gate_2", t * P, EXPERTS_PER * g + e)
                dense("w_e_up_2", t * P, EXPERTS_PER * g + e)
        for t in range(KT):
            dense("w_e_down_2", t * P, 0, g * D)
    return tiles


class At:

    def __init__(self, kinds):
        self.kinds = kinds
        self.u = self.d = self.n = 0
        self.it = None
        self.per = (0, 0, 0)

    def enter(self, it, u, d, n):
        self.it, self.per = it, (u, d, n)

    def leave(self, trips):
        self.u += (trips - 1) * self.per[0]
        self.d += (trips - 1) * self.per[1]
        self.n += (trips - 1) * self.per[2]
        self.it, self.per = None, (0, 0, 0)

    def next_dense(self):
        self.u += 1
        self.d += 1
        self.to_dense()

    def to_dense(self):
        while self.u < len(self.kinds) and not self.kinds[self.u]:
            self.u += 1

    def _times(self, static, per, mod):
        if self.it is None or per == 0:
            return static
        assert per % mod == 0
        return self.it * (per // mod) + static

    def tile(self, add=1):
        return self._times(self.u // RING + add, self.per[0], RING)

    def landed(self):
        if self.it is None:
            return 16 * (self.u // RING + 1)
        return self.it * (16 * (self.per[0] // RING)) + 16 * (self.u // RING + 1)

    def dense(self, add):
        return self._times(self.d + add, self.per[1], 1)

    def group(self, add=1):
        return self._times(self.n + add, self.per[2], 1)

    def bank_uses(self):
        return self._times(self.n // BANKS, self.per[2], BANKS)


def parts_of(tokens):
    return [(0, LAT, 0), (LAT, T, 1)] if tokens == T else [(0, LAT, 0)]


def cuts_of(tokens):
    return [(0, 384), (384, 768)] if tokens == T else [(0, 512)]


def backbone_kernel(nc, a, out_d):
    ctx = ExitStack()
    kinds = [t[0] for t in schedule()]
    with ctx:
        sem_cache = {}

        def sem(name):
            if name not in sem_cache:
                sem_cache[name] = ctx.enter_context(nc.semaphore(name))
            return sem_cache[name]

        def sb(stack, name, shape, dt=F32):
            return stack.enter_context(nc.sbuf_tensor(name, shape, dt))

        X = sb(ctx, "X", [P, KT, T])
        HH = sb(ctx, "HH", [P, KT, T], FR)
        HL = sb(ctx, "HL", [P, KT, T], FR)
        AH = sb(ctx, "AH", [P, KT, T], FR)
        AL = sb(ctx, "AL", [P, KT, T], FR)
        RAW = sb(ctx, "RAW", [P, RING, TILE])
        WH = sb(ctx, "WH", [P, WRING, TILE], FR)
        WL = sb(ctx, "WL", [P, WRING, TILE], FR)
        TQ = sb(ctx, "TQ", [P, 2, T])
        TR = sb(ctx, "TR", [P, T])
        VECS = sb(ctx, "VECS", [P, NVEC])
        ROWS = sb(ctx, "ROWS", [P, NROW])
        CONST = sb(ctx, "CONST", [P, 4 * P])
        MOD = sb(ctx, "MOD", [P, 96, 2])
        MODT = sb(ctx, "MODT", [P, 16, 2])
        AMP = sb(ctx, "AMP", [P, 4, KT, 2])
        GATE = sb(ctx, "GATE", [P, 4, KT, 2])
        EPSV = sb(ctx, "EPSV", [P, 1])
        QUARTER = sb(ctx, "QUARTER", [P, 1])
        SSMP = sb(ctx, "SSMP", [P, 13, 16])
        NIL = sb(ctx, "NIL", [P, 1])
        IDENT, ONES, SWAP, HALVES = (CONST[:, i * P:(i + 1) * P] for i in range(4))

        def vec(name, i=0, n=1):
            at = VEC[name][0] + i
            return VECS[:, at:at + n]

        with ExitStack() as s1:
            KDH = sb(s1, "KDH", [P, KV_HEADS, T], FR)
            KDL = sb(s1, "KDL", [P, KV_HEADS, T], FR)
            VHL = sb(s1, "VHL", [P, T // P, KV_HEADS, 2 * HD], FR)
            COND = sb(s1, "COND", [P, 2, D])
            MPROD = sb(s1, "MPROD", [P, D])
            COS = sb(s1, "COS", [P, LAT])
            SIN = sb(s1, "SIN", [P, LAT])
            BAND = sb(s1, "BAND", [P, 3 * P])
            BANDF = sb(s1, "BANDF", [P, 2, P], FR)
            IDF = sb(s1, "IDF", [P, P], FR)
            ST = sb(s1, "ST", [P, 2, 5, GROUP])
            OS = sb(s1, "OS", [P, GROUP * HD])
        with ExitStack() as s3:
            QT = sb(s3, "QT", [P, T])
            KEYS = sb(s3, "KEYS", [P, T])
            VT = sb(s3, "VT", [P, T // P, GLA_DV])
            B = sb(s3, "B", [P, 2, T])
            BC = sb(s3, "BC", [P, T])
            QD = sb(s3, "QD", [P, 2, LAT])
            KI = sb(s3, "KI", [P, 2, LAT])
            KEF = sb(s3, "KEF", [P, 2, T])
            KE = sb(s3, "KE", [P, T // P, P])
            O = sb(s3, "O", [P, 2, LAT])
            S = sb(s3, "S", [P, 4, GLA_DV])
            ATM = sb(s3, "ATM", [P, 2, 2, P])
            LOW = sb(s3, "LOW", [64, T])
            WU = sb(s3, "WU", [64, 512])
            CAUSAL = sb(s3, "CAUSAL", [P, 2, P])
            TOT = sb(s3, "TOT", [P, 2, T // CHUNK])
            DEC = sb(s3, "DEC", [P, 2, T // CHUNK])
        with ExitStack() as s4:
            QN = sb(s4, "QN", [P, LAT])
            KN = sb(s4, "KN", [P, LAT])
            V2 = sb(s4, "V2", [P, LAT // P, 2 * P])
            SS = sb(s4, "SS", [P, 2, LAT])
            PB2 = sb(s4, "PB2", [P, 2, LAT])
            PTS2 = sb(s4, "PTS2", [P, 2, 4, 2 * P])
            SQ2 = sb(s4, "SQ2", [P, 2, LAT])
            QR = sb(s4, "QR", [P, 2, LAT])
            RS = sb(s4, "RS", [P, 2, LAT])
            BW = sb(s4, "BW", [P, 2, 2, LAT])
            ST2 = sb(s4, "ST2", [P, 2, 8])
        with ExitStack() as s5:
            GATES = sb(s5, "GATES", [P, 16, LAT])
            TRIG = sb(s5, "TRIG", [P, 2, 2, LAT])
            PR = sb(s5, "PR", [P, 4, LAT])
            MATS = sb(s5, "MATS", [P, 2, 4, P])
            TURN = sb(s5, "TURN", [P, LAT])
            IOTA = sb(s5, "IOTA", [P, LAT])
        with ExitStack() as s6:
            RW = sb(s6, "RW", [P, KT * 20])
            RWH = sb(s6, "RWH", [P, KT * 20], FR)
            RWL = sb(s6, "RWL", [P, KT * 20], FR)
            SEL = sb(s6, "SEL", [P, 4, P])
            GT = sb(s6, "GT", [P, 4 * LAT])
            GTS = sb(s6, "GTS", [P, 4, 16])
            GB = sb(s6, "GB", [P, 2, LAT])
            SG = sb(s6, "SG", [P, 2, LAT])
            RT = sb(s6, "RT", [P, 14, 16])
            EL = sb(s6, "EL", [P, 4, 16])
            PREF = sb(s6, "PREF", [P, 4])

        def PV(i):
            return SSMP[:, i, :]

        def UT(t):
            return X[:, 2 * t:2 * t + 2, LAT:T]

        def CM(i):
            return TQ[:, i // 2, LAT + P * (i % 2):LAT + P * (i % 2) + P]

        def nil(k, s):
            return NIL[:, 0:1]

        TWO_PI = 6.283185
        SSM_PREP = 28
        STEP_FILL, SCAN_FILL, HEAD_FILL = 1, 2, 12
        MN = TQ
        SCAN_TILES = [[4, 5, 0, 1, 2, 3], [5, 4, 3, 2, 1, 0]]
        Y = sb(ctx, "Y", [P, KT, T])

        SQ = sb(ctx, "SQ", [P, 2, 512])

        DP = ctx.enter_context(nc.psum_tensor("DP", [P, BANKS, 512], F32))
        XP = ctx.enter_context(nc.psum_tensor("XP", [P, 4, 512], F32))
        XPF = XP[:, :, :].rearrange("p b n -> p (b n)")
        DPF = DP[:, :, :].rearrange("p b n -> p (b n)")
        WDH, WDL = (x[:, 0:2, LAT:T] for x in (AH, AL))
        PTH, PTL = (x[:, 0:2, 0:5 * P].rearrange("p b (k n) -> p b k n", n=P) for x in (HH, HL))
        PB = TQ

        raw_full = [sem(f"weight_landed{i}") for i in range(RING)]
        raw_done = [sem(f"weight_taken{i}") for i in range(RING)]
        hi_done = sem("weight_high")
        mm_done = sem("group_written")
        bank_free = [sem(f"bank_read{i}") for i in range(BANKS)]
        loads = sem("small_loads")
        rope_loads = sem("rope_loads")
        cond_done = sem("cond_done")
        mods_read = sem("modulation_read")
        amp_done = sem("amplitude_ready")
        NLOADS = 3
        QUERY = HD ** -0.5
        AMP_NORMS = [(0, 1, "g_pre_mix", 0), (0, 4, "g_pre_mlp", 0), (1, 1, "g_pre_mix", 8), (1, 4, "g_pre_mlp", 8)]
        GATE_NORMS = [(0, 2, "g_post_mix", 0), (0, 5, "g_post_mlp", 0), (1, 2, "g_post_mix", 8), (1, 5, "g_post_mlp", 8)]

        def mod_chunk(layer, chunk, s):
            return MOD[:, layer * 48 + chunk * 8:layer * 48 + chunk * 8 + 8, s]

        def shift(layer, chunk):
            return lambda k, s: MOD[:, layer * 48 + chunk * 8 + k, s:s + 1]

        def amp(i):
            return lambda k, s: AMP[:, i, k, s:s + 1]

        def gate(i):
            return lambda k, s: GATE[:, i, k, s:s + 1]

        ALL_GROUPS = (2 * 2 + 6) + 4 * 4 + 16 + 4 * 32 + 4 * (4 + 6 + 2) + 8 + 64 + 4 + 4 * 2 + 2 * 4 + 16 + 4 + 16 + 8 + 4 * 24

        def bank(at):
            return at.n % BANKS

        def wait_group(e, at):
            e.wait_ge(mm_done, at.group())

        def wait_read(e, at, back=0):
            e.wait_ge(bank_free[(at.n - back) % BANKS], at._times((at.n - back) // BANKS + 1, at.per[2], BANKS))

        def split_high(act, at, nxt):
            if nxt.u >= len(kinds):
                return
            act.wait_ge(raw_full[nxt.u % RING], nxt.landed())
            if at is not None and at.n:
                act.wait_ge(mm_done, at.group(0))
            act.activation(WH[:, nxt.d % WRING, :], RAW[:, nxt.u % RING, :], ACT.Copy).then_inc(hi_done, 1)
            nxt.next_dense()

        def split_low(dve, nxt):
            if nxt.u >= len(kinds):
                return
            w = nxt.d % WRING
            dve.wait_ge(hi_done, nxt.dense(1))
            dve.tensor_tensor(WL[:, w, :], RAW[:, nxt.u % RING, :], WH[:, w, :].bitcast(F32), ALU.subtract
                              ).then_inc(raw_done[nxt.u % RING], 1)
            nxt.next_dense()

        def three(pe, out, ah, al, bh, bl, first, last):
            pe.matmul(out, al, bh, start=first, stop=False)
            pe.matmul(out, ah, bh, start=False, stop=False)
            return pe.matmul(out, ah, bl, start=False, stop=last)

        def group_begin(pe, at):
            if at.n >= BANKS:
                pe.wait_ge(bank_free[at.n % BANKS], at.bank_uses())

        def tile_begin(pe, at):
            pe.wait_ge(raw_done[at.u % RING], at.tile())

        def feature_group(pe, at, xh, xl, cut, ready=None, ks=range(KT), wk=0):
            w = at.d % WRING
            group_begin(pe, at)
            for i, k in enumerate(ks):
                if ready is not None:
                    ready(pe, k)
                kk = (wk + i) * P
                last = three(pe, DP[:, bank(at), 0:cut[1] - cut[0]], WH[:, w, kk:kk + P], WL[:, w, kk:kk + P],
                             xh[:, k, cut[0]:cut[1]], xl[:, k, cut[0]:cut[1]], i == 0, i == len(ks) - 1)
            last.then_inc(mm_done, 1)
            at.n += 1

        def feature_tile(pe, at, xh, xl, cuts, ready=None):
            tile_begin(pe, at)
            for c, cut in enumerate(cuts):
                feature_group(pe, at, xh, xl, cut, ready if c == 0 else None)
            at.u += 1
            at.d += 1

        def token_tiles(pe, at, tiles, n=1, xh=HH, xl=HL):
            w = at.d % WRING
            for i in range(n):
                tile_begin(pe, at)
                at.u += 1
                at.d += 1
            for m in range(tiles):
                group_begin(pe, at)
                for k in range(KT):
                    wh, wl = (x[:, w:w + n, k * P:(k + 1) * P] for x in (WH, WL))
                    last = three(pe, DP[:, bank(at), 0:n * P].rearrange("p (a n) -> p a n", n=P),
                                 xh[:, k, m * P:(m + 1) * P], xl[:, k, m * P:(m + 1) * P], wh, wl, k == 0, k == KT - 1)
                last.then_inc(mm_done, 1)
                at.n += 1

        def keep_clock(pe, n, out):
            for _ in range(n):
                pe.matmul(out, HH[:, KT - 1, 0:P], HH[:, KT - 1, P:P + 512], start=True, stop=True)

        def mod_stream(dve, at, col, s, count):
            if s == 0:
                dve.wait_ge(raw_full[at.u % RING], at.landed())
            if not isinstance(count, int) or count:
                dve.wait_ge(sem("mod_summed"), count)
            dve.scalar_tensor_tensor(MPROD[:, :], RAW[:, at.u % RING, :], 1.0, COND[:, s, :], ALU.mult, ALU.mult,
                                     accum_out=MODT[:, col, s:s + 1]).then_inc(sem("mod_summed"), 1)
            if s == 1:
                dve.wait_ge(sem("mod_summed"), count + 1)
                dve.sem_inc(raw_done[at.u % RING], 1)
                at.u += 1

        def mod_tile(dve, at, col, count):
            mod_stream(dve, at, col, 0, count * 2)
            mod_stream(dve, at, col, 1, count * 2 + 1)

        def mod_add_bias(dve, n, dst):
            for s in range(2):
                ins = dve.tensor_tensor(MOD[:, dst(n), s], MODT[:, 0:n, s],
                                        VECS[:, dst(n, VEC["b_mod"][0])], ALU.add)
            ins.then_inc(mods_read, 1)

        NORMS = [("pre0", T, "product"), ("post0", T, "sum"), ("pre1", T, "product"), ("post1", T, "sum"),
                 ("pre2", T, "product"), ("post2", LAT, "sum"), ("pre3", LAT, "product"), ("post3", LAT, "sum"),
                 ("mix", LAT, "product"), ("ffn", LAT, "product")]

        def norm_count(nm, step, count):
            for name, tokens, kind in NORMS:
                if name == nm:
                    return count
                parts = KT * len(parts_of(tokens))
                if step in ("squared", "summed"):
                    count += KT
                elif step == "rstd":
                    count += 2
                elif kind == "product" and step in ("scaled", "high", "low"):
                    count += parts
                elif kind == "sum" and step in ("term", "x"):
                    count += parts if step == "term" else KT

        def norm_wait(e, nm, step, count):
            e.wait_ge(sem("norm_" + step), norm_count(nm, step, count))

        def norm_square(act, nm, src, tokens, k):
            if k >= 2:
                norm_wait(act, nm, "summed", k - 1)
            act.activation(TQ[:, k % 2, 0:tokens], src(k), ACT.Square).then_inc(sem("norm_squared"), 1)

        def norm_sum(pe, nm, tokens, k, tiles=KT):
            norm_wait(pe, nm, "squared", k + 1)
            for c, (a0, b0) in enumerate(cuts_of(tokens)):
                last = pe.matmul(XP[:, c, 0:b0 - a0], ONES, TQ[:, k % 2, a0:b0],
                                 start=(k == 0), stop=(k == tiles - 1))
            last.then_inc(sem("norm_summed"), 1)

        def norm_rstd(act, nm, tokens, tiles=KT, n=D):
            norm_wait(act, nm, "summed", tiles)
            cuts = cuts_of(tokens)
            w = cuts[0][1]
            act.activation(TR[:, 0:tokens].rearrange("p (c n) -> p c n", n=w), XP[:, 0:len(cuts), 0:w], ACT.Ln,
                           scale=1.0 / n, bias=EPSV[:, 0:1]).then_inc(sem("norm_rstd"), 1)
            norm_wait(act, nm, "rstd", 1)
            act.activation(TR[:, 0:tokens], TR[:, 0:tokens], ACT.Exp, scale=-0.5).then_inc(sem("norm_rstd"), 1)

        def norm_low(dve, nm, k, np_, tokens, sh):
            norm_wait(dve, nm, "high", np_ * (k + 1))
            for a0, b0, s in parts_of(tokens):
                dve.scalar_tensor_tensor(HL[:, k, a0:b0], TQ[:, k % 2, a0:b0], sh(k, s), HH[:, k, a0:b0].bitcast(F32),
                                         ALU.add, ALU.subtract).then_inc(sem("norm_low"), 1)

        def norm_scale(dve, nm, src, tokens, am, sh):
            norm_wait(dve, nm, "rstd", 2)
            np_ = len(parts_of(tokens))
            for k in range(KT):
                if k >= 2:
                    norm_wait(dve, nm, "low", np_ * (k - 1))
                for a0, b0, s in parts_of(tokens):
                    dve.scalar_tensor_tensor(TQ[:, k % 2, a0:b0], src(k)[:, a0:b0], am(k, s), TR[:, a0:b0],
                                             ALU.mult, ALU.mult).then_inc(sem("norm_scaled"), 1)
                if k >= 1:
                    norm_low(dve, nm, k - 1, np_, tokens, sh)
            norm_low(dve, nm, KT - 1, np_, tokens, sh)

        def norm_high(act, nm, tokens, sh):
            np_ = len(parts_of(tokens))
            for k in range(KT):
                for i, (a0, b0, s) in enumerate(parts_of(tokens)):
                    norm_wait(act, nm, "scaled", np_ * k + i + 1)
                    act.activation(HH[:, k, a0:b0], TQ[:, k % 2, a0:b0], ACT.Identity, bias=sh(k, s)
                                   ).then_inc(sem("norm_high"), 1)

        def norm_ready(nm, tokens):
            np_ = len(parts_of(tokens))
            return lambda pe, k: norm_wait(pe, nm, "low", np_ * (k + 1))

        def residual(dve, nm, tokens, am):
            norm_wait(dve, nm, "rstd", 2)
            np_ = len(parts_of(tokens))
            for k in range(KT + 1):
                if k < KT:
                    for a0, b0, s in parts_of(tokens):
                        dve.scalar_tensor_tensor(Y[:, k, a0:b0], Y[:, k, a0:b0], am(k, s), TR[:, a0:b0],
                                                 ALU.mult, ALU.mult).then_inc(sem("norm_term"), 1)
                if k >= 1:
                    norm_wait(dve, nm, "term", np_ * k)
                    dve.tensor_tensor(X[:, k - 1, 0:tokens], X[:, k - 1, 0:tokens], Y[:, k - 1, 0:tokens],
                                      ALU.add).then_inc(sem("norm_x"), 1)

        def after(name, per=1, base=0):
            return lambda e, k: e.wait_ge(sem(name), base + per * (k + 1))

        def Xk(tokens):
            return lambda k: X[:, k, 0:tokens]

        def Yk(tokens):
            return lambda k: Y[:, k, 0:tokens]

        def heads_of_blocks():
            for g in range(KV_HEADS):
                for b in range(T // P):
                    near = [kb for kb in (b - 1, b, b + 1) if 0 <= kb < LAT // P] if b < LAT // P else []
                    for hh in range(GROUP):
                        yield (g * (T // P) + b) * GROUP + hh, g, b, hh, near

        def rope_splits(r):
            return 4 * (r + 1) if r < 2 else 8 + r - 1

        block = ctx.enter_context(nc.Block())

        @block.sync
        def _(sp):
            sp.dma_start(COND[:, :, :], a["cond"]).then_inc(sem("cond_landed"), 16)
            sp.dma_start(VECS[:, :], a["vec"]).then_inc(loads, 16)
            sp.dma_start(CONST[:, :], a["const"]).then_inc(loads, 16)
            sp.dma_start(ROWS[:, :], a["row"]).then_inc(loads, 16)
            for k in range(KT):
                sp.dma_start(X[:, k, :], a["x"][:, k, :]).then_inc(sem(f"x_landed{k // 4}"), 16)
            for i in range(RING):
                sp.dma_start(RAW[:, i, :], a["stream"][i]).then_inc(raw_full[i], 16)
            sp.dma_start(COS[:, :], a["rope"][:, 0:LAT]).then_inc(rope_loads, 16)
            sp.dma_start(SIN[:, :], a["rope"][:, LAT:2 * LAT]).then_inc(rope_loads, 16)
            sp.dma_start(BAND[:, :], a["rope"][:, 2 * LAT:]).then_inc(rope_loads, 16)
            rounds = len(kinds) // RING
            with sp.Fori(1, rounds) as r:
                for i in range(RING):
                    sp.wait_ge(raw_done[i], r)
                    sp.dma_start(RAW[:, i, :], a["stream"][bass.ds(r * RING + i, 1)].rearrange("o p n -> (o p) n")
                                 ).then_inc(raw_full[i], 16)
            for t in range(RING * rounds, len(kinds) + 1):
                sp.wait_ge(raw_done[t % RING], t // RING)
                sp.dma_start(RAW[:, t % RING, :], a["stream"][min(t, len(kinds) - 1)]).then_inc(raw_full[t % RING], 16)
            at = At(kinds)
            at.n = ALL_GROUPS - KT
            for k in range(KT):
                wait_read(sp, at)
                sp.dma_start(out_d[:, k, :], X[:, k, 0:LAT]).then_inc(sem("stored"), 16)
                at.n += 1
            sp.wait_ge(sem("stored"), 16 * KT)

        @block.gpsimd
        def _(pool):
            pool.memset(EPSV[:, :], EPS).then_inc(sem("eps_set"), 1)
            pool.memset(QUARTER[:, :], TWO_PI / 4.0).then_inc(sem("eps_set"), 1)
            norm_wait(pool, "post0", "x", KT)
            for k in range(KT):
                pool.memset(Y[:, k, :], 0.0).then_inc(sem("y_zero"), 1)

            norm_wait(pool, "post2", "x", KT)
            for k in range(KT):
                pool.memset(Y[:, k, 0:LAT], 0.0).then_inc(sem("y_zero"), 1)

            pool.wait_ge(sem("ssm_prep"), SSM_PREP)
            MAGIC = 1.5 * 2.0 ** 23

            def turns(i):
                pool.wait_ge(sem("turn_scaled"), i + 1)
                pool.tensor_scalar(TR[:, 0:LAT], TURN[:, :], MAGIC, MAGIC, ALU.add, ALU.subtract
                                   ).then_inc(sem("turn_steps"), 1)
                pool.wait_ge(sem("turn_steps"), i + 1)
                pool.tensor_tensor(TURN[:, :], TURN[:, :], TR[:, 0:LAT], ALU.subtract).then_inc(sem("ssm_turns"), 1)
                pool.wait_ge(sem("ssm_turns"), 2 * i + 1)
                pool.tensor_scalar(TR[:, 0:LAT], TURN[:, :], 0.25, None, ALU.is_gt).then_inc(sem("turn_back"), 1)
                pool.wait_ge(sem("turn_back"), i + 1)
                pool.tensor_tensor(TR[:, 0:LAT], TURN[:, :], TR[:, 0:LAT], ALU.subtract).then_inc(sem("ssm_turns"), 1)

            def outputs_scaled(i):
                pool.wait_ge(sem(f"ssm_mats{i % 2}"), 16 * (i // 2 + 1))
                if i:
                    pool.wait_ge(sem("ssm_out"), i)
                for c, f in ((0, 11), (1, 5)):
                    pool.tensor_scalar(TQ[:, 0:2, LAT + c * P:LAT + (c + 1) * P], MATS[:, i % 2, 2:4, :],
                                       PV(f)[:, i:i + 1], None, ALU.mult).then_inc(sem("c_steps"), 1)
                pool.wait_ge(sem("c_steps"), 2 * i + 2)
                pool.tensor_tensor(CM(0), CM(0), CM(3), ALU.add).then_inc(sem("ssm_c"), 1)
                pool.tensor_tensor(CM(2), CM(1), CM(2), ALU.subtract).then_inc(sem("ssm_c"), 1)

            turns(0)
            for i in range(16):
                if i < 15:
                    turns(i + 1)
                outputs_scaled(i)

            pool.wait_ge(sem("merged_low"), KT)
            pool.memset(GT[:, :], 0.0).then_inc(sem("gate_rows_zero"), 1)
        @block.tensor
        def _(pe):
            at = At(kinds)
            c768, c512 = cuts_of(T), cuts_of(LAT)

            pe.wait_ge(loads, 16 * NLOADS)
            for k in range(KT):
                norm_sum(pe, "pre0", T, k)
            at.u = 16
            def rotate(r, back):
                if r >= 2:
                    pe.wait_ge(sem("rope_sine"), r - 1)
                wait_read(pe, at, back)
                wait_read(pe, at, back - 1)
                pe.matmul(XP[:, r % 2, :], SWAP, TQ[:, r % 2, 0:LAT], start=True, stop=True).then_inc(sem("rope_swapped"), 1)

            feature_tile(pe, at, HH, HL, c768, norm_ready("pre0", T))
            feature_tile(pe, at, HH, HL, c768)
            rotate(0, 4)
            for r in range(2, 10):
                feature_tile(pe, at, HH, HL, c768)
                rotate(r - 1, 4)
            rotate(9, 2)
            token_tiles(pe, at, T // P, 2)

            def scores(aa, g, b, hh, near):
                p, j, rows = aa % 2, 2 * g + hh // 2, slice(64 * (hh % 2), 64 * (hh % 2) + 64)
                qh, ql = (x[rows, j, b * P:(b + 1) * P] for x in (AH, AL))
                if near:
                    w = P * len(near)
                    out = DP[:, 2 * p, 512 - w:512]
                    kh, kl = (x[rows, g, near[0] * P:(near[-1] + 1) * P] for x in (KDH, KDL))
                    pe.matmul(out, ql, kh, start=True, stop=False)
                    pe.matmul(out, qh, kh, start=False, stop=False)
                    pe.matmul(out, qh, kl, start=False, stop=False)
                    if b > 0:
                        pe.matmul(DP[:, 2 * p, 512 - w:512 - w + P], IDF[:, :], BANDF[:, 0, :], start=False,
                                  stop=(b == LAT // P - 1))
                    if b < LAT // P - 1:
                        pe.matmul(DP[:, 2 * p, 512 - P:512], IDF[:, :], BANDF[:, 1, :], start=False, stop=True)
                three(pe, DP[:, 2 * p + 1, 0:CTX], qh, ql, KDH[rows, g, LAT:T], KDL[rows, g, LAT:T], True, True
                      ).then_inc(sem("scored"), 1)

            def transposes(aa, near):
                p, n = aa % 2, len(near) + 2
                pe.wait_ge(sem("exponentials"), aa + 1)
                if aa:
                    pe.wait_ge(sem("turned_low"), aa)
                for i in range(n):
                    to = 512 + (i - len(near)) * P
                    last = pe.matmul(XPF[:, to:to + P], PB[:, p, i * P:(i + 1) * P], IDENT, start=True, stop=True)
                last.then_inc(sem("transposed"), 1)

            def weighted_values(aa, g, b, hh, near):
                pe.wait_ge(sem("turned_low"), aa + 1)
                if hh == 0 and aa:
                    pe.wait_ge(sem("out_scaled"), aa // GROUP)
                keys, at0 = near + [4, 5], hh * 2 * HD
                out, out_high = XP[:, 2, at0:at0 + 2 * HD], XP[:, 2, at0:at0 + HD]
                pe.matmul(out, PTH[:, aa % 2, 0, :], VHL[:, keys[0], g, :], start=True, stop=False)
                for i, kt in enumerate(keys):
                    pe.matmul(out_high, PTL[:, aa % 2, i, :], VHL[:, kt, g, 0:HD], start=False, stop=False)
                for i, kt in enumerate(keys[1:]):
                    last = pe.matmul(out, PTH[:, aa % 2, i + 1, :], VHL[:, kt, g, :], start=False, stop=(kt == 5))
                last.then_inc(sem("attended"), 1)

            def out_turned(blk):
                pe.wait_ge(sem("out_scaled"), blk + 1)
                if blk:
                    pe.wait_ge(sem("mixed_low"), blk)
                for j in range(2):
                    last = pe.transpose(XP[:, 3, j * P:(j + 1) * P], OS[:, j * P:(j + 1) * P], IDENT)
                last.then_inc(sem("out_turned"), 1)

            work = list(heads_of_blocks())
            for b in range(BANKS):
                wait_read(pe, at, b + 1)
            pe.wait_ge(sem("rope_low"), rope_splits(9))
            pe.wait_ge(sem("band_ready"), 2)
            scores(*work[0])
            scores(*work[1])
            for aa, g, b, hh, near in work:
                transposes(aa, near)
                if aa + 2 < len(work):
                    keep_clock(pe, STEP_FILL, DP[:, 2 * (aa % 2), :])
                    scores(*work[aa + 2])
                if aa:
                    weighted_values(*work[aa - 1])
                blk = aa // GROUP
                if hh == 1 and blk:
                    out_turned(blk - 1)
            weighted_values(*work[-1])
            out_turned(blk)
            at.u += 32

            pe.wait_ge(sem("mixed_low"), 24)
            for t in range(KT):
                feature_tile(pe, at, AH, AL, c768)
                if t >= 1:
                    norm_sum(pe, "post0", T, t - 1)
            norm_sum(pe, "post0", T, KT - 1)
            for k in range(KT):
                norm_sum(pe, "pre1", T, k)

            tile_begin(pe, at)
            for k in range(KT):
                norm_ready("pre1", T)(pe, k)
            with pe.Fori(0, MLP_STEPS) as it:
                at.enter(it, 28, 16, 32)
                for t in range(2 * KT):
                    if t < KT:
                        feature_tile(pe, at, HH, HL, c768)
                    else:
                        feature_tile(pe, at, AH, AL, c768, (lambda e, k: e.wait_ge(sem("hidden_low"), it * 16 + 2 * (k + 1)))
                                     if t == KT else None)
                    if t < 12:
                        at.u += 1
                at.leave(MLP_STEPS)
            for k in range(KT):
                norm_sum(pe, "post1", T, k)

            for k in range(KT):
                norm_sum(pe, "pre2", T, k)

            pe.wait_ge(sem("gate_down_split"), 2)
            for c, (a0, b0) in enumerate(c768):
                for k in range(KT):
                    if c == 0:
                        norm_ready("pre2", T)(pe, k)
                    last = three(pe, XP[0:64, c, 0:384], WDH[:, k // 4, (k % 4) * 64:(k % 4 + 1) * 64], WDL[:, k // 4, (k % 4) * 64:(k % 4 + 1) * 64],
                                 HH[:, k, a0:b0], HL[:, k, a0:b0], k == 0, k == KT - 1)
            last.then_inc(sem("gate_low_made"), 1)

            def gate_product(h, d):
                if h == 0 and d == 0:
                    pe.wait_ge(sem("gate_low_read"), 1)
                else:
                    pe.wait_ge(sem("gate_logits_read"), 2 * h + d)
                if h and not d:
                    pe.wait_ge(sem("out_rstd"), 2 * h)
                rows = slice(32 * d, 32 * d + 32)
                for c, (a0, b0) in enumerate(c768):
                    last = pe.matmul(XP[:, c, 0:384], WU[rows, h * P:(h + 1) * P], LOW[rows, a0:b0], start=True, stop=True)
                last.then_inc(sem("gate_logits_made"), 1)

            def key_transposes(h, d):
                s = 2 * h + d
                pe.wait_ge(sem("keys_decayed"), s + 1)
                pe.wait_ge(sem("gate_logits_read"), 2 * h + 2)
                if s:
                    pe.wait_ge(sem("keys_turned_copied"), s)
                for m in range(T // P):
                    last = pe.transpose(XP[:, m // 3, (m % 3) * P:(m % 3 + 1) * P], KEF[:, d, m * P:(m + 1) * P], IDENT)
                last.then_inc(sem("keys_turned"), 1)

            def scan(h, d):
                s = 2 * h + d
                order = SCAN_TILES[d]
                halves = (0, 1) if d == 0 else (1, 0)

                def mixing(i):
                    m = order[i]
                    if m < LAT // P:
                        j = i - 2
                        n = s * 4 + j
                        if n >= 2:
                            pe.wait_ge(sem("mixing_masked"), n - 1)
                        pe.matmul(DP[:, 2 + j % 2, 0:P], KI[:, d, m * P:(m + 1) * P], QD[:, d, m * P:(m + 1) * P],
                                  start=True, stop=True).then_inc(sem("mixing_made"), 1)

                def updates(i):
                    m = order[i]
                    for e, half in enumerate(halves):
                        c = 2 * i + e
                        if c == 11:
                            continue
                        n = s * 11 + c
                        rows = slice(64 * half, 64 * half + 64)
                        if n >= 2:
                            pe.wait_ge(sem("state_updated"), n - 1 if c >= 1 else n)
                        pe.matmul(XP[:, 2 + c % 2, 0:GLA_DV], KE[rows, m, :], VT[rows, m, :], start=True, stop=True
                                  ).then_inc(sem("update_made"), 1)

                def output(i):
                    m = order[i]
                    if m >= LAT // P:
                        return
                    j = i - 2
                    n = s * 4 + j
                    pe.wait_ge(sem("mixing_masked"), n + 1)
                    pe.wait_ge(sem("state_updated"), s * 11 + 2 * i + 1)
                    if n >= 2:
                        pe.wait_ge(sem("mixed_out_read"), n - 1)
                    keep_clock(pe, SCAN_FILL, DP[:, j % 2, :])
                    for v in range(2):
                        pe.matmul(DP[:, j % 2, v * P:(v + 1) * P], VT[:, m, v * P:(v + 1) * P], ATM[:, d, j % 2, :],
                                  start=True, stop=False)
                        for e, half in enumerate(halves):
                            out = DP[:, j % 2, v * P + 64 * half:v * P + 64 * half + 64]
                            last = pe.matmul(out, S[:, (2 * i + e) % 4, v * P:(v + 1) * P],
                                             QD[:, d, m * P + 64 * half:m * P + 64 * half + 64], start=False, stop=(e == 1))
                    last.then_inc(sem("mixed_out_made"), 1)

                pe.wait_ge(sem("queries_decayed"), s + 1)
                pe.wait_ge(sem("keys_turned_copied"), s + 1)
                mixing(0)
                updates(0)
                for i in range(6):
                    if i < 5:
                        mixing(i + 1)
                        updates(i + 1)
                    output(i)

            for h in range(GLA_HEADS):
                if h:
                    pe.wait_ge(sem("mixed_out_read"), 8 * h)
                feature_tile(pe, at, HH, HL, c768)
                feature_tile(pe, at, HH, HL, c768)
                gate_product(h, 0)
                gate_product(h, 1)
                token_tiles(pe, at, T // P, 2)
                if h:
                    pe.wait_ge(sem("state_updated"), 22 * h)
                keep_clock(pe, HEAD_FILL, XP[:, 2, :])
                for b in range(BANKS):
                    wait_read(pe, at, b + 1)
                for d in range(2):
                    key_transposes(h, d)
                    scan(h, d)
                pe.wait_ge(sem("mixed_out_read"), 8 * (h + 1))
                feature_tile(pe, at, HH, HL, c512)
                for v in range(2):
                    pe.wait_ge(sem("out_squared"), 2 * h + v + 1)
                    last = pe.matmul(XP[:, 0, :], ONES, TQ[:, v, 0:LAT], start=(v == 0), stop=(v == 1))
                last.then_inc(sem("out_summed"), 1)
                feature_tile(pe, at, HH, HL, c512)

            pe.wait_ge(sem("gla_low"), 8)
            for t in range(KT):
                feature_tile(pe, at, AH, AL, c512)
                if t >= 1:
                    norm_sum(pe, "post2", LAT, t - 1)
            norm_sum(pe, "post2", LAT, KT - 1)
            for k in range(KT):
                norm_sum(pe, "pre3", LAT, k)

            for k in range(KT):
                norm_ready("pre3", LAT)(pe, k)
            with pe.Fori(0, MLP_STEPS) as it:
                at.enter(it, 16, 16, 16)
                for t in range(2 * KT):
                    if t < KT:
                        feature_tile(pe, at, HH, HL, c512)
                    else:
                        feature_tile(pe, at, AH, AL, c512, (lambda e, k: e.wait_ge(sem("hidden_low"), it * 8 + (64 + k + 1)))
                                     if t == KT else None)
                at.leave(MLP_STEPS)
            for k in range(KT):
                norm_sum(pe, "post3", LAT, k)

            for k in range(KT):
                norm_sum(pe, "mix", LAT, k)
            for t in range(4):
                feature_tile(pe, at, HH, HL, c512, norm_ready("mix", LAT) if t == 0 else None)

            def scores2(n, p, b, e):
                rows = slice(64 * e, 64 * e + 64)
                pe.matmul(XP[:, 2 + e, 0:P * (b + 1)], QN[rows, b * P:(b + 1) * P], KN[rows, 0:P * (b + 1)],
                          start=True, stop=True).then_inc(sem("scored2"), 1)

            def transposes2(n, b, e):
                pe.wait_ge(sem("probabilities2"), n + 1)
                if n:
                    pe.wait_ge(sem("transposes_copied2"), n)
                for i in range(b + 1):
                    last = pe.transpose(XP[:, 0, i * P:(i + 1) * P], PB2[:, e, i * P:(i + 1) * P], IDENT)
                last.then_inc(sem("transposed2"), 1)

            def values2(q, p, b):
                pe.wait_ge(sem("transposes_copied2"), 2 * q + 2)
                if q:
                    pe.wait_ge(sem("mixed_low2"), q)
                for e in range(2):
                    for i in range(b + 1):
                        last = pe.matmul(XP[64 * e:64 * e + 64, 1, 0:P], V2[:, i, (p % 2) * P + e * HD:(p % 2) * P + (e + 1) * HD],
                                         PTS2[:, q % 2, i, e * P:(e + 1) * P], start=(i == 0), stop=(i == b))
                last.then_inc(sem("attended2"), 1)

            for p in range(4):
                feature_tile(pe, at, HH, HL, c512)
                feature_tile(pe, at, HH, HL, c512)
                if p:
                    pe.wait_ge(sem("transposes_copied2"), 8 * p)
                    pe.wait_ge(sem("mixed_low2"), 4 * p)
                for i in range(2):
                    pe.wait_ge(sem("head_squared"), 2 * p + i + 1)
                    pe.matmul(XP[:, i, :], HALVES, SQ2[:, i, :], start=True, stop=True).then_inc(sem("head_summed"), 1)
                if p % 2 == 0:
                    token_tiles(pe, at, LAT // P, 2)
                for b in range(BANKS):
                    wait_read(pe, at, b + 1)
                pe.wait_ge(sem("head_normed"), 2 * p + 2)
                work = [(p * 8 + 2 * b + e, b, e) for b in range(4) for e in range(2)]
                for n, b, e in work[:2]:
                    scores2(n, p, b, e)
                for i, (n, b, e) in enumerate(work):
                    if i + 2 < len(work):
                        n2, b2, e2 = work[i + 2]
                        pe.wait_ge(sem("bias_used"), n + 1)
                        scores2(n2, p, b2, e2)
                    transposes2(n, b, e)
                    if i >= 2 and i % 2 == 0:
                        values2(n // 2 - 1, p, b - 1)
                values2(n // 2, p, b)

            def ssm_inputs(i):
                pe.wait_ge(sem(f"ssm_mats{i % 2}"), 16 * (i // 2 + 1))
                if i:
                    pe.wait_ge(sem("ssm_turned"), 4 * i)
                u = UT(i // 4)
                for z in range(2):
                    last = pe.matmul(XP[:, z, :].rearrange("p (a n) -> p a n", a=2), MATS[:, i % 2, z, :], u,
                                     start=True, stop=True)
                last.then_inc(sem("ssm_driven"), 1)

            def ssm_outputs(i):
                pe.wait_ge(sem("ssm_c"), 2 * i + 2)
                t, j = i // 4, i % 4
                if t >= 2 and j == 0:
                    pe.wait_ge(sem("ssm_y"), t - 1)
                for q, k in enumerate((0, 2)):
                    pe.wait_ge(sem("ssm_state"), 2 * i + q + 1)
                    last = pe.matmul(XP[:, 2 + t % 2, :], CM(k), PR[:, k, :], start=(j == 0 and q == 0), stop=(j == 3 and q == 1))
                last.then_inc(sem("ssm_out"), 1)

            pe.wait_ge(sem("mixed_low2"), 16)
            ssm_inputs(0)
            for i in range(16):
                feature_tile(pe, at, HH, HL, c512)
                if i < 15:
                    ssm_inputs(i + 1)
                ssm_outputs(i)

            def ZT(x, k):
                return x[:, 2 * k:2 * k + 2, LAT:T]

            for t in range(2):
                w = at.d % WRING
                tile_begin(pe, at)
                for jj in range(2):
                    group_begin(pe, at)
                    for k in range(4):
                        if t == 0 and jj == 0:
                            pe.wait_ge(sem("z_low"), k + 1)
                        kk = (4 * jj + k) * P
                        last = three(pe, DP[:, bank(at), :].rearrange("p (a n) -> p a n", a=2), WH[:, w, kk:kk + P],
                                     WL[:, w, kk:kk + P], ZT(AH, k), ZT(AL, k), k == 0, k == 3)
                    last.then_inc(mm_done, 1)
                    at.n += 1
                at.u, at.d = at.u + 1, at.d + 1

            for t in range(KT):
                tile_begin(pe, at)
                for half in range(2):
                    if half and t == 0:
                        pe.wait_ge(sem("z_low"), 8)
                    feature_group(pe, at, AH, AL, (0, LAT), ks=range(4 * half, 4 * half + 4), wk=4 * half)
                at.u, at.d = at.u + 1, at.d + 1

            for t in range(KT):
                feature_tile(pe, at, HH, HL, c512, after("merged_low") if t == 0 else None)
                if t >= 1:
                    norm_sum(pe, "ffn", LAT, t - 1)
            norm_sum(pe, "ffn", LAT, KT - 1)

            for m in range(4):
                for k in range(KT):
                    if m == 0:
                        norm_ready("ffn", LAT)(pe, k)
                        pe.wait_ge(sem("router_split"), 2)
                    last = three(pe, XP[:, 0, m * 20:(m + 1) * 20], HH[:, k, m * P:(m + 1) * P], HL[:, k, m * P:(m + 1) * P],
                                 RWH[:, k * 20:(k + 1) * 20], RWL[:, k * 20:(k + 1) * 20], k == 0, k == KT - 1)
            last.then_inc(sem("router_made"), 1)
            pe.wait_ge(sem("expert_low"), 1)
            for g in range(EXPERT_GROUPS):
                for m in range(4):
                    last = pe.transpose(XP[0:4, g, m * P:(m + 1) * P], GTS[:, m, 4 * g:4 * g + 4], IDENT)
            last.then_inc(sem("gates_turned"), 1)

            with pe.Fori(0, EXPERT_GROUPS) as g:
                at.enter(g, 24, 24, 24)
                for e in range(EXPERTS_PER):
                    pe.wait_ge(sem("gate_row_read"), g * 4 + (e + 1))
                    pe.matmul(XP[:, e % 2, :], SEL[:, e, :], GT[:, bass.ds(g * 512, 512)], start=True, stop=True
                              ).then_inc(sem("gate_row_made"), 1)
                    for j in range(4):
                        feature_tile(pe, at, HH, HL, c512)
                for t in range(KT):
                    feature_tile(pe, at, AH, AL, c512, (lambda q, k: q.wait_ge(sem("expert_low"), g * 8 + (k + 2)))
                                 if t == 0 else None)
                at.leave(EXPERT_GROUPS)

        @block.scalar
        def _(act):
            at, nxt = At(kinds), At(kinds)
            nxt.to_dense()

            act.wait_ge(loads, 16 * NLOADS)
            act.wait_ge(sem("cond_landed"), 16)
            for s in range(2):
                if s:
                    act.wait_ge(cond_done, 4)
                act.activation(MPROD[:, :], COND[:, s, :], ACT.Exp, scale=-1.0).then_inc(cond_done, 1)
            for k in range(KT):
                act.wait_ge(sem(f"x_landed{k // 4}"), 64)
                norm_square(act, "pre0", Xk(T), T, k)
            act.wait_ge(sem("eps_set"), 2)
            norm_rstd(act, "pre0", T)
            norm_high(act, "pre0", T, shift(0, 0))
            at.u = 16

            def copy_group(out, scale=1.0):
                wait_group(act, at)
                act.activation(out, DP[:, bank(at), 0:384] if out.shape[-1] == 384 else DP[:, bank(at), 0:out.shape[-1]],
                               ACT.Copy, scale=scale).then_inc(bank_free[bank(at)], 1)
                at.n += 1

            def copy_feature(r, scale):
                if r >= 2:
                    act.wait_ge(sem("rope_low"), rope_splits(r - 2))
                for c in range(2):
                    copy_group(TQ[:, r % 2, 384 * c:384 * c + 384], scale)
                at.u += 1
                at.d += 1

            def rope_high(r):
                act.wait_ge(sem("rope_done"), r + 1)
                if r >= 2:
                    act.activation(AH[:, r - 2, :], TQ[:, r % 2, :], ACT.Copy).then_inc(sem("rope_high"), 1)
                else:
                    for e in range(2):
                        for half in range(2):
                            act.activation(KDH[64 * half:64 * half + 64, 2 * r + e, :], TQ[64 * e:64 * e + 64, r % 2, :],
                                           ACT.Copy).then_inc(sem("rope_high"), 1)

            split_high(act, at, nxt)
            split_high(act, None, nxt)
            act.wait_ge(rope_loads, 48)
            act.activation(IDF[:, :], IDENT, ACT.Copy).then_inc(sem("band_ready"), 1)
            act.activation(BANDF[:, :, :], BAND[:, :].rearrange("p (b n) -> p b n", n=P)[:, 0:3:2, :], ACT.Copy
                           ).then_inc(sem("band_ready"), 1)
            copy_feature(0, 1.0)
            split_high(act, at, nxt)
            copy_feature(1, 1.0)
            for r in range(2, 10):
                rope_high(r - 2)
                split_high(act, at, nxt)
                copy_feature(r, QUERY)
            split_high(act, at, nxt)
            rope_high(8)
            for m in range(T // P):
                wait_group(act, at)
                act.activation(VHL[:, m, :, 0:HD], DP[:, bank(at), 0:2 * P].rearrange("p (h n) -> p h n", n=HD),
                               ACT.Copy).then_inc(sem("value_high"), 1)
                at.n += 1
                if m == 1:
                    rope_high(9)
            at.u += 2
            at.d += 2

            def exps(aa, g, b, hh, near):
                p, n, q = aa % 2, P * (len(near) + 2), aa // GROUP % 2
                act.wait_ge(sem("shift_ready"), aa + 1)
                if aa >= 2:
                    act.wait_ge(sem("transposed"), aa - 1)
                act.activation(PB[:, p, 0:n], DPF[:, p * 1024 + 768 - n:p * 1024 + 768], ACT.Exp,
                               bias=ST[:, q, 1, hh:hh + 1], accum_out=ST[:, q, 2, hh:hh + 1]
                               ).then_inc(sem("exponentials"), 1)

            def turned_high(aa, near):
                act.wait_ge(sem("transposed"), aa + 1)
                if aa >= 2:
                    act.wait_ge(sem("attended"), aa - 1)
                n = len(near)
                act.activation(PTH[:, aa % 2, 0:n + 2, :],
                               XPF[:, 512 - n * P:512 + 2 * P].rearrange("p (k n) -> p k n", n=P), ACT.Copy
                               ).then_inc(sem("turned_high"), 1)

            def mixed_high(blk, g, b):
                act.wait_ge(sem("out_turned"), blk + 1)
                act.activation(AH[:, 2 * g:2 * g + 2, b * P:(b + 1) * P],
                               XP[:, 3, 0:2 * P].rearrange("p (j n) -> p j n", n=P), ACT.Copy).then_inc(sem("mixed_high"), 1)

            work = list(heads_of_blocks())
            exps(*work[0])
            for aa, g, b, hh, near in work:
                if aa + 1 < len(work):
                    exps(*work[aa + 1])
                turned_high(aa, near)
                if hh == 2:
                    act.wait_ge(sem("sink_shifted"), aa // GROUP + 1)
                    act.activation(ST[:, aa // GROUP % 2, 3, :], ST[:, aa // GROUP % 2, 3, :], ACT.Exp
                                   ).then_inc(sem("sink_term"), 1)
                if hh == 1 and aa > GROUP:
                    mixed_high(aa // GROUP - 1, *work[aa - GROUP][1:3])
            mixed_high(aa // GROUP, g, b)
            at.u += 32
            split_high(act, at, nxt)

            for t in range(KT):
                split_high(act, at, nxt)
                for c in range(2):
                    copy_group(Y[:, t, 384 * c:384 * c + 384])
                at.u += 1
                at.d += 1
                wait_read(act, at, 1)
                norm_square(act, "post0", Yk(T), T, t)
            norm_rstd(act, "post0", T)
            for k in range(KT):
                norm_wait(act, "post0", "x", k + 1)
                norm_square(act, "pre1", Xk(T), T, k)
            norm_rstd(act, "pre1", T)
            norm_high(act, "pre1", T, shift(0, 3))

            with act.Fori(0, MLP_STEPS) as it:
                at.enter(it, 28, 16, 32)
                nxt.enter(it, 28, 16, 32)
                for t in range(2 * KT):
                    split_high(act, at, nxt)
                    if t < KT:
                        for c in range(2):
                            i = 2 * t + c
                            wait_read(act, at, 0)
                            if i >= 2:
                                act.wait_ge(sem("hidden_low"), it * 16 + (i - 1))
                            r = TQ[:, i % 2, 0:384]
                            act.activation(SQ[:, i % 2, 0:384], r, ACT.Square)
                            act.activation(AH[:, t, 384 * c:384 * c + 384], r, ACT.Square).then_inc(sem("hidden_high"), 1)
                            at.n += 1
                    else:
                        at.n += 2
                    at.u += 1
                    at.d += 1
                    if t < 12:
                        at.u += 1
                at.leave(MLP_STEPS)
                nxt.leave(MLP_STEPS)
                nxt.u = at.u + 1
            for b in range(BANKS):
                wait_read(act, at, b + 1)
            for k in range(KT):
                norm_square(act, "post1", Yk(T), T, k)
            norm_rstd(act, "post1", T)

            for k in range(KT):
                norm_wait(act, "post1", "x", k + 1)
                norm_square(act, "pre2", Xk(T), T, k)
            act.dma_start(QD[:, 0, :], a["gla_down"]).then_inc(sem("gla_loads"), 16)
            act.dma_start(WU[:, :], a["gla_up"]).then_inc(sem("gla_loads"), 16)
            act.dma_start(CAUSAL[:, :, :], a["causal"]).then_inc(sem("gla_loads"), 16)
            norm_rstd(act, "pre2", T)
            act.wait_ge(sem("gla_loads"), 48)
            act.activation(WDH, QD[:, 0, :].rearrange("p (a n) -> p a n", a=2), ACT.Copy).then_inc(sem("gate_down_split"), 1)
            norm_high(act, "pre2", T, shift(1, 0))
            act.wait_ge(sem("gate_low_made"), 1)
            act.activation(LOW[:, :].rearrange("p (c n) -> p c n", n=384), XP[0:64, 0:2, 0:384], ACT.Copy
                           ).then_inc(sem("gate_low_read"), 1)
            INV = 1.0 / 16.0
            exps_n = [0]

            def gate_exps(h):
                for d in range(2):
                    act.wait_ge(sem("gate_folded"), 2 * h + d + 1)
                    act.activation(B[:, d, :], B[:, d, :], ACT.Exp).then_inc(sem("gate_exp"), 1)
                for d in range(2):
                    act.wait_ge(sem("gate_exp"), 2 * h + d + 1)
                    act.activation(B[:, d, :], B[:, d, :], ACT.Ln, bias=1.0).then_inc(sem("gate_log"), 1)

            def decay_exps(h, d):
                s = 2 * h + d
                act.wait_ge(sem("decays_summed"), s + 1)
                if h:
                    act.wait_ge(sem("mixed_out_made"), 4 * (s - 1))
                act.activation(B[:, d, :], B[:, d, :], ACT.Exp, scale=INV).then_inc(sem("decay_exps"), 1)
                act.activation(QD[:, d, :], BC[:, 0:LAT], ACT.Exp, scale=INV).then_inc(sem("decay_exps"), 1)
                act.activation(KI[:, d, :], BC[:, 0:LAT], ACT.Exp, scale=-INV).then_inc(sem("decay_exps"), 1)
                act.activation(DEC[:, d, :], TOT[:, d, :], ACT.Exp, scale=INV).then_inc(sem("decay_exps"), 1)

            def scan_outputs(h, d):
                s = 2 * h + d
                act.wait_ge(sem("keys_turned"), s + 1)
                if s:
                    act.wait_ge(sem("update_made"), 11 * s)
                act.activation(KE[:, :, :].rearrange("p (c m) n -> p c (m n)", c=2), XP[:, 0:2, 0:384], ACT.Copy
                               ).then_inc(sem("keys_turned_copied"), 1)
                if d == 0:
                    for i in range(2, 6):
                        m, n = SCAN_TILES[d][i], 4 * s + i - 2
                        act.wait_ge(sem("mixed_out_made"), n + 1)
                        if h and i == 2:
                            act.wait_ge(sem("gla_high"), 2 * h)
                        act.activation(O[:, :, m * P:(m + 1) * P], DP[:, i % 2, 0:2 * P].rearrange("p (v n) -> p v n", v=2),
                                       ACT.Copy).then_inc(sem("mixed_out_read"), 1)

            for h in range(GLA_HEADS):
                split_high(act, at, nxt)
                for c in range(2):
                    copy_group(QT[:, 384 * c:384 * c + 384], P ** -0.5)
                at.u, at.d = at.u + 1, at.d + 1
                split_high(act, at, nxt)
                for c in range(2):
                    copy_group(KEYS[:, 384 * c:384 * c + 384])
                at.u, at.d = at.u + 1, at.d + 1
                split_high(act, at, nxt)
                gate_exps(h)
                for m in range(T // P):
                    copy_group(VT[:, m, :])
                    if m in (2, 3):
                        decay_exps(h, m - 2)
                at.u, at.d = at.u + 2, at.d + 2
                split_high(act, at, nxt)
                for d in range(2):
                    scan_outputs(h, d)
                for v in range(2):
                    act.wait_ge(sem("mixed_out_read"), 8 * (h + 1))
                    act.activation(TQ[:, v, 0:LAT], O[:, v, :], ACT.Square).then_inc(sem("out_squared"), 1)
                act.wait_ge(sem("out_summed"), h + 1)
                act.activation(TR[:, 0:LAT], XP[:, 0, :], ACT.Ln, scale=1.0 / GLA_DV, bias=EPSV[:, 0:1]
                               ).then_inc(sem("out_rstd"), 1)
                act.wait_ge(sem("out_rstd"), 2 * h + 1)
                act.activation(TR[:, 0:LAT], TR[:, 0:LAT], ACT.Exp, scale=-0.5).then_inc(sem("out_rstd"), 1)
                for v in range(2):
                    split_high(act, at, nxt)
                    n = 2 * h + v
                    wait_group(act, at)
                    act.activation(TQ[:, v, 0:LAT], DP[:, bank(at), :], ACT.Sigmoid).then_inc(sem("gla_sigmoid"), 1)
                    at.n, at.u, at.d = at.n + 1, at.u + 1, at.d + 1
                for v in range(2):
                    n = 2 * h + v
                    act.wait_ge(sem("gla_gated"), n + 1)
                    act.activation(AH[:, n, 0:LAT], O[:, v, :], ACT.Copy).then_inc(sem("gla_high"), 1)

            for t in range(KT):
                split_high(act, at, nxt)
                copy_group(Y[:, t, 0:LAT])
                at.u, at.d = at.u + 1, at.d + 1
                wait_read(act, at, 1)
                norm_square(act, "post2", Yk(LAT), LAT, t)
            norm_rstd(act, "post2", LAT)
            for k in range(KT):
                norm_wait(act, "post2", "x", k + 1)
                norm_square(act, "pre3", Xk(LAT), LAT, k)
            norm_rstd(act, "pre3", LAT)
            norm_high(act, "pre3", LAT, shift(1, 3))

            with act.Fori(0, MLP_STEPS) as it:
                at.enter(it, 16, 16, 16)
                nxt.enter(it, 16, 16, 16)
                for t in range(2 * KT):
                    split_high(act, at, nxt)
                    if t < KT:
                        wait_read(act, at, 0)
                        if t >= 2:
                            act.wait_ge(sem("hidden_low"), it * 8 + (64 + t - 1))
                        r = TQ[:, t % 2, 0:LAT]
                        act.activation(SQ[:, t % 2, :], r, ACT.Square)
                        act.activation(AH[:, t, 0:LAT], r, ACT.Square).then_inc(sem("hidden_high"), 1)
                    at.n, at.u, at.d = at.n + 1, at.u + 1, at.d + 1
                at.leave(MLP_STEPS)
                nxt.leave(MLP_STEPS)
            for b in range(BANKS):
                wait_read(act, at, b + 1)
            for k in range(KT):
                norm_square(act, "post3", Yk(LAT), LAT, k)
            norm_rstd(act, "post3", LAT)

            for k in range(KT):
                norm_wait(act, "post3", "x", k + 1)
                norm_square(act, "mix", Xk(LAT), LAT, k)
            for p in range(2):
                act.dma_start(BW[:, p, :, :], a["rel"][p]).then_inc(sem(f"bias_landed{p}"), 16)
            norm_rstd(act, "mix", LAT)
            norm_high(act, "mix", LAT, nil)
            act.activation(PV(0), vec("log_step", 0, 16), ACT.Exp).then_inc(sem("ssm_prep"), 1)
            act.wait_ge(sem("ssm_prep"), 3)
            act.activation(PV(2), PV(1), ACT.Exp).then_inc(sem("ssm_prep"), 1)

            for t in range(4):
                split_high(act, at, nxt)
                wait_group(act, at)
                act.activation(UT(t), DP[:, bank(at), :].rearrange("p (a n) -> p a n", a=2), ACT.Copy
                               ).then_inc(bank_free[bank(at)], 1)
                at.n, at.u, at.d = at.n + 1, at.u + 1, at.d + 1

            def exps2(n, b, e):
                act.wait_ge(sem("shift_ready2"), n + 1)
                if n >= 2:
                    act.wait_ge(sem("transposed2"), n - 1)
                w = P * (b + 1)
                act.activation(PB2[:, e, 0:w], SS[:, e, 0:w], ACT.Exp, bias=ST2[:, e, 1:2], accum_out=ST2[:, e, 2:3]
                               ).then_inc(sem("exponentials2"), 1)

            def copy_transposes2(n, b, e):
                act.wait_ge(sem("transposed2"), n + 1)
                q = n // 2
                if q >= 2:
                    act.wait_ge(sem("attended2"), q - 1)
                act.activation(PTS2[:, q % 2, 0:b + 1, e * P:(e + 1) * P],
                               XP[:, 0, 0:P * (b + 1)].rearrange("p (k n) -> p k n", n=P), ACT.Copy
                               ).then_inc(sem("transposes_copied2"), 1)

            def mixed_high2(q, p, b):
                act.wait_ge(sem("attended2"), q + 1)
                act.activation(AH[:, p, b * P:(b + 1) * P], XP[:, 1, 0:P], ACT.Copy).then_inc(sem("mixed_high2"), 1)

            for p in range(4):
                for i in range(2):
                    split_high(act, at, nxt)
                    wait_group(act, at)
                    if p:
                        act.wait_ge(sem("head_normed"), 2 * p)
                    act.activation(SQ2[:, i, :], DP[:, bank(at), :], ACT.Square).then_inc(sem("head_squared"), 1)
                    act.activation(QR[:, i, :], DP[:, bank(at), :], ACT.Copy).then_inc(bank_free[bank(at)], 1)
                    at.n, at.u, at.d = at.n + 1, at.u + 1, at.d + 1
                for i in range(2):
                    act.wait_ge(sem("head_summed"), 2 * p + i + 1)
                    act.activation(RS[:, i, :], XP[:, i, :], ACT.Ln, scale=1.0 / HD, bias=EPSV[:, 0:1]
                                   ).then_inc(sem("head_ln"), 1)
                    act.wait_ge(sem("head_ln"), 2 * p + i + 1)
                    act.activation(RS[:, i, :], RS[:, i, :], ACT.Exp, scale=-0.5).then_inc(sem("head_rstd"), 1)
                if p % 2 == 0:
                    split_high(act, at, nxt)
                    if p:
                        act.wait_ge(sem("attended2"), 4 * p)
                    for m in range(LAT // P):
                        copy_group(V2[:, m, :])
                    at.u, at.d = at.u + 2, at.d + 2
                    split_high(act, at, nxt)
                work = [(p * 8 + 2 * b + e, b, e) for b in range(4) for e in range(2)]
                exps2(*work[0])
                for i, (n, b, e) in enumerate(work):
                    if i + 1 < len(work):
                        exps2(*work[i + 1])
                    copy_transposes2(n, b, e)
                    if i >= 2 and i % 2 == 0:
                        mixed_high2(n // 2 - 1, p, b - 1)
                mixed_high2(n // 2, p, b)
                if p < 2:
                    act.wait_ge(sem("bias_used"), 8 * (p + 1))
                    act.dma_start(BW[:, p, :, :], a["rel"][p + 2]).then_inc(sem(f"bias_landed{p}"), 16)

            act.wait_ge(sem("attended2"), 16)
            act.wait_ge(sem("mixed_low2"), 16)
            act.dma_start(IOTA[:, :], a["iota"]).then_inc(sem("ssm_loads"), 16)
            act.dma_start(MATS[:, 0, :, :], a["ssm"][0]).then_inc(sem("ssm_mats0"), 16)
            act.wait_ge(sem("ssm_prep"), 12)
            act.activation(PV(7), PV(5), ACT.Sin, scale=TWO_PI).then_inc(sem("ssm_trig0"), 1)
            act.activation(PV(8), PV(6), ACT.Sin, scale=TWO_PI).then_inc(sem("ssm_trig0"), 1)

            def trig(i):
                if i >= 2:
                    act.wait_ge(sem("ssm_products"), 4 * (i - 1))
                act.wait_ge(sem("ssm_turns"), 2 * i + 1)
                act.activation(TRIG[:, i % 2, 0, :], TURN[:, :], ACT.Sin, scale=TWO_PI).then_inc(sem("ssm_trig"), 1)
                act.wait_ge(sem("ssm_turns"), 2 * i + 2)
                act.activation(TRIG[:, i % 2, 1, :], TR[:, 0:LAT], ACT.Sin, scale=TWO_PI, bias=QUARTER[:, 0:1]
                               ).then_inc(sem("ssm_trig"), 1)
                if i < 15:
                    angles(i + 1)

            def angles(i):
                if i:
                    act.wait_ge(sem("ssm_trig"), 2 * i)
                act.activation(TURN[:, :], IOTA[:, :], ACT.Copy, scale=PV(3)[:, i:i + 1]).then_inc(sem("turn_scaled"), 1)

            act.wait_ge(sem("ssm_loads"), 16)
            angles(0)
            trig(0)
            for i in range(16):
                split_high(act, at, nxt)
                if i < 15:
                    if i >= 1:
                        act.wait_ge(sem("ssm_c"), 2 * i)
                        act.wait_ge(sem("ssm_driven"), i)
                    act.dma_start(MATS[:, (i + 1) % 2, :, :], a["ssm"][i + 1]).then_inc(sem(f"ssm_mats{(i + 1) % 2}"), 16)
                    trig(i + 1)
                wait_group(act, at)
                act.activation(GATES[:, i, :], DP[:, bank(at), :], ACT.Sigmoid, bias=vec("b_gate", i)
                               ).then_inc(bank_free[bank(at)], 1)
                at.n, at.u, at.d = at.n + 1, at.u + 1, at.d + 1
            for t in range(4):
                act.wait_ge(sem("gelu_inner"), 3 * t + 3)
                act.activation(PR[:, t, :], PR[:, t, :], ACT.Sigmoid, scale=2.0 * 0.7978845608028654
                               ).then_inc(sem("gelu_sigmoid"), 1)
            for t in range(4):
                act.wait_ge(sem("z_made"), t + 1)
                act.activation(AH[:, 2 * t:2 * t + 2, LAT:T], UT(t), ACT.Copy).then_inc(sem("z_high"), 1)
            for t in range(2):
                split_high(act, at, nxt)
                for jj in range(2):
                    j = 2 * t + jj
                    wait_group(act, at)
                    act.activation(PR[:, j, :], DP[:, bank(at), :], ACT.Sigmoid, bias=vec("b_glu", j)
                                   ).then_inc(bank_free[bank(at)], 1)
                    at.n += 1
                at.u, at.d = at.u + 1, at.d + 1
            for j in range(4):
                act.wait_ge(sem("ssm_gated"), j + 1)
                act.activation(AH[:, 4 + j, 0:LAT], PR[:, j, :], ACT.Copy).then_inc(sem("z_high"), 1)

            for t in range(KT):
                split_high(act, at, nxt)
                act.wait_ge(sem("merged"), t + 1)
                act.activation(HH[:, t, 0:LAT], TQ[:, t % 2, 0:LAT], ACT.Copy).then_inc(sem("merged_high"), 1)
                at.n, at.u, at.d = at.n + 2, at.u + 1, at.d + 1
            act.wait_ge(sem("merged_low"), KT)
            act.dma_start(RW[:, :], a["router"]).then_inc(sem("moe_loads"), 16)
            act.dma_start(SEL[:, :, :], a["select"]).then_inc(sem("moe_loads"), 16)
            for t in range(KT):
                if t == 2:
                    act.wait_ge(sem("moe_loads"), 32)
                    act.activation(RWH[:, :], RW[:, :], ACT.Copy).then_inc(sem("router_split"), 1)
                split_high(act, at, nxt)
                wait_read(act, at, 0)
                norm_square(act, "ffn", Xk(LAT), LAT, t)
                at.n, at.u, at.d = at.n + 1, at.u + 1, at.d + 1
            norm_rstd(act, "ffn", LAT)
            norm_high(act, "ffn", LAT, nil)
            act.wait_ge(sem("route"), 3)
            act.activation(RT[:, 1, 0:16], RT[:, 1, 0:16], ACT.Exp).then_inc(sem("route_exp"), 1)
            act.wait_ge(sem("route"), 12)
            act.activation(RT[:, 6, 0:16], RT[:, 6, 0:16], ACT.Exp).then_inc(sem("route_exp"), 1)
            act.wait_ge(sem("gates_turned"), 1)
            act.wait_ge(sem("gate_rows_zero"), 1)
            act.activation(GT[0:4, :].rearrange("p (g n) -> p g n", g=4), XP[0:4, :, :], ACT.Copy
                           ).then_inc(sem("gate_row_read"), 1)

            with act.Fori(0, EXPERT_GROUPS) as g:
                at.enter(g, 24, 24, 24)
                nxt.enter(g, 24, 24, 24)
                for e in range(EXPERTS_PER):
                    act.wait_ge(sem("gate_row_made"), g * 4 + (e + 1))
                    act.wait_ge(sem("expert_low"), g * 8 + max(1, 2 * e - 1))
                    act.activation(GB[:, e % 2, :], XP[:, e % 2, :], ACT.Copy).then_inc(sem("gate_row_read"), 1)
                    for j in range(2):
                        f = 2 * e + j
                        split_high(act, at, nxt)
                        wait_group(act, at)
                        if f >= 2:
                            act.wait_ge(sem("expert_low"), g * 8 + f)
                        act.activation(SG[:, j, :], DP[:, bank(at), :], ACT.Sigmoid).then_inc(sem("expert_sigmoid"), 1)
                        at.n, at.u, at.d = at.n + 1, at.u + 1, at.d + 1
                        split_high(act, at, nxt)
                        at.n, at.u, at.d = at.n + 1, at.u + 1, at.d + 1
                        wait_read(act, at, 1)
                        act.activation(AH[:, f, 0:LAT], SG[:, j, :], ACT.Copy).then_inc(sem("expert_high"), 1)
                for t in range(KT):
                    split_high(act, at, nxt)
                    at.n, at.u, at.d = at.n + 1, at.u + 1, at.d + 1
                at.leave(EXPERT_GROUPS)
                nxt.leave(EXPERT_GROUPS)

        @block.vector
        def _(dve):
            at, nxt = At(kinds), At(kinds)
            nxt.to_dense()
            dve.memset(NIL[:, :], 0.0)
            for s in range(2):
                dve.wait_ge(cond_done, 4 * s + 1)
                dve.tensor_scalar(MPROD[:, :], MPROD[:, :], 1.0, None, ALU.add).then_inc(cond_done, 1)
                dve.wait_ge(cond_done, 4 * s + 2)
                dve.reciprocal(MPROD[:, :], MPROD[:, :]).then_inc(cond_done, 1)
                dve.wait_ge(cond_done, 4 * s + 3)
                dve.tensor_tensor(COND[:, s, :], COND[:, s, :], MPROD[:, :], ALU.mult).then_inc(cond_done, 1)
            dve.wait_ge(cond_done, 8)

            def amplitude(i):
                layer, chunk, name, off = AMP_NORMS[i]
                for s in range(2):
                    dve.scalar_tensor_tensor(AMP[:, i, :, s], mod_chunk(layer, chunk, s), 1.0, vec(name, off, 8),
                                             ALU.add, ALU.mult).then_inc(amp_done, 1)

            def gating(i):
                layer, chunk, name, off = GATE_NORMS[i]
                for s in range(2):
                    dve.tensor_tensor(GATE[:, i, :, s], mod_chunk(layer, chunk, s), vec(name, off, 8), ALU.mult
                                      ).then_inc(amp_done, 1)

            for t in range(16):
                mod_tile(dve, at, t, t)
            dve.wait_ge(sem("mod_summed"), 32)
            mod_add_bias(dve, 16, lambda n, o=0: slice(o, o + n))
            dve.wait_ge(mods_read, 1)
            amplitude(0)
            dve.wait_ge(amp_done, 2)
            norm_scale(dve, "pre0", Xk(T), T, amp(0), shift(0, 0))
            split_low(dve, nxt)
            split_low(dve, nxt)

            def groups(n):
                at.n += n
                at.u += 1
                at.d += 1

            def rope(r):
                dve.wait_ge(sem("rope_swapped"), r + 1)
                if r:
                    dve.wait_ge(sem("rope_done"), r)
                dve.tensor_tensor(TR[:, 0:LAT], XP[:, r % 2, :], SIN[:, :], ALU.mult).then_inc(sem("rope_sine"), 1)
                dve.tensor_tensor(TQ[:, r % 2, 0:LAT], TQ[:, r % 2, 0:LAT], COS[:, :], ALU.mult).then_inc(sem("rope_cosine"), 1)
                dve.wait_ge(sem("rope_sine"), r + 1)
                dve.wait_ge(sem("rope_cosine"), r + 1)
                dve.tensor_tensor(TQ[:, r % 2, 0:LAT], TQ[:, r % 2, 0:LAT], TR[:, 0:LAT], ALU.add
                                  ).then_inc(sem("rope_done"), 1)

            def rope_low(r):
                if r >= 2:
                    dve.wait_ge(sem("rope_high"), 8 + r - 1)
                    dve.tensor_tensor(AL[:, r - 2, :], TQ[:, r % 2, :], AH[:, r - 2, :].bitcast(F32), ALU.subtract
                                      ).then_inc(sem("rope_low"), 1)
                    return
                dve.wait_ge(sem("rope_high"), 4 * (r + 1))
                for e in range(2):
                    rows, head = slice(64 * e, 64 * e + 64), 2 * r + e
                    for half in range(2):
                        dve.tensor_tensor(KDL[64 * half:64 * half + 64, head, :], TQ[rows, r % 2, :],
                                          KDH[rows, head, :].bitcast(F32), ALU.subtract).then_inc(sem("rope_low"), 1)

            groups(2)
            split_low(dve, nxt)
            groups(2)
            dve.wait_ge(rope_loads, 48)
            for r in range(2, 10):
                rope(r - 2)
                rope_low(r - 2)
                split_low(dve, nxt)
                groups(2)
            rope(8)
            rope_low(8)
            split_low(dve, nxt)
            for m in range(T // P):
                dve.wait_ge(sem("value_high"), m + 1)
                dve.tensor_tensor(VHL[:, m, :, HD:2 * HD], DP[:, bank(at), 0:2 * P].rearrange("p (h n) -> p h n", n=HD),
                                  VHL[:, m, :, 0:HD].bitcast(F32), ALU.subtract).then_inc(bank_free[bank(at)], 1)
                at.n += 1
                if m == 1:
                    rope(9)
                    rope_low(9)
            at.u += 2
            at.d += 2

            def maxima(aa, g, b, hh, near):
                p, n, q = aa % 2, P * (len(near) + 2), aa // GROUP % 2
                dve.wait_ge(sem("scored"), aa + 1)
                dve.tensor_reduce(ST[:, q, 0, hh:hh + 1], DPF[:, p * 1024 + 768 - n:p * 1024 + 768], AX.X, ALU.max
                                  ).then_inc(sem("row_max"), 1)
                dve.wait_ge(sem("row_max"), aa + 1)
                head = GROUP * g + hh
                dve.tensor_scalar(ST[:, q, 1, hh:hh + 1], ST[:, q, 0, hh:hh + 1], ROWS[:, head:head + 1], -1.0,
                                  ALU.max, ALU.mult).then_inc(sem("shift_ready"), 1)
                if hh == GROUP - 1:
                    dve.wait_ge(sem("shift_ready"), aa + 1)
                    dve.tensor_tensor(ST[:, q, 3, :], ST[:, q, 1, :], ROWS[:, GROUP * g:GROUP * g + GROUP], ALU.add
                                      ).then_inc(sem("sink_shifted"), 1)

            def turned_low(aa, near):
                dve.wait_ge(sem("turned_high"), aa + 1)
                n, p = len(near), aa % 2
                dve.tensor_tensor(PTL[:, p, 0:n + 2, :], XPF[:, 512 - n * P:512 + 2 * P].rearrange("p (k n) -> p k n", n=P),
                                  PTH[:, p, 0:n + 2, :].bitcast(F32), ALU.subtract).then_inc(sem("turned_low"), 1)

            def scale_out(blk):
                q = blk % 2
                dve.wait_ge(sem("attended"), GROUP * (blk + 1))
                dve.wait_ge(sem("sink_term"), blk + 1)
                dve.tensor_tensor(ST[:, q, 4, :], ST[:, q, 2, :], ST[:, q, 3, :], ALU.add).then_inc(sem("out_steps"), 1)
                dve.wait_ge(sem("out_steps"), 4 * blk + 1)
                dve.reciprocal(ST[:, q, 4, :], ST[:, q, 4, :]).then_inc(sem("out_steps"), 1)
                dve.wait_ge(sem("out_steps"), 4 * blk + 2)
                if blk:
                    dve.wait_ge(sem("out_turned"), blk)
                parts = XP[:, 2, :].rearrange("p (h n) -> p h n", n=2 * HD)
                recip = ST[:, q, 4, :].unsqueeze(2).to_broadcast((P, GROUP, HD))
                low = TR[:, 0:GROUP * HD].rearrange("p (h n) -> p h n", n=HD)
                out = OS[:, :].rearrange("p (h n) -> p h n", n=HD)
                dve.tensor_tensor(low, parts[:, :, HD:2 * HD], recip, ALU.mult).then_inc(sem("out_steps"), 1)
                dve.tensor_tensor(out, parts[:, :, 0:HD], recip, ALU.mult).then_inc(sem("out_steps"), 1)
                dve.wait_ge(sem("out_steps"), 4 * blk + 4)
                dve.tensor_tensor(out, out, low, ALU.add).then_inc(sem("out_scaled"), 1)

            def mixed_low(blk, g, b):
                dve.wait_ge(sem("mixed_high"), blk + 1)
                to = (slice(None), slice(2 * g, 2 * g + 2), slice(b * P, (b + 1) * P))
                dve.tensor_tensor(AL[to], XP[:, 3, 0:2 * P].rearrange("p (j n) -> p j n", n=P), AH[to].bitcast(F32),
                                  ALU.subtract).then_inc(sem("mixed_low"), 1)

            work = list(heads_of_blocks())
            maxima(*work[0])
            maxima(*work[1])
            streams = 0
            for aa, g, b, hh, near in work:
                turned_low(aa, near)
                if aa + 2 < len(work):
                    maxima(*work[aa + 2])
                blk = aa // GROUP
                if hh == 0 and blk:
                    scale_out(blk - 1)
                if hh == 1 and blk:
                    mixed_low(blk - 1, *work[aa - GROUP][1:3])
                if hh and streams < 64:
                    tile, s = streams // 2, streams % 2
                    if tile % 8 == 0 and s == 0:
                        dve.wait_ge(mods_read, 1 + tile // 8)
                    mod_stream(dve, at, tile % 8, s, 32 + streams)
                    streams += 1
                    if tile % 8 == 7 and s == 1:
                        mod_add_bias(dve, 8, lambda n, o=0: slice(o + 9 + tile, o + 9 + tile + n))
            scale_out(blk)
            mixed_low(blk, g, b)
            split_low(dve, nxt)
            dve.wait_ge(mods_read, 5)
            gating(0)
            amplitude(1)
            gating(1)
            dve.wait_ge(amp_done, 8)

            for t in range(KT):
                split_low(dve, nxt)
                groups(2)
            residual(dve, "post0", T, gate(0))
            norm_scale(dve, "pre1", Xk(T), T, amp(1), shift(0, 3))

            with dve.Fori(0, MLP_STEPS) as it:
                at.enter(it, 28, 16, 32)
                nxt.enter(it, 28, 16, 32)

                def hidden_low(i):
                    t, c = i // 2, i % 2
                    out = slice(384 * c, 384 * c + 384)
                    dve.wait_ge(sem("hidden_high"), it * 16 + (i + 1))
                    dve.tensor_tensor(AL[:, t, out], SQ[:, i % 2, 0:384], AH[:, t, out].bitcast(F32), ALU.subtract
                                      ).then_inc(sem("hidden_low"), 1)

                for t in range(2 * KT):
                    split_low(dve, nxt)
                    for c in range(2):
                        i = 2 * t + c
                        wait_group(dve, at)
                        if t < KT:
                            if i >= 2:
                                dve.wait_ge(sem("hidden_high"), it * 16 + (i - 1))
                            dve.tensor_scalar(TQ[:, i % 2, 0:384], DP[:, bank(at), 0:384], 0.0, None, ALU.max
                                              ).then_inc(bank_free[bank(at)], 1)
                            if i >= 1:
                                hidden_low(i - 1)
                            if i == 15:
                                hidden_low(i)
                        else:
                            k = t - KT
                            if k == 0 and c == 0:
                                dve.wait_ge(sem("y_zero"), KT)
                            y = Y[:, k, 384 * c:384 * c + 384]
                            dve.tensor_tensor(y, DP[:, bank(at), 0:384], y, ALU.add).then_inc(bank_free[bank(at)], 1)
                        at.n += 1
                    at.u += 1
                    at.d += 1
                    if t == 0:
                        dve.wait_ge(mods_read, it + 5)
                    if t < 12:
                        mod_tile(dve, at, t, it * 12 + (48 + t))
                    if t == 11:
                        mod_add_bias(dve, 12, lambda n, o=0: bass.ds(it * 12 + (o + 48), n))
                at.leave(MLP_STEPS)
                nxt.leave(MLP_STEPS)
                nxt.u = at.u + 1
            dve.wait_ge(mods_read, 9)
            for i in (2, 3):
                gating(i)
                amplitude(i)
            dve.wait_ge(amp_done, 16)
            residual(dve, "post1", T, gate(1))
            dve.wait_ge(sem("gate_down_split"), 1)
            dve.tensor_tensor(WDL, QD[:, 0, :].rearrange("p (a n) -> p a n", a=2), WDH.bitcast(F32), ALU.subtract).then_inc(sem("gate_down_split"), 1)
            dve.memset(ATM[:, :, :, :], 0.0).then_inc(sem("mixing_zero"), 1)
            dve.wait_ge(sem("mixing_zero"), 1)
            norm_scale(dve, "pre2", Xk(T), T, amp(2), shift(1, 0))
            dve.wait_ge(sem("gla_loads"), 48)
            CH = T // CHUNK

            def gate_logs(h, d):
                s = 2 * h + d
                dve.wait_ge(sem("gate_logits_made"), s + 1)
                dve.tensor_scalar(B[:, d, :].rearrange("p (c n) -> p c n", n=384), XP[:, 0:2, 0:384],
                                  vec("gate_bias", 2 * h + d), None, ALU.add).then_inc(sem("gate_logits_read"), 1)
                dve.wait_ge(sem("gate_logits_read"), s + 1)
                dve.tensor_scalar(MN[:, d, :], B[:, d, :], 0.0, None, ALU.min).then_inc(sem("gate_min"), 1)
                dve.wait_ge(sem("gate_min"), s + 1)
                dve.scalar_tensor_tensor(B[:, d, :], MN[:, d, :], 2.0, B[:, d, :], ALU.mult, ALU.subtract
                                         ).then_inc(sem("gate_folded"), 1)

            def decays(h, d):
                s = 2 * h + d
                dve.wait_ge(sem("gate_log"), s + 1)
                dve.tensor_tensor(B[:, d, :], MN[:, d, :], B[:, d, :], ALU.subtract).then_inc(sem("log_decay"), 1)
                dve.wait_ge(sem("log_decay"), s + 1)
                if s:
                    dve.wait_ge(sem("decay_exps"), 4 * s)
                for c in range(CH):
                    cols = slice(c * CHUNK, (c + 1) * CHUNK)
                    dve.tensor_tensor_scan(BC[:, cols], ONES[:, 0:CHUNK], B[:, d, cols], 0.0, ALU.mult, ALU.add
                                           ).then_inc(sem("scanned"), 1)
                dve.wait_ge(sem("scanned"), CH * (s + 1))
                last_of = BC[:, :].rearrange("p (c n) -> p c n", n=CHUNK)[:, :, CHUNK - 1:CHUNK]
                dve.tensor_copy(TOT[:, d, :], last_of.rearrange("p c o -> p (c o)")).then_inc(sem("chunk_total"), 1)
                dve.wait_ge(sem("chunk_total"), s + 1)
                tot = TOT[:, d, :].unsqueeze(2).to_broadcast((P, CH, CHUNK))
                bc = BC[:, :].rearrange("p (c n) -> p c n", n=CHUNK)
                bd = B[:, d, :].rearrange("p (c n) -> p c n", n=CHUNK)
                if d == 0:
                    dve.tensor_tensor(bd, tot, bc, ALU.subtract).then_inc(sem("decays_summed"), 1)
                else:
                    dve.tensor_tensor(bd, bc, bd, ALU.subtract).then_inc(sem("end_decay"), 1)
                    dve.wait_ge(sem("end_decay"), h + 1)
                    dve.tensor_tensor(bc, tot, bd, ALU.subtract).then_inc(sem("decays_summed"), 1)
                dve.wait_ge(sem("decay_exps"), 4 * s + 1)
                if h:
                    dve.wait_ge(sem("keys_turned"), s - 1)
                dve.tensor_tensor(KEF[:, d, :], KEYS[:, :], B[:, d, :], ALU.mult).then_inc(sem("keys_decayed"), 1)
                dve.wait_ge(sem("decay_exps"), 4 * s + 3)
                dve.tensor_tensor(QD[:, d, :], QD[:, d, :], QT[:, 0:LAT], ALU.mult)
                dve.tensor_tensor(KI[:, d, :], KI[:, d, :], KEYS[:, 0:LAT], ALU.mult).then_inc(sem("queries_decayed"), 1)

            def scan_steps(h, d):
                s = 2 * h + d
                order = SCAN_TILES[d]
                halves = (0, 1) if d == 0 else (1, 0)
                dve.wait_ge(sem("decay_exps"), 4 * s + 4)

                def mask(i):
                    if order[i] >= LAT // P:
                        return
                    j = i - 2
                    n = 4 * s + j
                    dve.wait_ge(sem("mixing_made"), n + 1)
                    if n >= 2:
                        dve.wait_ge(sem("mixed_out_made"), n - 1)
                    dve.copy_predicated(ATM[:, d, j % 2, :], CAUSAL[:, d, :].bitcast(I32), DP[:, 2 + j % 2, 0:P]
                                        ).then_inc(sem("mixing_masked"), 1)

                def state(i):
                    for e, half in enumerate(halves):
                        c = 2 * i + e
                        if c == 11:
                            continue
                        n = 11 * s + c
                        dve.wait_ge(sem("update_made"), n + 1)
                        if n:
                            dve.wait_ge(sem("state_updated"), n)
                        done = 4 * s + max(0, (c - 3) // 2 - 2 + 1)
                        if done:
                            dve.wait_ge(sem("mixed_out_made"), done)
                        out, u = S[:, (c + 1) % 4, :], XP[:, 2 + c % 2, 0:GLA_DV]
                        if c == 0:
                            dve.tensor_copy(out, u).then_inc(sem("state_updated"), 1)
                        else:
                            ch = 2 * order[i] + half
                            dve.scalar_tensor_tensor(out, S[:, c % 4, :], DEC[:, d, ch:ch + 1], u, ALU.mult, ALU.add
                                                     ).then_inc(sem("state_updated"), 1)

                def add_output(i):
                    if d == 0 or order[i] >= LAT // P:
                        return
                    m, n = order[i], 4 * s + i - 2
                    dve.wait_ge(sem("mixed_out_made"), n + 1)
                    o = O[:, :, m * P:(m + 1) * P]
                    dve.tensor_tensor(o, DP[:, i % 2, 0:2 * P].rearrange("p (v n) -> p v n", v=2), o, ALU.add
                                      ).then_inc(sem("mixed_out_read"), 1)

                if d == 1:
                    dve.wait_ge(sem("mixed_out_read"), 8 * h + 4)
                mask(0)
                state(0)
                for i in range(6):
                    if i < 5:
                        mask(i + 1)
                        state(i + 1)
                    add_output(i)

            for h in range(GLA_HEADS):
                split_low(dve, nxt)
                groups(2)
                split_low(dve, nxt)
                groups(2)
                if h:
                    dve.wait_ge(sem("decay_exps"), 8 * h)
                split_low(dve, nxt)
                gate_logs(h, 0)
                gate_logs(h, 1)
                decays(h, 0)
                decays(h, 1)
                groups(6)
                at.u, at.d = at.u + 1, at.d + 1
                split_low(dve, nxt)
                for d in range(2):
                    scan_steps(h, d)
                dve.wait_ge(sem("out_rstd"), 2 * h + 2)
                for v in range(2):
                    dve.scalar_tensor_tensor(O[:, v, :], O[:, v, :], vec("gla_g", v), TR[:, 0:LAT], ALU.mult, ALU.mult
                                             ).then_inc(sem("out_normed"), 1)
                for v in range(2):
                    split_low(dve, nxt)
                    n = 2 * h + v
                    dve.wait_ge(sem("gla_sigmoid"), n + 1)
                    dve.tensor_tensor(TQ[:, v, 0:LAT], DP[:, bank(at), :], TQ[:, v, 0:LAT], ALU.mult
                                      ).then_inc(bank_free[bank(at)], 1)
                    groups(1)
                    wait_read(dve, at, 1)
                    dve.wait_ge(sem("out_normed"), n + 1)
                    dve.tensor_tensor(O[:, v, :], O[:, v, :], TQ[:, v, 0:LAT], ALU.mult).then_inc(sem("gla_gated"), 1)
                for v in range(2):
                    n = 2 * h + v
                    dve.wait_ge(sem("gla_high"), n + 1)
                    dve.tensor_tensor(AL[:, n, 0:LAT], O[:, v, :], AH[:, n, 0:LAT].bitcast(F32), ALU.subtract
                                      ).then_inc(sem("gla_low"), 1)

            for t in range(KT):
                split_low(dve, nxt)
                groups(1)
            residual(dve, "post2", LAT, gate(2))
            norm_scale(dve, "pre3", Xk(LAT), LAT, amp(3), shift(1, 3))

            with dve.Fori(0, MLP_STEPS) as it:
                at.enter(it, 16, 16, 16)
                nxt.enter(it, 16, 16, 16)

                def hidden_low1(t):
                    dve.wait_ge(sem("hidden_high"), it * 8 + (64 + t + 1))
                    dve.tensor_tensor(AL[:, t, 0:LAT], SQ[:, t % 2, :], AH[:, t, 0:LAT].bitcast(F32), ALU.subtract
                                      ).then_inc(sem("hidden_low"), 1)

                for t in range(2 * KT):
                    split_low(dve, nxt)
                    wait_group(dve, at)
                    if t < KT:
                        if t >= 2:
                            dve.wait_ge(sem("hidden_high"), it * 8 + (64 + t - 1))
                        dve.tensor_scalar(TQ[:, t % 2, 0:LAT], DP[:, bank(at), :], 0.0, None, ALU.max
                                          ).then_inc(bank_free[bank(at)], 1)
                        if t >= 1:
                            hidden_low1(t - 1)
                        if t == KT - 1:
                            hidden_low1(t)
                    else:
                        if t == KT:
                            dve.wait_ge(sem("y_zero"), 2 * KT)
                        y = Y[:, t - KT, 0:LAT]
                        dve.tensor_tensor(y, DP[:, bank(at), :], y, ALU.add).then_inc(bank_free[bank(at)], 1)
                    at.n, at.u, at.d = at.n + 1, at.u + 1, at.d + 1
                at.leave(MLP_STEPS)
                nxt.leave(MLP_STEPS)
            residual(dve, "post3", LAT, gate(3))

            norm_scale(dve, "mix", Xk(LAT), LAT, lambda k, s: vec("mix_gain", k), nil)
            lre, lim = vec("lam_re", 0, 16), vec("lam_im", 0, 16)
            steps = [1]

            def prep(ins):
                ins.then_inc(sem("ssm_prep"), 1)
                steps[0] += 1
                dve.wait_ge(sem("ssm_prep"), steps[0])

            MAGIC = 1.5 * 2.0 ** 23
            dve.wait_ge(sem("ssm_prep"), 1)
            prep(dve.tensor_tensor(PV(1), lre, PV(0), ALU.mult))
            prep(dve.tensor_tensor(PV(3), lim, PV(0), ALU.mult))
            steps[0] += 1
            prep(dve.tensor_scalar(PV(3), PV(3), 1.0 / (2.0 * np.pi), None, ALU.mult))
            prep(dve.tensor_scalar(PV(4), PV(3), MAGIC, MAGIC, ALU.add, ALU.subtract))
            prep(dve.tensor_tensor(PV(3), PV(3), PV(4), ALU.subtract))
            prep(dve.tensor_scalar(PV(4), PV(3), MAGIC, MAGIC, ALU.add, ALU.subtract))
            prep(dve.tensor_tensor(PV(5), PV(3), PV(4), ALU.subtract))
            prep(dve.tensor_scalar(PV(6), PV(3), 0.25, None, ALU.add))
            prep(dve.tensor_scalar(PV(4), PV(6), MAGIC, MAGIC, ALU.add, ALU.subtract))
            prep(dve.tensor_tensor(PV(6), PV(6), PV(4), ALU.subtract))
            for t in range(4):
                split_low(dve, nxt)
                groups(1)

            def maxima2(n, p, b, e):
                w = P * (b + 1)
                dve.wait_ge(sem("scored2"), n + 1)
                if n >= 2:
                    dve.wait_ge(sem("exponentials2"), n - 1)
                dve.scalar_tensor_tensor(SS[:, e, 0:w], XP[:, 2 + e, 0:w], QUERY, BW[:, p % 2, e, 512 - w:512],
                                         ALU.mult, ALU.add).then_inc(sem("bias_used"), 1)
                dve.wait_ge(sem("bias_used"), n + 1)
                dve.tensor_reduce(ST2[:, e, 0:1], SS[:, e, 0:w], AX.X, ALU.max).then_inc(sem("row_max2"), 1)
                dve.wait_ge(sem("row_max2"), n + 1)
                dve.tensor_scalar(ST2[:, e, 1:2], ST2[:, e, 0:1], -1.0, None, ALU.mult).then_inc(sem("shift_ready2"), 1)

            def normalise2(n, b, e):
                dve.wait_ge(sem("exponentials2"), n + 1)
                dve.reciprocal(ST2[:, e, 5:6], ST2[:, e, 2:3]).then_inc(sem("denominator2"), 1)
                dve.wait_ge(sem("denominator2"), n + 1)
                w = P * (b + 1)
                dve.tensor_scalar(PB2[:, e, 0:w], PB2[:, e, 0:w], ST2[:, e, 5:6], None, ALU.mult
                                  ).then_inc(sem("probabilities2"), 1)

            def mixed_low2(q, p, b):
                dve.wait_ge(sem("mixed_high2"), q + 1)
                dve.tensor_tensor(AL[:, p, b * P:(b + 1) * P], XP[:, 1, 0:P], AH[:, p, b * P:(b + 1) * P].bitcast(F32),
                                  ALU.subtract).then_inc(sem("mixed_low2"), 1)

            for p in range(4):
                split_low(dve, nxt)
                groups(1)
                split_low(dve, nxt)
                groups(1)
                for i, (out, gain) in enumerate([(QN, "q_gain"), (KN, "k_gain")]):
                    dve.wait_ge(sem("head_rstd"), 2 * p + i + 1)
                    wait_read(dve, at, 2 - i)
                    dve.scalar_tensor_tensor(out[:, :], QR[:, i, :], vec(gain), RS[:, i, :], ALU.mult, ALU.mult
                                             ).then_inc(sem("head_normed"), 1)
                if p % 2 == 0:
                    split_low(dve, nxt)
                    groups(4)
                    at.u, at.d = at.u + 1, at.d + 1
                    split_low(dve, nxt)
                dve.wait_ge(sem(f"bias_landed{p % 2}"), 16 * (p // 2 + 1))
                dve.memset(BW[0:64, p % 2, :, 448:512], NEG).then_inc(sem("bias_masked"), 1)
                dve.wait_ge(sem("bias_masked"), p + 1)
                work = [(p * 8 + 2 * b + e, b, e) for b in range(4) for e in range(2)]
                maxima2(work[0][0], p, 0, 0)
                maxima2(work[1][0], p, 0, 1)
                for i, (n, b, e) in enumerate(work):
                    normalise2(n, b, e)
                    if i + 2 < len(work):
                        n2, b2, e2 = work[i + 2]
                        maxima2(n2, p, b2, e2)
                    if i >= 2 and i % 2 == 0:
                        mixed_low2(n // 2 - 1, p, b - 1)
                mixed_low2(n // 2, p, b)

            dve.wait_ge(sem("ssm_trig0"), 2)
            prep(dve.tensor_tensor(PV(8), PV(2), PV(8), ALU.mult))
            prep(dve.tensor_tensor(PV(7), PV(2), PV(7), ALU.mult))
            prep(dve.tensor_scalar(PV(8), PV(8), -1.0, None, ALU.add))
            prep(dve.tensor_tensor(PV(9), lre, lre, ALU.mult))
            prep(dve.tensor_tensor(PV(10), lim, lim, ALU.mult))
            prep(dve.tensor_tensor(PV(9), PV(9), PV(10), ALU.add))
            prep(dve.reciprocal(PV(10), PV(9)))
            prep(dve.tensor_tensor(PV(4), PV(8), lre, ALU.mult))
            prep(dve.tensor_tensor(PV(5), PV(7), lim, ALU.mult))
            prep(dve.tensor_tensor(PV(4), PV(4), PV(5), ALU.add))
            prep(dve.tensor_tensor(PV(11), PV(4), PV(10), ALU.mult))
            prep(dve.tensor_tensor(PV(4), PV(7), lre, ALU.mult))
            prep(dve.tensor_tensor(PV(5), PV(8), lim, ALU.mult))
            prep(dve.tensor_tensor(PV(4), PV(4), PV(5), ALU.subtract))
            prep(dve.tensor_tensor(PV(12), PV(4), PV(10), ALU.mult))
            prep(dve.tensor_scalar(PV(5), PV(12), -1.0, None, ALU.mult))
            assert steps[0] == SSM_PREP

            def ssm_y(t):
                dve.wait_ge(sem("ssm_out"), 4 * (t + 1))
                dve.scalar_tensor_tensor(UT(t), UT(t), vec("ssm_d", t), XP[:, 2 + t % 2, :].rearrange("p (a n) -> p a n", a=2),
                                         ALU.mult, ALU.add).then_inc(sem("ssm_y"), 1)

            def turned(i):
                dve.wait_ge(sem("ssm_driven"), i + 1)
                dve.wait_ge(sem("ssm_trig"), 2 * i + 2)
                if i:
                    dve.wait_ge(sem("ssm_products"), 4 * i)
                    dve.wait_ge(sem("ssm_out"), i)
                sin, cos = TRIG[:, i % 2, 0, :], TRIG[:, i % 2, 1, :]
                for k, (w, q) in enumerate([(0, cos), (1, sin), (1, cos), (0, sin)]):
                    dve.tensor_tensor(PR[:, k, :], XP[:, w, :], q, ALU.mult).then_inc(sem("ssm_turned"), 1)
                dve.wait_ge(sem("ssm_turned"), 4 * i + 4)
                for z, op in ((0, ALU.add), (1, ALU.subtract)):
                    dve.tensor_tensor(TQ[:, z, 0:LAT], PR[:, 2 * z, :], PR[:, 2 * z + 1, :], op).then_inc(sem("ssm_v"), 1)
                dve.wait_ge(sem("ssm_v"), 2 * i + 2)
                for z in range(2):
                    dve.tensor_tensor_scan(TQ[:, z, 0:LAT], PV(2)[:, i:i + 1].to_broadcast((P, LAT)), TQ[:, z, 0:LAT], 0.0,
                                           ALU.mult, ALU.add).then_inc(sem("ssm_z"), 1)
                dve.wait_ge(sem("ssm_z"), 2 * i + 2)
                for k, (z, q) in enumerate([(0, cos), (1, sin), (0, sin), (1, cos)]):
                    dve.tensor_tensor(PR[:, k, :], TQ[:, z, 0:LAT], q, ALU.mult).then_inc(sem("ssm_products"), 1)
                dve.wait_ge(sem("ssm_products"), 4 * i + 4)
                for z, op in ((0, ALU.subtract), (2, ALU.add)):
                    dve.tensor_tensor(PR[:, z, :], PR[:, z, :], PR[:, z + 1, :], op).then_inc(sem("ssm_state"), 1)

            for i in range(16):
                split_low(dve, nxt)
                turned(i)
                groups(1)
                if i % 4 == 0 and i:
                    ssm_y(i // 4 - 1)
            ssm_y(3)
            for t in range(4):
                dve.wait_ge(sem("ssm_out"), 16)
                pr = PR[:, t, :].rearrange("p (a n) -> p a n", a=2)
                dve.wait_ge(sem("ssm_y"), t + 1)
                dve.tensor_tensor(pr, UT(t), UT(t), ALU.mult).then_inc(sem("gelu_inner"), 1)
                dve.wait_ge(sem("gelu_inner"), 3 * t + 1)
                dve.tensor_scalar(PR[:, t, :], PR[:, t, :], 0.044715, 1.0, ALU.mult, ALU.add).then_inc(sem("gelu_inner"), 1)
                dve.wait_ge(sem("gelu_inner"), 3 * t + 2)
                dve.tensor_tensor(pr, pr, UT(t), ALU.mult).then_inc(sem("gelu_inner"), 1)
            for t in range(4):
                dve.wait_ge(sem("gelu_sigmoid"), t + 1)
                pr = PR[:, t, :].rearrange("p (a n) -> p a n", a=2)
                dve.tensor_tensor(UT(t), UT(t), pr, ALU.mult).then_inc(sem("z_made"), 1)
            for t in range(4):
                dve.wait_ge(sem("z_high"), t + 1)
                dve.tensor_tensor(AL[:, 2 * t:2 * t + 2, LAT:T], UT(t), AH[:, 2 * t:2 * t + 2, LAT:T].bitcast(F32),
                                  ALU.subtract).then_inc(sem("z_low"), 1)
            for t in range(2):
                split_low(dve, nxt)
                for jj in range(2):
                    j = 2 * t + jj
                    wait_read(dve, at, 0)
                    pr = PR[:, j, :].rearrange("p (a n) -> p a n", a=2)
                    dve.tensor_tensor(pr, pr, UT(j), ALU.mult).then_inc(sem("ssm_gated"), 1)
                    at.n += 1
                at.u, at.d = at.u + 1, at.d + 1
            for j in range(4):
                dve.wait_ge(sem("z_high"), 4 + j + 1)
                dve.tensor_tensor(AL[:, 4 + j, 0:LAT], PR[:, j, :], AH[:, 4 + j, 0:LAT].bitcast(F32), ALU.subtract
                                  ).then_inc(sem("z_low"), 1)

            for t in range(KT):
                split_low(dve, nxt)
                if t >= 1:
                    dve.wait_ge(sem("merged_low"), t)
                for half in range(2):
                    wait_group(dve, at)
                    out = TQ[:, t % 2, 0:LAT] if half == 0 else TR[:, 0:LAT]
                    dve.tensor_tensor(out, DP[:, bank(at), :], GATES[:, 8 * half + t, :], ALU.mult
                                      ).then_inc(bank_free[bank(at)], 1)
                    at.n += 1
                at.u, at.d = at.u + 1, at.d + 1
                wait_read(dve, at, 1)
                wait_read(dve, at, 2)
                dve.tensor_tensor(TQ[:, t % 2, 0:LAT], TQ[:, t % 2, 0:LAT], TR[:, 0:LAT], ALU.add).then_inc(sem("merged"), 1)
                dve.wait_ge(sem("merged_high"), t + 1)
                dve.tensor_tensor(HL[:, t, 0:LAT], TQ[:, t % 2, 0:LAT], HH[:, t, 0:LAT].bitcast(F32), ALU.subtract
                                  ).then_inc(sem("merged_low"), 1)

            def add_to_x(t):
                dve.tensor_tensor(X[:, t, 0:LAT], DP[:, bank(at), :], X[:, t, 0:LAT], ALU.add
                                  ).then_inc(bank_free[bank(at)], 1)

            for t in range(KT):
                split_low(dve, nxt)
                wait_group(dve, at)
                add_to_x(t)
                at.n, at.u, at.d = at.n + 1, at.u + 1, at.d + 1
            dve.wait_ge(sem("router_split"), 1)
            dve.tensor_tensor(RWL[:, :], RW[:, :], RWH[:, :].bitcast(F32), ALU.subtract).then_inc(sem("router_split"), 1)
            norm_scale(dve, "ffn", Xk(LAT), LAT, lambda k, s: vec("ffn_gain", k), nil)

            steps = [0]

            def route(ins):
                ins.then_inc(sem("route"), 1)
                steps[0] += 1
                dve.wait_ge(sem("route"), steps[0])

            def r4(i):
                return RT[:, i, 0:16].rearrange("p (m g) -> p m g", g=4)

            def r1(i):
                return RT[:, i, 0:4].unsqueeze(2)

            def over4(i):
                return RT[:, i, 0:4].unsqueeze(2).to_broadcast((P, 4, 4))

            pref = PREF[:, :].unsqueeze(1).to_broadcast((P, 4, 4))

            def first_of(src, top, out):
                route(dve.tensor_tensor(r4(out), r4(src), over4(top), ALU.is_ge))
                route(dve.tensor_tensor(r4(out), r4(out), pref, ALU.mult))
                route(dve.tensor_reduce(r1(13), r4(out), AX.X, ALU.max))
                route(dve.tensor_tensor(r4(out), r4(out), over4(13), ALU.is_ge))

            dve.wait_ge(sem("router_made"), 1)
            logits = XP[:, 0, 0:80].rearrange("p (m n) -> p m n", n=20)
            bias_g = ROWS[:, 16:20].unsqueeze(1).to_broadcast((P, 4, 4))
            bias_e = ROWS[:, 20:36].unsqueeze(1).to_broadcast((P, 4, 16))
            for i in range(4):
                ins = dve.memset(PREF[:, i:i + 1], float(4 - i))
            ins.then_inc(sem("router_steps"), 1)
            dve.wait_ge(sem("router_steps"), 1)
            dve.tensor_tensor(EL[:, :, :], logits[:, :, 4:20], bias_e, ALU.add).then_inc(sem("router_steps"), 1)
            route(dve.tensor_tensor(r4(0), logits[:, :, 0:4], bias_g, ALU.add))
            route(dve.tensor_reduce(r1(2), r4(0), AX.X, ALU.max))
            route(dve.tensor_tensor(r4(1), r4(0), over4(2), ALU.subtract))
            first_of(0, 2, 3)
            dve.wait_ge(sem("router_steps"), 2)
            elg = EL[:, :, :].rearrange("p m (g e) -> p (m g) e", g=4)
            ohg = RT[:, 3, 0:16].unsqueeze(2).to_broadcast((P, 16, 4))
            route(dve.tensor_tensor(elg, elg, ohg, ALU.mult))
            el = EL[:, :, :].rearrange("p m (g e) -> p m g e", g=4)
            route(dve.tensor_tensor(r4(4), el[:, :, 0, :], el[:, :, 1, :], ALU.add))
            route(dve.tensor_tensor(r4(5), el[:, :, 2, :], el[:, :, 3, :], ALU.add))
            route(dve.tensor_tensor(r4(4), r4(4), r4(5), ALU.add))
            steps_before = steps[0]
            assert steps_before == 11
            dve.tensor_reduce(r1(7), r4(4), AX.X, ALU.max).then_inc(sem("router_steps"), 1)
            dve.wait_ge(sem("router_steps"), 3)
            route(dve.tensor_tensor(r4(6), r4(4), over4(7), ALU.subtract))
            first_of(4, 7, 8)
            route(dve.scalar_tensor_tensor(RT[:, 9, 0:16], RT[:, 8, 0:16], NEG, RT[:, 4, 0:16], ALU.mult, ALU.add))
            route(dve.tensor_reduce(r1(10), r4(9), AX.X, ALU.max))
            first_of(9, 10, 11)
            route(dve.tensor_tensor(r4(8), r4(8), r4(11), ALU.add))
            dve.wait_ge(sem("route_exp"), 2)
            route(dve.tensor_reduce(r1(2), r4(1), AX.X, ALU.add))
            route(dve.tensor_tensor(r4(6), r4(6), r4(8), ALU.mult))
            route(dve.tensor_reduce(r1(7), r4(6), AX.X, ALU.add))
            route(dve.tensor_tensor(r1(7), r1(7), r1(2), ALU.mult))
            route(dve.reciprocal(r1(10), r1(7)))
            route(dve.tensor_tensor(r4(6), r4(6), over4(10), ALU.mult))
            gts = GTS[:, :, :].rearrange("p m (g e) -> p m g e", g=4)
            for g in range(4):
                ins = dve.tensor_tensor(gts[:, :, g, :], r4(6), r4(3)[:, :, g:g + 1].to_broadcast((P, 4, 4)), ALU.mult)
            ins.then_inc(sem("expert_low"), 1)

            with dve.Fori(0, EXPERT_GROUPS) as g:
                at.enter(g, 24, 24, 24)
                nxt.enter(g, 24, 24, 24)
                for e in range(EXPERTS_PER):
                    for j in range(2):
                        f = 2 * e + j
                        split_low(dve, nxt)
                        dve.wait_ge(sem("expert_sigmoid"), g * 8 + (f + 1))
                        dve.tensor_tensor(SG[:, j, :], DP[:, bank(at), :], SG[:, j, :], ALU.mult
                                          ).then_inc(bank_free[bank(at)], 1)
                        at.n, at.u, at.d = at.n + 1, at.u + 1, at.d + 1
                        wait_read(dve, at, 1)
                        dve.wait_ge(sem("gate_row_read"), g * 4 + (e + 2))
                        dve.tensor_tensor(SG[:, j, :], SG[:, j, :], GB[:, e % 2, :], ALU.mult).then_inc(sem("expert_weighed"), 1)
                        split_low(dve, nxt)
                        wait_group(dve, at)
                        dve.wait_ge(sem("expert_weighed"), g * 8 + (f + 1))
                        dve.tensor_tensor(SG[:, j, :], DP[:, bank(at), :], SG[:, j, :], ALU.mult
                                          ).then_inc(bank_free[bank(at)], 1)
                        at.n, at.u, at.d = at.n + 1, at.u + 1, at.d + 1
                        wait_read(dve, at, 1)
                        dve.wait_ge(sem("expert_high"), g * 8 + (f + 1))
                        dve.tensor_tensor(AL[:, f, 0:LAT], SG[:, j, :], AH[:, f, 0:LAT].bitcast(F32), ALU.subtract
                                          ).then_inc(sem("expert_low"), 1)
                for t in range(KT):
                    split_low(dve, nxt)
                    wait_group(dve, at)
                    add_to_x(t)
                    at.n, at.u, at.d = at.n + 1, at.u + 1, at.d + 1
                at.leave(EXPERT_GROUPS)
                nxt.leave(EXPERT_GROUPS)



def feature_major(v):
    return np.ascontiguousarray(v.reshape(-1, P).T)


def kernel(**inputs):
    import concourse.bacc as _bacc
    from concourse.bass_utils import run_bass_kernel_spmd as _run

    x = {k: np.ascontiguousarray(v) for k, v in inputs.items()}
    w = {
        "w_mod": x["w_mod"], "attn_w_qkv": x["attn_w_qkv"], "attn_w_o": x["attn_w_o"], "w_mlp_in": x["w_mlp_in"],
        "w_mlp_out": x["w_mlp_out"], "gla_w_in": x["gla_w_in"], "gla_w_o": x["gla_w_o"], "w_in_2": x["w_in_2"],
        "w_branch_2": x["w_branch_2"], "w_out_2": x["w_out_2"], "w_e_gate_2": x["w_e_gate_2"][0],
        "w_e_up_2": x["w_e_up_2"][0], "w_e_down_2": x["w_e_down_2"].reshape(1, -1, D),
    }
    tiles = schedule()
    stream = np.zeros((len(tiles), P, TILE), np.float32)
    for i, (_, name, which, row, col) in enumerate(tiles):
        if name == "w_glu_2":
            two = x[name][0][:, col:col + 2 * P].reshape(4, P, 2, P)
            stream[i] = two.transpose(1, 2, 0, 3).reshape(P, TILE)
        elif name == "w_mod":
            stream[i] = w[name][which, :, col:col + P].T
        else:
            stream[i] = w[name][which, row:row + D, col:col + P].reshape(KT, P, P).transpose(1, 0, 2).reshape(P, TILE)

    gla_bias = x["gla_gate_bias"][0].reshape(2, 4, P).transpose(2, 1, 0).reshape(P, 8)
    vec = np.concatenate([
        feature_major(x["b_mod"]), feature_major(x["g_pre_mix"]),
        feature_major(x["g_post_mix"]), feature_major(x["g_pre_mlp"]), feature_major(x["g_post_mlp"]), gla_bias,
        feature_major(x["gla_g_norm"]), feature_major(x["mix_norm_gain_2"]), feature_major(x["b_gate_2"]),
        np.tile(x["q_gain_2"][0], 2)[:, None], np.tile(x["k_gain_2"][0], 2)[:, None], feature_major(x["ssm_d_2"]),
        feature_major(x["b_glu_2"]), feature_major(x["ffn_norm_gain_2"]), feature_major(x["ssm_lambda_re_2"]),
        feature_major(x["ssm_lambda_im_2"]), feature_major(np.repeat(x["ssm_log_step_2"][0], HD)),
    ], axis=1)
    row = np.concatenate([x["attn_sink"][0], x["group_bias_2"][0], x["expert_bias_2"][0]])
    row = np.ascontiguousarray(np.broadcast_to(row[None], (P, NROW)))

    cond = np.ascontiguousarray(np.broadcast_to(np.stack([x["c"][0], x["c_ctx"]])[None], (P, 2, D)))

    i = np.arange(P)
    const = np.concatenate([np.eye(P), np.ones((P, P)), i[:, None] == (i ^ 16)[None], (i[:, None] // HD) == (i[None] // HD)],
                           axis=1).astype(np.float32)
    pos = np.arange(LAT)
    inv = np.float32(10000.0) ** (-np.arange(16, dtype=np.float32) * np.float32(2.0) / np.float32(32))
    r = i % HD
    where = np.where((r // 32 == 0)[:, None], (pos // HD)[None], (pos % HD)[None]).astype(np.float32)
    angle = where * inv[r % 16][:, None]
    sign = np.where(r % 32 < 16, -1.0, 1.0)[:, None]
    j = np.arange(3 * P)
    band = np.where(np.abs(j[None] - P - i[:, None]) <= P, 0.0, NEG)
    rope = np.concatenate([np.cos(angle), sign * np.sin(angle), band], axis=1).astype(np.float32)
    same = (i[:, None] // CHUNK) == (i[None] // CHUNK)
    causal = np.stack([same & (i[:, None] <= i[None]), same & (i[:, None] >= i[None])], axis=1).astype(np.float32)
    gla_down = np.zeros((P, KT, 64), np.float32)
    gla_up = np.zeros((64, 512), np.float32)
    for d in range(2):
        gla_down[:, :, 32 * d:32 * d + 16] = x["gla_w_gate_down"][0, d].reshape(KT, P, 16).transpose(1, 0, 2)
        gla_up[32 * d:32 * d + 16] = x["gla_w_gate_up"][0, d]
    c = np.arange(LAT)
    distance = np.clip(i[:, None] - c[None] + 384, -63, 256) + 63
    rel = x["rel_bias_2"][0][:, distance].reshape(4, 2, P, LAT).transpose(0, 2, 1, 3)
    ssm = np.zeros((16, P, 4, P), np.float32)
    for t in range(16):
        for g in range(2):
            group, at = 2 * t + g, 32 * (t % 4) + 16 * g
            states = slice(HD * g, HD * g + HD)
            for z, (b, cc) in enumerate([("ssm_b_re_2", "ssm_c_re_2"), ("ssm_b_im_2", "ssm_c_im_2")]):
                ssm[t, at:at + 16, z, states] = x[b][0, group].T
                ssm[t, states, 2 + z, at:at + 16] = x[cc][0, group].T
    router = np.concatenate([x["w_group_router_2"][0], x["w_expert_router_2"][0]], axis=1)
    select = np.zeros((P, 4, P), np.float32)
    for e in range(4):
        select[e, e] = 1.0
    both = np.concatenate([x["x"][0], x["ctx"][0]], axis=0)
    arrays = {
        "stream": stream, "cond": cond, "vec": np.ascontiguousarray(vec), "row": row, "const": const, "rope": rope,
        "causal": causal, "gla_down": gla_down.reshape(P, 512), "gla_up": gla_up,
        "rel": np.ascontiguousarray(rel), "ssm": ssm, "select": select,
        "iota": np.ascontiguousarray(np.broadcast_to(np.arange(LAT, dtype=np.float32)[None], (P, LAT))),
        "router": np.ascontiguousarray(router.reshape(KT, P, 20).transpose(1, 0, 2).reshape(P, KT * 20)),
        "x": np.ascontiguousarray(both.T.reshape(KT, P, T).transpose(1, 0, 2)),
    }
    nc = _bacc.Bacc("TRN2", target_bir_lowering=False, num_devices=1, dynamic_dma_scratch_size=1024)
    args = {name: nc.dram_tensor("in_" + name, v.shape, mybir.dt.from_np(v.dtype), kind="ExternalInput").ap()
            for name, v in arrays.items()}
    out = nc.dram_tensor("out", (P, KT, LAT), F32, kind="ExternalOutput").ap()
    backbone_kernel(nc, args, out)
    result = _run(nc, [{"in_" + k: v for k, v in arrays.items()}], core_ids=[0]).results[0]["out"]
    return np.ascontiguousarray(result.transpose(2, 1, 0).reshape(1, LAT, D))
```
